# Optimizing a Trainium2 kernel written in Bass

```python
import jax
import jax.numpy as jnp
from jax import lax
import numpy as np

D_MODEL = 1024
BATCH = 1
SEQ = 512
DEPTH = 2
DEC_BATCH = 8
DEC_SEQ = 8
PAST_LEN = 4096
PAGE_SIZE = 128

N_MIXERS = 2
N_DELTA_LAYERS = (DEPTH + 1) // 2
N_SSM_LAYERS = DEPTH // 2
GDN_HEADS = 8
GDN_DK = 128
GDN_DV = 128
GDN_QK_DIM = GDN_HEADS * GDN_DK
GDN_V_DIM = GDN_HEADS * GDN_DV
GDN_CONV_DIM = 2 * GDN_QK_DIM + GDN_V_DIM
GDN_IN = GDN_CONV_DIM + GDN_V_DIM + 2 * GDN_HEADS
CONV_W = 4
CHUNK = 64
SSM_GROUP = 16
SSM_GROUPS = D_MODEL // SSM_GROUP
SSM_P = 64
N_GROUPS = 4
EXPERTS_PER_GROUP = 4
N_EXPERTS = N_GROUPS * EXPERTS_PER_GROUP
TOP_K = 2
D_FF_EXPERT = 256
EPS = 1e-6

kernel_name = "hybrid_gdn_s5_hmoe_step"

F32 = jnp.float32

def rmsnorm(x, w):
    x32 = x.astype(F32)
    y = x32 * lax.rsqrt(jnp.mean(x32 * x32, axis=-1, keepdims=True) + EPS)
    return (y * w.astype(F32)).astype(x.dtype)

def l2norm(x):
    x32 = x.astype(F32)
    return x32 * lax.rsqrt(jnp.sum(x32 * x32, axis=-1, keepdims=True) + EPS)

def ada_mod(c, w_mod, b_mod):
    m = (jax.nn.silu(c) @ w_mod + b_mod)[:, None, :]
    shift, scale, gate = jnp.split(m, 3, axis=-1)
    return shift, scale, gate

def causal_short_conv(x, buf, w):
    L = x.shape[1]
    xc = jnp.concatenate([buf.astype(x.dtype), x], axis=1)
    y = xc[:, 0:L] * w[0]
    for j in range(1, CONV_W):
        y = y + xc[:, j:j + L] * w[j]
    return jax.nn.silu(y), xc[:, -(CONV_W - 1):]

def gated_delta_rule(q, k, v, g, beta, s0):
    B, L, H, DK = q.shape
    DV = v.shape[-1]
    C = min(CHUNK, L)
    n = -(-L // C)
    pad = n * C - L

    def prep(t):
        t = t.astype(F32)
        t = jnp.pad(t, [(0, 0), (0, pad)] + [(0, 0)] * (t.ndim - 2))
        t = jnp.moveaxis(t, 2, 1)
        return t.reshape((B, H, n, C) + t.shape[3:])

    q, k, v, g, beta = prep(q), prep(k), prep(v), prep(g), prep(beta)
    g = jnp.cumsum(g, axis=-1)
    k_beta = k * beta[..., None]
    v_beta = v * beta[..., None]
    tril = jnp.tril(jnp.ones((C, C), bool))
    strict = jnp.tril(jnp.ones((C, C), bool), -1)
    decay = jnp.exp(jnp.where(tril, g[..., :, None] - g[..., None, :], -jnp.inf))
    a = jnp.where(strict, jnp.einsum('bhnik,bhnjk->bhnij', k_beta, k) * decay, 0.0)
    eye = jnp.eye(C, dtype=F32)
    rhs = jnp.concatenate([v_beta, k_beta * jnp.exp(g)[..., None]], axis=-1)
    sol = lax.linalg.triangular_solve(a + eye, rhs, left_side=True, lower=True, unit_diagonal=True)
    u, w = sol[..., :DV], sol[..., DV:]
    qk = jnp.where(tril, jnp.einsum('bhnik,bhnjk->bhnij', q, k) * decay, 0.0)
    q_dec = q * jnp.exp(g)[..., None]
    k_dec = k * jnp.exp(g[..., -1:] - g)[..., None]
    g_last = jnp.exp(g[..., -1])

    def step(s, xs):
        u_c, w_c, qk_c, qd_c, kd_c, gl_c = xs
        v_new = u_c - w_c @ s
        o = qd_c @ s + qk_c @ v_new
        s = s * gl_c[..., None, None] + jnp.swapaxes(kd_c, -1, -2) @ v_new
        return s, o

    xs = tuple(jnp.moveaxis(t, 2, 0) for t in (u, w, qk, q_dec, k_dec, g_last))
    s, o = lax.scan(step, s0.astype(F32), xs)
    o = jnp.moveaxis(o, 0, 2).reshape(B, H, n * C, DV)[:, :, :L]
    return jnp.moveaxis(o, 1, 2), s

def gdn_mixer(h, conv_buf, s0, w_in, conv_w, a_log, dt_bias, o_norm, w_out):
    B, L, _ = h.shape
    proj = h @ w_in
    i1 = GDN_CONV_DIM
    i2 = i1 + GDN_V_DIM
    i3 = i2 + GDN_HEADS
    qkv, z, b_raw, a_raw = jnp.split(proj, [i1, i2, i3], axis=-1)
    qkv, conv_new = causal_short_conv(qkv, conv_buf, conv_w)
    q, k, v = jnp.split(qkv, [GDN_QK_DIM, 2 * GDN_QK_DIM], axis=-1)
    q = l2norm(q.reshape(B, L, GDN_HEADS, GDN_DK)) * (GDN_DK ** -0.5)
    k = l2norm(k.reshape(B, L, GDN_HEADS, GDN_DK))
    v = v.reshape(B, L, GDN_HEADS, GDN_DV)
    beta = jax.nn.sigmoid(b_raw.astype(F32))
    g = -jnp.exp(a_log.astype(F32)) * jax.nn.softplus(a_raw.astype(F32) + dt_bias.astype(F32))
    o, s_new = gated_delta_rule(q, k, v, g, beta, s0)
    o = rmsnorm(o, o_norm) * jax.nn.silu(z.reshape(B, L, GDN_HEADS, GDN_DV).astype(F32))
    out = o.reshape(B, L, GDN_V_DIM).astype(h.dtype) @ w_out
    return out, conv_new, s_new.astype(s0.dtype)

def s5_mixer(h, s_re0, s_im0, w_in, lam_re, lam_im, log_dt, b_re, b_im, c_re, c_im, d_skip, w_glu):
    B, L, _ = h.shape
    u = (h @ w_in).astype(F32).reshape(B, L, SSM_GROUPS, SSM_GROUP)
    dt = jnp.exp(log_dt.astype(F32))[:, None]
    lr, li = lam_re.astype(F32), lam_im.astype(F32)
    mag = jnp.exp(lr * dt)
    ang = li * dt
    ab_re, ab_im = mag * jnp.cos(ang), mag * jnp.sin(ang)
    den = lr * lr + li * li
    f_re = ((ab_re - 1.0) * lr + ab_im * li) / den
    f_im = (ab_im * lr - (ab_re - 1.0) * li) / den
    br, bi = b_re.astype(F32), b_im.astype(F32)
    bb_re = f_re[..., None] * br - f_im[..., None] * bi
    bb_im = f_re[..., None] * bi + f_im[..., None] * br
    x_re = jnp.einsum('blgc,gpc->blgp', u, bb_re)
    x_im = jnp.einsum('blgc,gpc->blgp', u, bb_im)
    s_re0 = s_re0.astype(F32)
    s_im0 = s_im0.astype(F32)
    x_re = x_re.at[:, 0].add(ab_re * s_re0 - ab_im * s_im0)
    x_im = x_im.at[:, 0].add(ab_re * s_im0 + ab_im * s_re0)
    a_re = jnp.broadcast_to(ab_re, x_re.shape)
    a_im = jnp.broadcast_to(ab_im, x_im.shape)

    def combine(e1, e2):
        a1r, a1i, b1r, b1i = e1
        a2r, a2i, b2r, b2i = e2
        return (a1r * a2r - a1i * a2i, a1r * a2i + a1i * a2r,
                a2r * b1r - a2i * b1i + b2r, a2r * b1i + a2i * b1r + b2i)

    _, _, st_re, st_im = lax.associative_scan(combine, (a_re, a_im, x_re, x_im), axis=1)
    y = (jnp.einsum('blgp,gcp->blgc', st_re, c_re.astype(F32))
         - jnp.einsum('blgp,gcp->blgc', st_im, c_im.astype(F32))
         + d_skip.astype(F32) * u)
    y = jax.nn.gelu(y.reshape(B, L, D_MODEL)).astype(h.dtype)
    a, gt = jnp.split(y @ w_glu, 2, axis=-1)
    out = a * jax.nn.sigmoid(gt)
    return out, st_re[:, -1].astype(h.dtype), st_im[:, -1].astype(h.dtype)

def hier_moe(h, w_rg, b_rg, w_re, b_re, w1, w3, w2):
    shp = h.shape
    t = h.reshape(-1, D_MODEL)
    lg = (t @ w_rg + b_rg).astype(F32)
    pg = jax.nn.softmax(lg, axis=-1)
    g_idx = jnp.argmax(lg, axis=-1)
    p_group = jnp.take_along_axis(pg, g_idx[:, None], axis=-1)
    le = (t @ w_re + b_re).astype(F32).reshape(-1, N_GROUPS, EXPERTS_PER_GROUP)
    le = jnp.take_along_axis(le, g_idx[:, None, None], axis=1)[:, 0]
    pe = jax.nn.softmax(le, axis=-1)
    top_p, top_i = lax.top_k(pe, TOP_K)
    top_p = top_p / jnp.sum(top_p, axis=-1, keepdims=True) * p_group
    e_idx = g_idx[:, None] * EXPERTS_PER_GROUP + top_i
    comb = jnp.sum(jax.nn.one_hot(e_idx, N_EXPERTS, dtype=F32) * top_p[..., None], axis=1)
    hid = jax.nn.silu(jnp.einsum('td,edf->tef', t, w1)) * jnp.einsum('td,edf->tef', t, w3)
    hid = hid * comb.astype(hid.dtype)[..., None]
    out = jnp.einsum('tef,efd->td', hid, w2)
    return out.reshape(shp)

def run_trunk(x, c, conv0, delta0, ssm_re0, ssm_im0,
              norm_mix, w_mod_mix, b_mod_mix, norm_ffn, w_mod_ffn, b_mod_ffn, norm_final,
              gdn_w_in, gdn_conv_w, gdn_a_log, gdn_dt_bias, gdn_o_norm, gdn_w_out,
              s5_w_in, s5_lam_re, s5_lam_im, s5_log_dt, s5_b_re, s5_b_im, s5_c_re, s5_c_im, s5_d, s5_w_glu,
              moe_w_rg, moe_b_rg, moe_w_re, moe_b_re, moe_w1, moe_w3, moe_w2):
    new_conv, new_delta, new_re, new_im = [], [], [], []
    for i in range(DEPTH):
        j = i // N_MIXERS
        shift, scale, gate = ada_mod(c, w_mod_mix[i], b_mod_mix[i])
        hn = rmsnorm(x, norm_mix[i]) * (1.0 + scale) + shift
        if i % N_MIXERS == 0:
            out, cv, sd = gdn_mixer(hn, conv0[j], delta0[j], gdn_w_in[j], gdn_conv_w[j], gdn_a_log[j],
                                    gdn_dt_bias[j], gdn_o_norm[j], gdn_w_out[j])
            new_conv.append(cv)
            new_delta.append(sd)
        else:
            out, sr, si = s5_mixer(hn, ssm_re0[j], ssm_im0[j], s5_w_in[j], s5_lam_re[j], s5_lam_im[j],
                                   s5_log_dt[j], s5_b_re[j], s5_b_im[j], s5_c_re[j], s5_c_im[j],
                                   s5_d[j], s5_w_glu[j])
            new_re.append(sr)
            new_im.append(si)
        x = x + gate * out
        shift, scale, gate = ada_mod(c, w_mod_ffn[i], b_mod_ffn[i])
        hn = rmsnorm(x, norm_ffn[i]) * (1.0 + scale) + shift
        x = x + gate * hier_moe(hn, moe_w_rg[i], moe_b_rg[i], moe_w_re[i], moe_b_re[i],
                                moe_w1[i], moe_w3[i], moe_w2[i])
    y = rmsnorm(x, norm_final)
    return y, jnp.stack(new_delta), jnp.stack(new_conv), jnp.stack(new_re), jnp.stack(new_im)

def setup_inputs(seed: int = 0) -> dict:
    key = jax.random.key(seed)
    ks = iter(jax.random.split(key, 64))
    nrm = lambda shape, s: jax.random.normal(next(ks), shape, F32) * s
    D, NA, NB = D_MODEL, N_DELTA_LAYERS, N_SSM_LAYERS
    G, P = SSM_GROUPS, SSM_P
    inp = {}
    inp['x_prompt'] = nrm((BATCH, SEQ, D), 1.0)
    inp['x_sample'] = nrm((DEC_BATCH, DEC_SEQ, D), 1.0)
    inp['state_delta'] = nrm((NA, DEC_BATCH, GDN_HEADS, GDN_DK, GDN_DV), GDN_DK ** -0.5)
    inp['state_conv'] = nrm((NA, DEC_BATCH, CONV_W - 1, GDN_CONV_DIM), 1.0)
    inp['state_ssm_re'] = nrm((NB, DEC_BATCH, G, P), 0.3)
    inp['state_ssm_im'] = nrm((NB, DEC_BATCH, G, P), 0.3)
    inp['c_prompt'] = nrm((BATCH, D), 1.0)
    inp['c_sample'] = nrm((DEC_BATCH, D), 1.0)
    inp['norm_mix'] = 1.0 + nrm((DEPTH, D), 0.05)
    inp['w_mod_mix'] = nrm((DEPTH, D, 3 * D), 0.5 * D ** -0.5)
    inp['b_mod_mix'] = nrm((DEPTH, 3 * D), 0.01)
    inp['norm_ffn'] = 1.0 + nrm((DEPTH, D), 0.05)
    inp['w_mod_ffn'] = nrm((DEPTH, D, 3 * D), 0.5 * D ** -0.5)
    inp['b_mod_ffn'] = nrm((DEPTH, 3 * D), 0.01)
    inp['norm_final'] = 1.0 + nrm((D,), 0.05)
    inp['gdn_w_in'] = nrm((NA, D, GDN_IN), D ** -0.5)
    inp['gdn_conv_w'] = nrm((NA, CONV_W, GDN_CONV_DIM), CONV_W ** -0.5)
    inp['gdn_a_log'] = jnp.log(jax.random.uniform(next(ks), (NA, GDN_HEADS), F32, 1.0, 16.0))
    dt = jnp.exp(jax.random.uniform(next(ks), (NA, GDN_HEADS), F32, np.log(1e-3), np.log(1e-1)))
    inp['gdn_dt_bias'] = dt + jnp.log(-jnp.expm1(-dt))
    inp['gdn_o_norm'] = 1.0 + nrm((NA, GDN_DV), 0.05)
    inp['gdn_w_out'] = nrm((NA, GDN_V_DIM, D), GDN_V_DIM ** -0.5)
    inp['s5_w_in'] = nrm((NB, D, D), D ** -0.5)
    inp['s5_lam_re'] = -0.5 + nrm((NB, G, P), 0.01)
    inp['s5_lam_im'] = np.pi * jnp.arange(P, dtype=F32) + nrm((NB, G, P), 0.01)
    inp['s5_log_dt'] = jax.random.uniform(next(ks), (NB, G), F32, np.log(1e-3), np.log(1e-1))
    inp['s5_b_re'] = nrm((NB, G, P, SSM_GROUP), (2 * SSM_GROUP) ** -0.5)
    inp['s5_b_im'] = nrm((NB, G, P, SSM_GROUP), (2 * SSM_GROUP) ** -0.5)
    inp['s5_c_re'] = nrm((NB, G, SSM_GROUP, P), P ** -0.5)
    inp['s5_c_im'] = nrm((NB, G, SSM_GROUP, P), P ** -0.5)
    inp['s5_d'] = nrm((NB, G, SSM_GROUP), 1.0)
    inp['s5_w_glu'] = nrm((NB, D, 2 * D), D ** -0.5)
    inp['moe_w_rg'] = nrm((DEPTH, D, N_GROUPS), D ** -0.5)
    inp['moe_b_rg'] = nrm((DEPTH, N_GROUPS), 0.01)
    inp['moe_w_re'] = nrm((DEPTH, D, N_EXPERTS), D ** -0.5)
    inp['moe_b_re'] = nrm((DEPTH, N_EXPERTS), 0.01)
    inp['moe_w1'] = nrm((DEPTH, N_EXPERTS, D, D_FF_EXPERT), D ** -0.5)
    inp['moe_w3'] = nrm((DEPTH, N_EXPERTS, D, D_FF_EXPERT), D ** -0.5)
    inp['moe_w2'] = nrm((DEPTH, N_EXPERTS, D_FF_EXPERT, D), D_FF_EXPERT ** -0.5)
    return inp

def reference(x_prompt, x_sample, state_delta, state_conv, state_ssm_re, state_ssm_im, c_prompt, c_sample,
              norm_mix, w_mod_mix, b_mod_mix, norm_ffn, w_mod_ffn, b_mod_ffn, norm_final,
              gdn_w_in, gdn_conv_w, gdn_a_log, gdn_dt_bias, gdn_o_norm, gdn_w_out,
              s5_w_in, s5_lam_re, s5_lam_im, s5_log_dt, s5_b_re, s5_b_im, s5_c_re, s5_c_im, s5_d, s5_w_glu,
              moe_w_rg, moe_b_rg, moe_w_re, moe_b_re, moe_w1, moe_w3, moe_w2):
    weights = (norm_mix, w_mod_mix, b_mod_mix, norm_ffn, w_mod_ffn, b_mod_ffn, norm_final,
               gdn_w_in, gdn_conv_w, gdn_a_log, gdn_dt_bias, gdn_o_norm, gdn_w_out,
               s5_w_in, s5_lam_re, s5_lam_im, s5_log_dt, s5_b_re, s5_b_im, s5_c_re, s5_c_im, s5_d, s5_w_glu,
               moe_w_rg, moe_b_rg, moe_w_re, moe_b_re, moe_w1, moe_w3, moe_w2)
    bp = x_prompt.shape[0]
    p_conv0 = jnp.zeros((N_DELTA_LAYERS, bp, CONV_W - 1, GDN_CONV_DIM), state_conv.dtype)
    p_delta0 = jnp.zeros((N_DELTA_LAYERS, bp, GDN_HEADS, GDN_DK, GDN_DV), state_delta.dtype)
    p_re0 = jnp.zeros((N_SSM_LAYERS, bp, SSM_GROUPS, SSM_P), state_ssm_re.dtype)
    p_im0 = jnp.zeros((N_SSM_LAYERS, bp, SSM_GROUPS, SSM_P), state_ssm_im.dtype)
    y_prompt, p_delta, p_conv, p_ssm_re, p_ssm_im = run_trunk(
        x_prompt, c_prompt, p_conv0, p_delta0, p_re0, p_im0, *weights)
    y_sample, s_delta, s_conv, s_ssm_re, s_ssm_im = run_trunk(
        x_sample, c_sample, state_conv, state_delta, state_ssm_re, state_ssm_im, *weights)
    return (y_prompt, y_sample, p_delta, p_conv, p_ssm_re, p_ssm_im, s_delta, s_conv, s_ssm_re, s_ssm_im)


_drawn_inputs = setup_inputs


def setup_inputs(seed=0):
    import zlib

    import numpy as np

    out = dict(_drawn_inputs(seed))
    spreads = {}
    factors = {'b_mod_mix': 2.782,
     'b_mod_ffn': 6.33,
     'gdn_o_norm': 3.61,
     's5_lam_re': 13.631,
     'moe_b_rg': 3.381,
     'moe_b_re': 29.992}
    for name, (base, spread) in spreads.items():
        noise = np.random.default_rng([zlib.crc32(name.encode()), seed]).standard_normal(out[name].shape)
        drawn = base * np.exp(spread * noise) if base else spread * noise
        out[name] = jnp.asarray(drawn.astype(out[name].dtype))
    for name, factor in factors.items():
        out[name] = (out[name] * factor).astype(out[name].dtype)
    return out
```

```python
from contextlib import ExitStack

import numpy as np
import concourse.bass as bass
from concourse import mybir

F32 = mybir.dt.float32
ALU = mybir.AluOpType
ACT = mybir.ActivationFunctionType
AX = mybir.AxisListType

P = 128
D = 1024
KD = D // P
SEQ, NSEQ, LS = 512, 8, 8
TS = NSEQ * LS
T = SEQ + TS
HT = T // 2
H = 8
NCK = T // 8
NCP = SEQ // 8
NPAIR = 32
E, NG, EG = 16, 4, 4
EPS = 1e-6
NSLOT = 6
UNIT = 2048
NACC = 4
CW = 4
QKV = 24
NLEV = 7
IDENT, TRIU, TRIU8, ONES8, MISC, LEV = 0, 1, 2, 3, 4, 5
N_CONST = LEV + NLEV
MAGIC = 12582912.0
TWO_PI_HI = 6.28125
TWO_PI_LO = 0.0019353071795864769
BIG = 1e30
PI_LIM = 3.1415925
READ_BY_SCALAR = {"ssq", "ada", "l", "p", "X", "wT", "vn", "o", "vnT", "vtr", "oS", "on", "u", "zr", "zi", "yc", "gg"}


def constant_masks():
    j, i = np.meshgrid(np.arange(P), np.arange(P), indexing="ij")
    same = (i // LS) == (j // LS)
    misc = np.where(i < 4, j // 32 == i, np.where(i < 8, 8 - i, 0))
    m = [i == j, i >= j, (i >= j) & same, same, misc]
    for l in range(NLEV):
        b = 1 << l
        m.append((i // (2 * b) == j // (2 * b)) & ((i // b) % 2 == 1) & ((j // b) % 2 == 0))
    return np.ascontiguousarray(np.stack(m, 1).astype(np.float32))


class Counts:

    def __init__(self, book):
        self.book, self.n, self.loop = book, {}, {}

    def up(self, sem, *labels, by=1):
        self.n[id(sem)] = self.n.get(id(sem), 0) + by
        for label in labels:
            if label is not None:
                self.book["at", label] = self.n[id(sem)]
        return by

    def now(self, sem):
        n = self.n.get(id(sem), 0)
        if id(sem) in self.loop:
            i, per, _ = self.loop[id(sem)]
            return i * per + n
        return n

    def enter(self, sem, i, per):
        self.loop[id(sem)] = i, per, self.n.get(id(sem), 0)

    def leave(self, sem, times):
        _, per, base = self.loop.pop(id(sem))
        assert self.n[id(sem)] - base == per
        self.n[id(sem)] = base + times * per


def levels(t):
    return NLEV if t < 4 else 3


def ring_units():
    out = [("mod", m, u) for m in range(4) for u in range(12)]
    out += [("w_in", 0, u) for u in range(16)] + [("w_out", 0, u) for u in range(4)]
    out += [("moe", 0, u) for u in range(3 * E)]
    out += [("s5in", 0, u) for u in range(4)] + [("glu", 0, u) for u in range(8)]
    out += [("moe", 1, u) for u in range(3 * E)]
    return out



def trunk(nc, d, o, book):
    units = ring_units()
    unit_no = {u: n for n, u in enumerate(units)}
    with ExitStack() as ctx:
        def sb(name, shape):
            return ctx.enter_context(nc.sbuf_tensor(name, shape, F32))

        def sem(name):
            return ctx.enter_context(nc.semaphore(name))

        counts = Counts(book)
        up, now = counts.up, counts.now

        xT = sb("xT", [P, KD, T])
        hT = sb("hT", [P, KD, T])
        yT = sb("yT", [P, KD, T])
        zT = sb("zT", [P, KD, T])
        big = sb("big", [P, QKV * T])
        ring = sb("ring", [P, NSLOT, UNIT])
        modT = sb("modT", [P, 4, 24, 9])
        modA = sb("modA", [P, 4, KD, 9])
        rb = sb("rb", [P, T])
        extra = sb("extra", [P, 2, 1024])
        cst = sb("cst", [P, N_CONST, P])
        small = sb("small", [P, 4])
        ones = sb("ones", [P, P])
        cT = sb("cT", [P, KD, 9])
        scT = sb("scT", [P, KD, 9])
        bmod = sb("bmod", [P, 4, 24])
        nrm = sb("nrm", [P, 5, KD])
        w_ba = sb("w_ba", [P, KD, 16])
        hp = sb("hp", [P, 2, H])
        onrm = sb("onrm", [P, 1])
        lam = sb("lam", [P, 3, NPAIR])
        pw = sb("pw", [P, 2, 9, NPAIR])
        fz = sb("fz", [P, 2, NPAIR])
        s5t = sb("s5t", [P, 8, NPAIR])
        s5d = sb("s5d", [P, KD])
        wr = sb("wr", [P, 2, KD, 20])
        br = sb("br", [P, 2, 20])
        gt = sb("gt", [P, 10, 5, H])
        S = sb("S", [P, H, P])
        acc = ctx.enter_context(nc.psum_tensor("acc", [P, NACC, 2, 512], F32))

        hflat = hT[:, :, :].rearrange("p k t -> p (k t)")
        yflat = yT[:, :, :].rearrange("p k t -> p (k t)")
        m_sb = big[0:9, 0:2 * 3072].rearrange("p (b n) -> p b n", b=2)
        qkv = big[:, :].rearrange("p (m t) -> p m t", t=T)
        unit = [hflat[:, 1024 * i:1024 * (i + 1)] for i in range(4)]
        unit += [ring[:, s, 1024 * j:1024 * (j + 1)] for s in (2, 3) for j in range(2)]
        unit += [extra[:, j, :] for j in range(2)]
        EG, EX, AT, AB, M, MT, KBGT, KDECT, VB, QKE = range(10)
        raw = [yflat[:, 640 * i:640 * i + T + 3] for i in range(2)]
        sraw = [yflat[:, 1280 + 88 * i:1280 + 88 * (i + 1)].rearrange("p (b s) -> p b s", s=11) for i in range(2)]
        sq = [yflat[:, 1536 + T * i:1536 + T * (i + 1)] for i in range(2)]
        ln = [yflat[:, 2688 + T * i:2688 + T * (i + 1)] for i in range(2)]
        cs_in = extra[:, 0, 0:QKV * 24].rearrange("p (m b s) -> p m b s", b=NSEQ, s=3)
        cs_out = extra[:, 1, 0:QKV * 24].rearrange("p (m b s) -> p m b s", b=NSEQ, s=3)
        cp_out = extra[:, 1, 600:600 + QKV * 3].rearrange("p (m s) -> p m s", s=3)
        cw = extra[:, 1, 700:700 + QKV * CW].rearrange("p (m s) -> p m s", s=CW)
        BA, BB, BETA, GG, G1, G2, GCOL, GLAST, CKBG, CKDEC = range(10)
        s0v = [qkv[:, 8 * (h // 4):8 * (h // 4) + 8, P * (h % 4):P * (h % 4) + P] for h in range(H)]
        snew = [qkv[:, 16:24, P * i:P * i + P] for i in range(2)]
        vmask = [qkv[0:TS, 16:24, 256 + P * i:256 + P * i + P] for i in range(2)]
        half = 2 * NPAIR * NCK
        INC = big[:, 0:half].rearrange("p (r q c) -> p r q c", r=2, q=NPAIR)
        SIN = big[:, half:2 * half].rearrange("p (r q c) -> p r q c", r=2, q=NPAIR)
        Z = [big[:, half + 1024 * i:half + 1024 * (i + 1)] for i in range(2)]
        ZT = big[:, half + 2048:half + 4096].rearrange("p (r m n) -> p r m n", r=2, m=8)
        uM = [big[:, 2 * half + 4 * T * i:2 * half + 4 * T * (i + 1)].rearrange("p (j t) -> p j t", j=4)
              for i in range(2)]
        CA = [big[:, 2 * half + 1152 * i:2 * half + 1152 * (i + 1)].rearrange("p (m q c) -> p m q c", m=9, q=4)
              for i in range(2)]
        KB = big[:, 2 * half + 2304:2 * half + 3328].rearrange("p (m n) -> p m n", m=8)
        YS = big[0:NCK, 2 * half + 3328:2 * half + 4352].rearrange("p (t n) -> p t n", t=8)
        catmp = [big[:, 1152 * i:1152 * (i + 1)].rearrange("p (m q c) -> p m q c", m=9, q=4) for i in range(2)]
        BC = hflat[:, 0:4096].rearrange("p (k q c) -> p k q c", k=4, q=NPAIR)
        s0ri = hflat[:, 4096:4608].rearrange("p (r q b) -> p r q b", r=2, q=NPAIR)
        sflat = S[:, :, :].rearrange("p h n -> p (h n)")
        fin_p = sflat[:, 0:64].rearrange("p (r q) -> p r q", r=2)
        fin_s = sflat[:, 64:576].rearrange("p (r q b) -> p r q b", r=2, q=NPAIR)
        st1 = sflat[:, 576:640].rearrange("p (r q) -> p r q", r=2)
        st2 = sflat[:, 640:704].rearrange("p (r q) -> p r q", r=2)
        aim = sflat[:, 704:768].rearrange("p (r q) -> p r q", r=2)
        CB = big[:, 0:E * T].rearrange("p (e t) -> p e t", t=T)
        RC = [big[:, E * T + 1024 * i:E * T + 1024 * (i + 1)] for i in range(2)]
        hid = big[:, E * T:E * T + 4 * T].rearrange("p (b f t) -> p b f t", b=2, f=2)
        s1 = big[:, E * T + 4 * T:E * T + 6 * T].rearrange("p (f t) -> p f t", f=2)
        rt = extra[:, 0, :]

        acc_full = sem("acc_full")
        dve_drained = sem("dve_drained")
        act_drained = sem("act_drained")
        slot_loaded = [sem(f"slot{i}_loaded") for i in range(NSLOT)]
        consts_in, x_in, conv_in, s0_in, bc_in = (sem(n) for n in ("consts_in", "x_in", "conv_in", "s0_in", "bc_in"))
        snew_out = [sem("snew_out0"), sem("snew_out1")]
        stored, conv_stored = sem("stored"), sem("conv_stored")
        dve_order, act_order, pool_order = sem("dve_order"), sem("act_order"), sem("pool_order")
        hid_ready = sem("hid_ready")
        s5_angle_ready = sem("s5_angle_ready")
        gate_args_ready = sem("gate_args_ready")
        s5_b_ready = sem("s5_b_ready")
        ca_re_ready = sem("ca_re_ready")
        conv_done = sem("conv_done")
        decay_diff_ready = sem("decay_diff_ready")
        log_decay_ready = sem("log_decay_ready")
        g_ready = sem("g_ready")
        sample_input_ready = sem("sample_input_ready")
        l2_done = sem("l2_done")
        mod_ready = sem("mod_ready")
        x_scaled = sem("x_scaled")
        o_normed = sem("o_normed")
        out_ready = sem("out_ready")
        q_decayed = sem("q_decayed")
        route_diag_ready = sem("route_diag_ready")
        expert_diff_ready = sem("expert_diff_ready")
        group_diff_ready = sem("group_diff_ready")
        row_masks_ready = sem("row_masks_ready")
        s5_fin_ready = sem("s5_fin_ready")
        entry_states_ready = sem("entry_states_ready")
        x_ready = sem("x_ready")
        zr_ready = sem("zr_ready")
        qkv_silu_done = sem("qkv_silu_done")
        dt_ready = sem("dt_ready")
        decay_rows_ready = sem("decay_rows_ready")
        decay_cols_ready = sem("decay_cols_ready")
        decay_exp_ready = sem("decay_exp_ready")
        gelu_done = sem("gelu_done")
        prompt_input_ready = sem("prompt_input_ready")
        l2_squares_ready = sem("l2_squares_ready")
        squares_ready = sem("squares_ready")
        o_squares_ready = sem("o_squares_ready")
        expert_exp_ready = sem("expert_exp_ready")
        group_exp_ready = sem("group_exp_ready")
        silu_c_ready = sem("silu_c_ready")
        softplus_ready = sem("softplus_ready")
        trig_ready = sem("trig_ready")
        a_block_ready = sem("a_block_ready")
        ca_im_ready = sem("ca_im_ready")
        history_ready = sem("history_ready")
        ones_ready = sem("ones_ready")
        u_masked = sem("u_masked")
        v_masked = sem("v_masked")
        zi_ready = sem("zi_ready")

        def at(label):
            return book.get(("at", label), 1)

        def reader(name):
            stem = name[:min(name.find(c) for c in name if c.isdigit())] if any(c.isdigit() for c in name) else name
            return act_drained if stem in READ_BY_SCALAR else dve_drained

        def filled(name):
            return use(name) + 1

        def use(name):
            return book.get(("use", name), 0)

        def buf(name):
            return acc[:, use(name) % NACC, :, :]

        def flatbuf(name, n, w):
            return buf(name).rearrange("p b c -> p (b c)")[:, 0:n * w].rearrange("p (n w) -> p n w", w=w)

        def tok(name):
            return buf(name)[:, :, 0:HT]

        def halves(ap):
            return ap.rearrange("p (b t) -> p b t", b=2)

        def bc(ap, axis, n):
            x = ap.unsqueeze(axis)
            return x.broadcast_to([n if i == axis else s for i, s in enumerate(x.shape)])

        def um(k, n, rows=None):
            rows = n if rows is None else rows
            return unit[k][0:rows, 0:H * n].rearrange("p (h n) -> p h n", n=n)

        def ur(k, n):
            return unit[k][0:n, 0:H * P].rearrange("p (h n) -> p h n", n=P)

        tiles = [(t, P * t, P if t < 4 else TS) for t in range(5)]
        tri = lambda t: TRIU if t < 4 else TRIU8
        block = ctx.enter_context(nc.Block())

        rtv = {"L": rt[:, 0:100].rearrange("p (t c) -> p t c", t=5),
               "ge": rt[:, 100:120].rearrange("p (t c) -> p t c", t=5),
               "ohg": rt[:, 120:140].rearrange("p (t c) -> p t c", t=5),
               "t4": rt[:, 140:160].rearrange("p (t c) -> p t c", t=5),
               "t16": rt[:, 160:240].rearrange("p (t g e) -> p t g e", t=5, g=4),
               "sel": rt[:, 240:260].rearrange("p (t c) -> p t c", t=5),
               "oh1": rt[:, 260:280].rearrange("p (t c) -> p t c", t=5),
               "oh2": rt[:, 280:300].rearrange("p (t c) -> p t c", t=5),
               "gm": rt[:, 300:305], "pg": rt[:, 305:310], "m1": rt[:, 310:315], "m2": rt[:, 315:320],
               "e2": rt[:, 320:325], "w1": rt[:, 325:330], "w2": rt[:, 330:335], "tm": rt[:, 335:340],
               "comb": rt[:, 340:420].rearrange("p (t g e) -> p t g e", t=5, g=4)}

        def zview(ap):
            return ap.rearrange("p (m q c) -> p m q c", m=8, q=4)

        def powers(r, m0, m1, c):
            return bc(pw[:, r, m0:m1, 4 * c:4 * c + 4], 3, 32)

        def over_m(ap, n):
            return bc(ap, 1, n)

        def unit_source(kind, a, u):
            if kind == "mod":
                return d["w_mod_mix" if a % 2 == 0 else "w_mod_ffn"][a // 2, u]
            if kind == "moe":
                return d[("w1", "w3", "w2")[u % 3]][a, u // 3]
            return d[kind][u]

        @block.sync
        def _(sp):
            def consts(dst, src):
                sp.dma_start(dst, src).then_inc(consts_in, up(consts_in, by=16))

            sp.dma_start(xT[:, :, :], d["xT"]).then_inc(x_in, 16)
            consts(cT[:, :, :], d["cT"])
            for dst, src in ((cst[:, :, :], "masks"), (bmod[:, :, :], "bmod"), (nrm[:, :, :], "nrm"),
                             (w_ba[:, :, :], "w_ba"), (onrm[:, :], "onrm"), (s5d[:, :], "s5d"),
                             (wr[:, :, :, :], "wr")):
                consts(dst, d[src])
            for i, src in enumerate(("a_log", "dt_bias")):
                consts(hp[:, i, :], d[src].partition_broadcast(P))
            for l in range(2):
                consts(br[:, l, :], d["br"][l].partition_broadcast(P))
            consts(lam[:, 0:2, :], d["lam"])
            for g in range(2):
                consts(lam[64 * g:64 * g + 64, 2, :], d["log_dt"][g].partition_broadcast(64))
            book["consts"] = now(consts_in)

            def load(n):
                if n >= NSLOT:
                    sp.wait_ge(acc_full, book.get(("unit_read", n - NSLOT), 1))
                loaded = slot_loaded[n % NSLOT]
                sp.dma_start(ring[:, n % NSLOT, :], unit_source(*units[n])).then_inc(
                    loaded, up(loaded, ("unit", n), by=16))

            def moe_loads(layer):
                first = unit_no["moe", layer, 0]
                for j in range(6):
                    load(first + j)
                free = [book.get(("unit_read", first + j), 1) for j in range(6)]
                for s in slot_loaded:
                    counts.enter(s, None, 16)
                with sp.Fori(0, E // 2 - 1) as i:
                    for j in range(6):
                        s = slot_loaded[(first + j) % NSLOT]
                        sp.wait_ge(acc_full, i * 24 + free[j])
                        src = d[("w1", "w3", "w2")[j % 3]][layer]
                        sp.dma_start(ring[:, (first + j) % NSLOT, :], src[i * 2 + (2 + j // 3)]).then_inc(
                            s, up(s, by=16))
                for s in slot_loaded:
                    counts.leave(s, E // 2 - 1)

            for n in range(unit_no["w_in", 0, 0]):
                load(n)
            sp.dma_start(cs_in, d["conv"]).then_inc(conv_in, up(conv_in, by=16))
            sp.dma_start(cw, d["cw"]).then_inc(conv_in, up(conv_in, by=16))
            for n in range(unit_no["w_in", 0, 0], unit_no["moe", 0, 0]):
                load(n)
            sp.wait_ge(history_ready, at(f"cs{QKV - 1}"))
            sp.dma_start(o["s_conv"], cs_out).then_inc(conv_stored, up(conv_stored, by=16))
            sp.dma_start(o["p_conv"], cp_out).then_inc(conv_stored, up(conv_stored, by=16))
            sp.wait_ge(acc_full, filled("o3"))
            for h in range(H):
                sp.dma_start(s0v[h], d["s0"][h]).then_inc(s0_in, up(s0_in, by=16))
            sp.wait_ge(dve_drained, at("S3"))
            sp.dma_start(o["p_delta"], S[:, :, :]).then_inc(stored, up(stored, by=16))
            for h in range(H):
                sp.wait_ge(dve_drained, at(f"snew{h}"))
                sp.dma_start(o["s_delta"][h], snew[h % 2]).then_inc(snew_out[h % 2], up(snew_out[h % 2], by=16))
            sp.wait_ge(acc_full, filled("suS7"))
            moe_loads(0)
            for n in range(unit_no["s5in", 0, 0], unit_no["glu", 0, 0]):
                load(n)
            sp.wait_ge(acc_full, filled("u7"))
            sp.dma_start(BC, d["bc"]).then_inc(bc_in, up(bc_in, by=16))
            sp.dma_start(s0ri, d["s0ri"]).then_inc(bc_in, up(bc_in, by=16))
            for n in range(unit_no["glu", 0, 0], unit_no["moe", 1, 0]):
                load(n)
            sp.wait_ge(s5_fin_ready, at("s5fin"))
            sp.dma_start(o["p_ssm"], fin_p).then_inc(stored, up(stored, by=16))
            sp.dma_start(o["s_ssm"], fin_s).then_inc(stored, up(stored, by=16))
            moe_loads(1)
            sp.wait_ge(out_ready, at("out"))
            sp.dma_start(o["y"], yT[:, :, :]).then_inc(stored, up(stored, by=16))
            sp.wait_ge(stored, now(stored))
            sp.wait_ge(conv_stored, now(conv_stored))
            for s in snew_out:
                sp.wait_ge(s, now(s))

        @block.tensor
        def _(pe):
            state = {"n": 0}

            def begin(name):
                n = state["n"]
                book["use", name] = n
                book["name", n] = name
                if n >= NACC:
                    last = book["name", n - NACC]
                    pe.wait_ge(reader(last), at("read:" + last))
                state["n"] += 1
                return acc[:, n % NACC, :, :]

            def weights(n):
                pe.wait_ge(slot_loaded[n % NSLOT], at(("unit", n)))
                return ring[:, n % NSLOT, :]

            def project(name, w, rhs):
                ps = begin(name)
                for b in range(2):
                    for k in range(KD):
                        mm = pe.matmul(ps[:, b, 0:HT], w[:, k, :], rhs[:, k, HT * b:HT * b + HT],
                                       start=(k == 0), stop=(k == KD - 1))
                mm.then_inc(acc_full, 1)

            def norm_sums(i):
                pe.wait_ge(squares_ready, at(f"nsq{i}"))
                ps = begin(f"ssq{i}")
                for b in range(2):
                    for k in range(KD):
                        mm = pe.matmul(ps[:, b, 0:HT], ones[:, :], yT[:, k, HT * b:HT * b + HT],
                                       start=(k == 0), stop=(k == KD - 1))
                mm.then_inc(acc_full, 1)

            def await_input(i):
                pe.wait_ge(prompt_input_ready, at(f"h{i}"))
                pe.wait_ge(sample_input_ready, at(f"hs{i}"))

            def heads(name, lhsT, rhs, out=None):
                begin(name)
                for h in range(H):
                    mm = pe.matmul(out[:, h, :], lhsT(h), rhs(h), start=True, stop=True, skip_group_check=True)
                mm.then_inc(acc_full, 1)

            def adaln(m):
                for nb in range(6):
                    ps = begin(f"ada{m}_{nb}")
                    for kh in range(2):
                        n = unit_no["mod", m, 2 * nb + kh]
                        w = weights(n).rearrange("p (k c) -> p k c", k=4)
                        for k in range(4):
                            mm = pe.matmul(ps[0:9, 0, :], scT[:, 4 * kh + k, :], w[:, k, :],
                                           start=(kh + k == 0), stop=(kh + k == 4))
                        book["unit_read", n] = state["n"]
                    mm.then_inc(acc_full, 1)

            def adaln_turn(m):
                begin(f"adaT{m}")
                pe.wait_ge(act_drained, at(f"read:ada{m}_5"))
                out = flatbuf(f"adaT{m}", 24, 9)
                for j in range(24):
                    mm = pe.transpose(out[:, j, :], m_sb[:, m % 2, P * j:P * j + P], cst[0:9, IDENT, 0:9])
                mm.then_inc(acc_full, 1)

            def delta_tile(t, c0, n):
                k_ = lambda h: qkv[:, 8 + h, c0:c0 + n]
                q_ = lambda h: qkv[:, h, c0:c0 + n]
                v_ = lambda h: qkv[:, 16 + h, c0:c0 + n]
                for name, u, ready in ((f"gr{t}", M, f"ru{t}"), (f"br{t}", MT, f"rub{t}")):
                    pe.wait_ge(row_masks_ready, at(ready))
                    ps = begin(name)
                    w = min(512, H * n)
                    for b in range(H * n // w):
                        mm = pe.matmul(ps[:, b, 0:w], ones[0:n, :], unit[u][0:n, w * b:w * b + w],
                                       start=True, stop=True)
                    mm.then_inc(acc_full, 1)
                heads(f"kk{t}", k_, k_, flatbuf(f"kk{t}", H, n)[0:n])
                heads(f"qk{t}", k_, q_, flatbuf(f"qk{t}", H, n)[0:n])
                for name, src in ((f"kt{t}", k_), (f"vt{t}", v_)):
                    begin(name)
                    out = flatbuf(name, H, P)[0:n]
                    for h in range(H):
                        mm = pe.transpose(out[:, h, :], src(h), cst[:, IDENT, :])
                    mm.then_inc(acc_full, 1)
                pe.wait_ge(a_block_ready, at(f"ab{t}_0"))
                begin(f"A0{t}")
                out = flatbuf(f"A0{t}", H, n)[0:n]
                for h in range(H):
                    mm = pe.transpose(out[:, h, :], um(AB, n)[:, h, :], cst[0:n, IDENT, 0:n])
                mm.then_inc(acc_full, 1)
                for l in range(1, levels(t)):
                    pe.wait_ge(dve_drained, at(f"MT{t}_{l - 1}"))
                    pe.wait_ge(a_block_ready, at(f"ab{t}_{l}"))
                    heads(f"X{t}_{l}", lambda h: um(AB, n)[:, h, :], lambda h: um(M, n)[:, h, :],
                          flatbuf(f"X{t}_{l}", H, n)[0:n])
                    pe.wait_ge(act_drained, at(f"read:X{t}_{l}"))
                    if l < levels(t) - 1:
                        heads(f"MX{t}_{l}", lambda h: um(MT, n)[:, h, :], lambda h: um(EX, n)[:, h, :],
                              flatbuf(f"MX{t}_{l}", H, n)[0:n])
                    heads(f"MTX{t}_{l}", lambda h: um(EX, n)[:, h, :], lambda h: um(MT, n)[:, h, :],
                          flatbuf(f"MTX{t}_{l}", H, n)[0:n])
                pe.wait_ge(dve_drained, at(f"MT{t}_{levels(t) - 1}"))
                pe.wait_ge(dve_drained, at(f"read:kt{t}"))
                pe.wait_ge(dve_drained, at(f"read:vt{t}"))
                heads(f"wT{t}", lambda h: ur(KBGT, n)[:, h, :], lambda h: um(MT, n)[:, h, :],
                      flatbuf(f"wT{t}", H, n))
                pe.wait_ge(act_drained, at(f"read:wT{t}"))
                if t < 4:
                    if t:
                        pe.wait_ge(dve_drained, at(f"S{t - 1}"))
                    begin(f"vn{t}")
                    out = flatbuf(f"vn{t}", H, P)
                    for h in range(H):
                        pe.matmul(out[:, h, :], um(MT, n)[:, h, :], ur(VB, n)[:, h, :], start=True, stop=False,
                                  skip_group_check=True)
                        mm = pe.matmul(out[:, h, :], um(EX, n, P)[:, h, :], S[:, h, :], start=False, stop=True,
                                       skip_group_check=True)
                    mm.then_inc(acc_full, 1)
                    pe.wait_ge(act_drained, at(f"read:vn{t}"))
                    pe.wait_ge(q_decayed, at(f"qdT{t}"))
                    begin(f"o{t}")
                    out = flatbuf(f"o{t}", H, n)
                    for h in range(H):
                        pe.matmul(out[:, h, :], S[:, h, :], q_(h), start=True, stop=False, skip_group_check=True)
                        mm = pe.matmul(out[:, h, :], ur(AB, n)[:, h, :], um(QKE, n)[:, h, :], start=False,
                                       stop=True, skip_group_check=True)
                    mm.then_inc(acc_full, 1)
                    heads(f"su{t}", lambda h: ur(KDECT, n)[:, h, :], lambda h: ur(AB, n)[:, h, :],
                          flatbuf(f"su{t}", H, P))
                    return
                pe.wait_ge(s0_in, 16 * H)
                begin("vnT")
                out = flatbuf("vnT", H, n)
                for h in range(H):
                    pe.matmul(out[:, h, :], ur(VB, n)[:, h, :], um(MT, n)[:, h, :], start=True, stop=False,
                              skip_group_check=True)
                    for b in range(NSEQ):
                        mm = pe.matmul(out[:, h, LS * b:LS * b + LS], s0v[h][:, b, :],
                                       um(EX, n, P)[:, h, LS * b:LS * b + LS], start=False, stop=(b == NSEQ - 1),
                                       skip_group_check=True)
                mm.then_inc(acc_full, 1)
                pe.wait_ge(act_drained, at("read:vnT"))
                begin("vtr")
                out = flatbuf("vtr", H, P)[0:n]
                for h in range(H):
                    mm = pe.transpose(out[:, h, :], um(M, n, P)[:, h, :], cst[:, IDENT, :])
                mm.then_inc(acc_full, 1)
                pe.wait_ge(act_drained, at("read:vtr"))
                pe.wait_ge(q_decayed, at(f"qdT{t}"))
                begin("oS")
                out = flatbuf("oS", H, n)
                for h in range(H):
                    pe.matmul(out[:, h, :], ur(AB, n)[:, h, :], um(QKE, n)[:, h, :], start=True, stop=False,
                              skip_group_check=True)
                    for b in range(NSEQ):
                        mm = pe.matmul(out[:, h, LS * b:LS * b + LS], s0v[h][:, b, :],
                                       q_(h)[:, LS * b:LS * b + LS], start=False, stop=(b == NSEQ - 1),
                                       skip_group_check=True)
                mm.then_inc(acc_full, 1)
                for h in range(H):
                    pe.wait_ge(v_masked, at(f"vm{h}"))
                    ps = begin(f"suS{h}")
                    for b in range(2):
                        mm = pe.matmul(ps[:, b, :], ur(KDECT, n)[:, h, :], vmask[h % 2][:, 4 * b:4 * b + 4, :],
                                       start=True, stop=True)
                    mm.then_inc(acc_full, 1)

            def route(layer, i):
                await_input(i)
                ps = begin(f"rt{layer}")
                for t, c0, n in tiles:
                    for k in range(KD):
                        mm = pe.matmul(ps[0:n, 0, 20 * t:20 * t + 20], hT[:, k, c0:c0 + n], wr[:, layer, k, :],
                                       start=(k == 0), stop=(k == KD - 1), skip_group_check=True)
                mm.then_inc(acc_full, 1)
                for t, c0, n in tiles:
                    for g in range(2):
                        pe.wait_ge(route_diag_ready, at(f"rc{layer}_{t}_{g}"))
                        ps = begin(f"cb{layer}_{t}_{g}")
                        w = min(512, 8 * n)
                        for b in range(8 * n // w):
                            mm = pe.matmul(ps[:, b, 0:w], ones[0:n, :], RC[g][0:n, w * b:w * b + w],
                                           start=True, stop=True)
                        mm.then_inc(acc_full, 1)

            def moe(layer):
                n0 = state["n"]
                first = unit_no["moe", layer, 0]
                v0, a0 = book.get(("moe_v", layer), 4), book.get(("moe_a", layer), 4)
                h0 = (2 * E + 2) * layer
                with pe.Fori(0, E // 2) as i:
                    def claim(k):
                        if k in (0, 1, 2, 3):
                            pe.wait_ge(dve_drained, i * 20 + (v0 - 3 + k))
                        else:
                            j = (k - 4) % 12
                            if j in (0, 2):
                                pe.wait_ge(act_drained, i * 4 + (a0 + 2 * ((k - 4) // 12) + j // 2 + 1))
                            else:
                                r = {1: 1, 3: 2}.get(j, j - 1)
                                pe.wait_ge(dve_drained, i * 20 + (v0 + 10 * ((k - 4) // 12) + r))
                        return acc[:, (n0 + k) % NACC, :, :]

                    for e in range(2):
                        slots = [(first + 3 * e + s) % NSLOT for s in range(3)]
                        w1, w3, w2 = (ring[:, s, :] for s in slots)
                        loaded = [at(("unit", first + 3 * e + x)) for x in range(3)]
                        for f in range(2):
                            for x, w in ((0, w1), (1, w3)):
                                if f == 0:
                                    pe.wait_ge(slot_loaded[slots[x]], i * 16 + loaded[x])
                                ps = claim(12 * e + 2 * f + x)
                                wv = w.rearrange("p (m k c) -> p m k c", m=2, k=KD)
                                for b in range(2):
                                    for k in range(KD):
                                        mm = pe.matmul(ps[:, b, 0:HT], wv[:, f, k, :],
                                                       hT[:, k, HT * b:HT * b + HT],
                                                       start=(k == 0), stop=(k == KD - 1))
                                mm.then_inc(acc_full, 1)
                        pe.wait_ge(slot_loaded[slots[2]], i * 16 + loaded[2])
                        pe.wait_ge(hid_ready, i * 4 + (h0 + 2 * e + 4))
                        wv = w2.rearrange("p (m k c) -> p m k c", m=KD, k=2)
                        for m in range(KD):
                            ps = claim(12 * e + 4 + m)
                            for b in range(2):
                                for f in range(2):
                                    mm = pe.matmul(ps[:, b, 0:HT], wv[:, m, f, :],
                                                   hid[:, e, f, HT * b:HT * b + HT],
                                                   start=(f == 0), stop=(f == 1))
                            mm.then_inc(acc_full, 1)
                for e in range(2):
                    base = n0 + 12 * e
                    book["unit_read", first + 3 * e] = base + 3
                    book["unit_read", first + 3 * e + 1] = base + 4
                    book["unit_read", first + 3 * e + 2] = base + 12
                last = 24 * (E // 2 - 1)
                for j in range(6):
                    book["unit_read", first + 3 * E - 6 + j] = book["unit_read", first + j] + last
                state["n"] = n0 + 24 * (E // 2)
                book["moe_first_use", layer] = n0
                for j in range(8):
                    book["name", state["n"] - 8 + j] = f"y{layer}_{j}"
                    book["use", f"y{layer}_{j}"] = state["n"] - 8 + j

            def s5():
                await_input(2)
                for m in range(KD):
                    n = unit_no["s5in", 0, m // 2]
                    w = weights(n).rearrange("p (m k c) -> p m k c", m=2, k=KD)
                    project(f"u{m}", w[:, m % 2], hT)
                    book["unit_read", n] = state["n"]
                for c in range(KD):
                    for r, name in enumerate(("zr", "zi")):
                        if r == 0:
                            pe.wait_ge(zr_ready, at(f"zr{c}"))
                        else:
                            pe.wait_ge(zi_ready, at(f"zi{c}"))
                        begin(f"{name}{c}")
                        out = flatbuf(f"{name}{c}", 8, P)
                        for m in range(8):
                            mm = pe.transpose(out[:, m, :], Z[r][:, P * m:P * m + P], cst[:, IDENT, :])
                        mm.then_inc(acc_full, 1)
                    pe.wait_ge(act_drained, at(f"read:zi{c}"))
                    pe.wait_ge(u_masked, at(f"um{c}"))
                    ps = begin(f"inc{c}")
                    uv = uM[c % 2].rearrange("p j (c t) -> p t j c", t=8)
                    for r in range(2):
                        for tau in range(8):
                            mm = pe.matmul(ps[:, r, 0:4 * NCK].rearrange("p (j c) -> p j c", j=4),
                                           ZT[:, r, 7 - tau, :], uv[:, tau], start=(tau == 0), stop=(tau == 7))
                    mm.then_inc(acc_full, 1)
                pe.wait_ge(entry_states_ready, at("sin"))
                for c in range(KD):
                    pe.wait_ge(ca_re_ready, at(f"car{c}"))
                    pe.wait_ge(ca_im_ready, at(f"cai{c}"))
                    ps = begin(f"K{c}")
                    for j in range(4):
                        q = 4 * c + j
                        for r in range(2):
                            mm = pe.matmul(ps[32 * j:32 * j + 32, 0, 0:256].rearrange("p (m c) -> p m c", m=8),
                                           BC[:, r, q, :], CA[r][:, 0:8, j, :], start=(r == 0), stop=(r == 1),
                                           skip_group_check=True)
                    mm.then_inc(acc_full, 1)
                    ps = begin(f"yc{c}")
                    for j in range(4):
                        q = 4 * c + j
                        for r in range(2):
                            mm = pe.matmul(ps[0:NCK, j // 2, 256 * (j % 2):256 * (j % 2) + 256].rearrange(
                                               "p (m c) -> p m c", m=8),
                                           SIN[:, r, q, :], CA[r][:, 1:9, j, :], start=(r == 0), stop=(r == 1),
                                           skip_group_check=True)
                    mm.then_inc(acc_full, 1)
                    pe.wait_ge(dve_drained, at(f"kb{c}"))
                    pe.wait_ge(act_drained, at(f"read:yc{c}"))
                    ps = begin(f"ys{c}")
                    uv = zT[:, c, :].rearrange("p (c t) -> p t c", t=8)
                    for b in range(2):
                        ov = ps[:, b, 0:4 * NCK].rearrange("p (t c) -> p t c", t=4)
                        for lag in range(8):
                            lo, hi = max(4 * b, lag), 4 * b + 4
                            if lo >= hi:
                                continue
                            pe.matmul(ov[:, lo - 4 * b:4], KB[:, lag, :], uv[:, lo - lag:hi - lag],
                                      start=(lag == 0), stop=False, skip_group_check=True)
                        for tau in range(4):
                            mm = pe.matmul(ov[:, tau, :], YS[:, 4 * b + tau, :], cst[0:NCK, IDENT, 0:NCK],
                                           start=False, stop=(tau == 3), skip_group_check=True)
                    mm.then_inc(acc_full, 1)
                pe.wait_ge(gelu_done, at("gelu"))
                for m in range(KD):
                    n = unit_no["glu", 0, m]
                    w = weights(n).rearrange("p (m k c) -> p m k c", m=2, k=KD)
                    project(f"ga{m}", w[:, 0], yT)
                    project(f"gg{m}", w[:, 1], yT)
                    book["unit_read", n] = state["n"]

            pe.wait_ge(consts_in, book.get("consts", 16))
            pe.wait_ge(ones_ready, at("ones"))
            norm_sums(0)
            pe.wait_ge(silu_c_ready, at("silu_c"))
            for m in range(4):
                adaln(m)
                if m:
                    adaln_turn(m - 1)
            adaln_turn(3)
            await_input(0)
            ps = begin("ba")
            for t, c0, n in tiles:
                for k in range(KD):
                    mm = pe.matmul(ps[0:n, 0, 16 * t:16 * t + 16], hT[:, k, c0:c0 + n], w_ba[:, k, :],
                                   start=(k == 0), stop=(k == KD - 1), skip_group_check=True)
            mm.then_inc(acc_full, 1)
            for m in range(32):
                n = unit_no["w_in", 0, m // 2]
                w = weights(n).rearrange("p (m k c) -> p m k c", m=2, k=KD)
                project(f"p{m}", w[:, m % 2], hT)
                book["unit_read", n] = state["n"]
                if 2 <= m < 18:
                    pe.wait_ge(l2_squares_ready, at(f"l2sq{m - 2}"))
                    ps = begin(f"l{m - 2}")
                    for b in range(2):
                        mm = pe.matmul(ps[:, b, 0:HT], ones[:, :], sq[m % 2][:, HT * b:HT * b + HT],
                                       start=True, stop=True)
                    mm.then_inc(acc_full, 1)
            pe.wait_ge(g_ready, at("gg"))
            ps = begin("G")
            for t, c0, n in tiles:
                for b, mask in ((0, cst[0:n, tri(t), 0:n]), (1, ones[0:n, 0:n] if t < 4 else cst[0:n, ONES8, 0:n])):
                    mm = pe.matmul(ps[0:n, b, 8 * t:8 * t + 8], mask, gt[0:n, GG, t, :], start=True, stop=True,
                                   skip_group_check=True)
            mm.then_inc(acc_full, 1)
            pe.wait_ge(l2_done, at("l215"))
            pe.wait_ge(qkv_silu_done, at("act23"))
            for t, c0, n in tiles:
                delta_tile(t, c0, n)
            pe.wait_ge(o_squares_ready, at("osq"))
            for h in range(H):
                ps = begin(f"on{h}")
                for b in range(2):
                    mm = pe.matmul(ps[:, b, 0:HT], ones[:, :], hT[:, h, HT * b:HT * b + HT], start=True, stop=True)
                mm.then_inc(acc_full, 1)
            pe.wait_ge(o_normed, at("onorm"))
            for m in range(KD):
                n = unit_no["w_out", 0, m // 2]
                w = weights(n).rearrange("p (m k c) -> p m k c", m=2, k=KD)
                project(f"w{m}", w[:, m % 2], yT)
                book["unit_read", n] = state["n"]
            norm_sums(1)
            route(0, 1)
            moe(0)
            norm_sums(2)
            s5()
            norm_sums(3)
            route(1, 3)
            moe(1)
            norm_sums(4)

        @block.scalar
        def _(act):
            def step(ins):
                ins.then_inc(act_order, up(act_order))
                act.wait_ge(act_order, now(act_order))

            def norm(i, m):
                act.wait_ge(x_ready, at(f"x{i}"))
                act.activation(yT[:, :, :], xT[:, :, :], ACT.Square).then_inc(
                    squares_ready, up(squares_ready, f"nsq{i}"))
                act.wait_ge(squares_ready, now(squares_ready))
                act.wait_ge(acc_full, filled(f"ssq{i}"))
                act.activation(halves(rb[:, :]), tok(f"ssq{i}"), ACT.Sqrt, bias=small[:, 0:1], scale=1.0 / D).then_inc(
                    act_drained, up(act_drained, f"read:ssq{i}"))
                act.wait_ge(act_drained, now(act_drained))
                if m is None:
                    return
                act.wait_ge(x_scaled, at(f"npre{i}"))
                act.wait_ge(mod_ready, at(f"mod{m}"))
                for k in range(KD):
                    ins = act.activation(hT[:, k, 0:SEQ], yT[:, k, 0:SEQ], ACT.Identity,
                                         bias=modT[:, m, k, 0:1], scale=modA[:, m, k, 0:1])
                    if k < KD - 1:
                        ins.then_inc(act_order, up(act_order))
                act.wait_ge(act_order, now(act_order))
                ins.then_inc(prompt_input_ready, up(prompt_input_ready, f"h{i}"))
                act.wait_ge(prompt_input_ready, now(prompt_input_ready))

            def moe(layer):
                n0 = book.get(("moe_first_use", layer), 0)
                a0 = now(act_drained)
                book["moe_a", layer] = a0
                h0 = (2 * E + 2) * layer
                counts.enter(act_drained, None, 4)
                with act.Fori(0, E // 2) as i:
                    for e in range(2):
                        for f in range(2):
                            k = 12 * e + 2 * f
                            act.wait_ge(acc_full, i * 24 + (n0 + k + 1))
                            act.wait_ge(hid_ready, i * 4 + (h0 + 2 * e + f + 1))
                            act.activation(halves(s1[:, f, :]), acc[:, (n0 + k) % NACC, :, 0:HT],
                                           ACT.Silu).then_inc(act_drained, up(act_drained))
                counts.leave(act_drained, E // 2)

            act.wait_ge(consts_in, book.get("consts", 16))
            act.wait_ge(ones_ready, at("ones"))
            act.activation(scT[:, :, :], cT[:, :, :], ACT.Silu).then_inc(silu_c_ready, up(silu_c_ready, "silu_c"))
            act.wait_ge(silu_c_ready, now(silu_c_ready))
            step(act.activation(lam[:, 2, :], lam[:, 2, :], ACT.Exp))
            act.activation(hp[:, 0, :], hp[:, 0, :], ACT.Exp).then_inc(dt_ready, up(dt_ready, "dt"))
            act.wait_ge(dt_ready, now(dt_ready))
            act.wait_ge(s5_angle_ready, at("ang"))
            step(act.activation(s5t[:, 0, :], s5t[:, 0, :], ACT.Exp))
            step(act.activation(s5t[:, 3, :], s5t[:, 1, :], ACT.Sin))
            act.activation(s5t[:, 4, :], s5t[:, 2, :], ACT.Sin, bias=small[:, 2:3], scale=-1.0).then_inc(
                trig_ready, up(trig_ready, "trig"))
            act.wait_ge(trig_ready, now(trig_ready))
            act.wait_ge(x_in, 16)
            act.activation(yT[:, :, :], xT[:, :, :], ACT.Square).then_inc(squares_ready, up(squares_ready, "nsq0"))
            act.wait_ge(squares_ready, now(squares_ready))
            act.wait_ge(acc_full, filled("ssq0"))
            act.activation(halves(rb[:, :]), tok("ssq0"), ACT.Sqrt, bias=small[:, 0:1], scale=1.0 / D).then_inc(
                act_drained, up(act_drained, "read:ssq0"))
            act.wait_ge(act_drained, now(act_drained))
            for m in range(4):
                for nb in range(6):
                    act.wait_ge(acc_full, filled(f"ada{m}_{nb}"))
                    if m >= 2 and nb == 0:
                        act.wait_ge(acc_full, filled(f"adaT{m - 2}"))
                    act.activation(m_sb[:, m % 2, 512 * nb:512 * nb + 512], buf(f"ada{m}_{nb}")[0:9, 0, :],
                                         ACT.Copy).then_inc(act_drained, up(act_drained, f"read:ada{m}_{nb}"))
                    act.wait_ge(act_drained, now(act_drained))
            act.wait_ge(x_scaled, at("npre0"))
            act.wait_ge(mod_ready, at("mod0"))
            for k in range(KD):
                ins = act.activation(hT[:, k, 0:SEQ], yT[:, k, 0:SEQ], ACT.Identity,
                                     bias=modT[:, 0, k, 0:1], scale=modA[:, 0, k, 0:1])
                if k < KD - 1:
                    ins.then_inc(act_order, up(act_order))
            act.wait_ge(act_order, now(act_order))
            ins.then_inc(prompt_input_ready, up(prompt_input_ready, "h0"))
            act.wait_ge(prompt_input_ready, now(prompt_input_ready))
            act.wait_ge(gate_args_ready, at("ba"))
            step(act.activation(gt[:, BETA], gt[:, BB], ACT.Sigmoid))
            step(act.activation(gt[:, G1], gt[:, G2], ACT.Exp, scale=-1.0))
            act.activation(gt[:, G2], gt[:, G1], ACT.Ln, bias=1.0).then_inc(
                softplus_ready, up(softplus_ready, "splus"))
            act.wait_ge(softplus_ready, now(softplus_ready))
            for m in range(32 + 3):
                if m < QKV:
                    act.wait_ge(acc_full, filled(f"p{m}"))
                    if m >= 2:
                        act.wait_ge(conv_done, at(f"conv{m - 2}"))
                        act.wait_ge(history_ready, at(f"cs{m - 2}"))
                    act.activation(halves(raw[m % 2][:, 3:3 + T]), tok(f"p{m}"), ACT.Copy).then_inc(
                        act_drained, up(act_drained, f"read:p{m}"))
                    act.wait_ge(act_drained, now(act_drained))
                elif m < 32:
                    act.wait_ge(acc_full, filled(f"p{m}"))
                    act.activation(halves(zT[:, m - QKV, :]), tok(f"p{m}"), ACT.Silu).then_inc(
                        act_drained, up(act_drained, f"read:p{m}"))
                    act.wait_ge(act_drained, now(act_drained))
                if 1 <= m <= QKV:
                    act.wait_ge(conv_done, at(f"conv{m - 1}"))
                    act.activation(qkv[:, m - 1, :], qkv[:, m - 1, :], ACT.Silu).then_inc(
                        qkv_silu_done, up(qkv_silu_done, f"act{m - 1}"))
                    act.wait_ge(qkv_silu_done, now(qkv_silu_done))
                if 1 <= m <= 16:
                    if m >= 3:
                        act.wait_ge(acc_full, filled(f"l{m - 3}"))
                    act.activation(sq[(m - 1) % 2], qkv[:, m - 1, :], ACT.Square).then_inc(
                        l2_squares_ready, up(l2_squares_ready, f"l2sq{m - 1}"))
                    act.wait_ge(l2_squares_ready, now(l2_squares_ready))
                if 2 <= m < 18:
                    act.wait_ge(acc_full, filled(f"l{m - 2}"))
                    if m >= 4:
                        act.wait_ge(l2_done, at(f"l2{m - 4}"))
                    is_q = m - 2 < 8
                    act.activation(halves(ln[m % 2]), tok(f"l{m - 2}"), ACT.Sqrt,
                                         bias=small[:, 1:2] if is_q else small[:, 0:1],
                                         scale=float(P) if is_q else 1.0).then_inc(
                                             act_drained, up(act_drained, f"read:l{m - 2}"))
                    act.wait_ge(act_drained, now(act_drained))
            act.wait_ge(log_decay_ready, at("gcol"))
            step(act.activation(gt[:, G1], gt[:, GCOL], ACT.Exp))
            act.activation(gt[:, CKDEC], gt[:, G2], ACT.Exp).then_inc(decay_cols_ready, up(decay_cols_ready, "ecol"))
            act.wait_ge(decay_cols_ready, now(decay_cols_ready))
            for t, c0, n in tiles:
                act.wait_ge(acc_full, filled(f"gr{t}"))
                if t:
                    act.wait_ge(dve_drained, at(f"S{t - 1}"))
                act.activation(um(EG, n, P), flatbuf(f"gr{t}", H, n), ACT.Exp).then_inc(
                    decay_rows_ready, up(decay_rows_ready, f"eG{t}"))
                act.wait_ge(decay_rows_ready, now(decay_rows_ready))
                act.wait_ge(decay_diff_ready, at(f"diff{t}"))
                act.activation(um(EX, n), um(EX, n), ACT.Exp).then_inc(decay_exp_ready, up(decay_exp_ready, f"ex{t}"))
                act.wait_ge(decay_exp_ready, now(decay_exp_ready))
                for l in range(1, levels(t)):
                    act.wait_ge(acc_full, filled(f"X{t}_{l}"))
                    if l == 1:
                        act.wait_ge(dve_drained, at(f"read:qk{t}"))
                    else:
                        act.wait_ge(acc_full, filled(f"MTX{t}_{l - 1}"))
                    act.activation(um(EX, n), flatbuf(f"X{t}_{l}", H, n)[0:n], ACT.Copy).then_inc(
                        act_drained, up(act_drained, f"read:X{t}_{l}"))
                    act.wait_ge(act_drained, now(act_drained))
                act.wait_ge(acc_full, filled(f"wT{t}"))
                act.activation(um(EX, n, P), flatbuf(f"wT{t}", H, n), ACT.Copy).then_inc(
                    act_drained, up(act_drained, f"read:wT{t}"))
                act.wait_ge(act_drained, now(act_drained))
                if t < 4:
                    act.wait_ge(acc_full, filled(f"vn{t}"))
                    act.activation(ur(AB, n), flatbuf(f"vn{t}", H, P), ACT.Copy).then_inc(
                        act_drained, up(act_drained, f"read:vn{t}"))
                    act.wait_ge(act_drained, now(act_drained))
                    act.wait_ge(acc_full, filled(f"o{t}"))
                    act.activation(yT[:, :, c0:c0 + n], flatbuf(f"o{t}", H, n), ACT.Copy).then_inc(
                        act_drained, up(act_drained, f"read:o{t}"))
                    act.wait_ge(act_drained, now(act_drained))
                else:
                    act.wait_ge(acc_full, filled("vnT"))
                    act.activation(um(M, n, P), flatbuf("vnT", H, n), ACT.Copy).then_inc(
                        act_drained, up(act_drained, "read:vnT"))
                    act.wait_ge(act_drained, now(act_drained))
                    act.wait_ge(acc_full, filled("vtr"))
                    act.activation(ur(AB, n), flatbuf("vtr", H, P)[0:n], ACT.Copy).then_inc(
                        act_drained, up(act_drained, "read:vtr"))
                    act.wait_ge(act_drained, now(act_drained))
                    act.wait_ge(acc_full, filled("oS"))
                    act.activation(yT[:, :, c0:c0 + n], flatbuf("oS", H, n), ACT.Copy).then_inc(
                        act_drained, up(act_drained, "read:oS"))
                    act.wait_ge(act_drained, now(act_drained))
            act.wait_ge(dve_drained, at("snew7"))
            act.activation(hT[:, :, :], yT[:, :, :], ACT.Square).then_inc(o_squares_ready, up(o_squares_ready, "osq"))
            act.wait_ge(o_squares_ready, now(o_squares_ready))
            for h in range(H):
                act.wait_ge(acc_full, filled(f"on{h}"))
                act.activation(halves(hT[:, h, :]), tok(f"on{h}"), ACT.Sqrt, bias=small[:, 0:1],
                                     scale=1.0 / P).then_inc(act_drained, up(act_drained, f"read:on{h}"))
                act.wait_ge(act_drained, now(act_drained))
            norm(1, 1)

            def route(layer):
                act.wait_ge(group_diff_ready, at(f"rga{layer}"))
                act.activation(rtv["ge"], rtv["ge"], ACT.Exp).then_inc(
                    group_exp_ready, up(group_exp_ready, f"rgb{layer}"))
                act.wait_ge(group_exp_ready, now(group_exp_ready))
                act.wait_ge(expert_diff_ready, at(f"rea{layer}"))
                act.activation(rtv["e2"], rtv["e2"], ACT.Exp).then_inc(
                    expert_exp_ready, up(expert_exp_ready, f"reb{layer}"))
                act.wait_ge(expert_exp_ready, now(expert_exp_ready))

            route(0)
            moe(0)
            norm(2, 2)
            for m in range(KD):
                act.wait_ge(acc_full, filled(f"u{m}"))
                act.activation(halves(zT[:, m, :]), tok(f"u{m}"), ACT.Copy).then_inc(
                    act_drained, up(act_drained, f"read:u{m}"))
                act.wait_ge(act_drained, now(act_drained))
            for c in range(KD):
                for r, name in enumerate(("zr", "zi")):
                    act.wait_ge(acc_full, filled(f"{name}{c}"))
                    if c and r == 0:
                        act.wait_ge(acc_full, filled(f"inc{c - 1}"))
                    act.activation(ZT[:, r], flatbuf(f"{name}{c}", 8, P), ACT.Copy).then_inc(
                        act_drained, up(act_drained, f"read:{name}{c}"))
                    act.wait_ge(act_drained, now(act_drained))
            for c in range(KD):
                act.wait_ge(acc_full, filled(f"yc{c}"))
                if c:
                    act.wait_ge(acc_full, filled(f"ys{c - 1}"))
                else:
                    act.wait_ge(entry_states_ready, at("sin"))
                act.activation(YS.rearrange("p t (j c) -> p j t c", j=4),
                                     flatbuf(f"yc{c}", 4, 256)[0:NCK].rearrange("p j (t c) -> p j t c", t=8),
                                     ACT.Copy).then_inc(act_drained, up(act_drained, f"read:yc{c}"))
                act.wait_ge(act_drained, now(act_drained))
            act.wait_ge(dve_drained, at("ysum"))
            act.activation(yT[:, :, :], yT[:, :, :], ACT.Gelu_apprx_tanh).then_inc(gelu_done, up(gelu_done, "gelu"))
            act.wait_ge(gelu_done, now(gelu_done))
            for m in range(KD):
                act.wait_ge(acc_full, filled(f"gg{m}"))
                if m >= 2:
                    act.wait_ge(dve_drained, at(f"glu{m - 2}"))
                act.activation(halves(extra[:, m % 2, 0:T]), tok(f"gg{m}"), ACT.Sigmoid).then_inc(
                    act_drained, up(act_drained, f"read:gg{m}"))
                act.wait_ge(act_drained, now(act_drained))
            norm(3, 3)
            route(1)
            moe(1)
            norm(4, None)

        @block.vector
        def _(dve):
            def step(ins):
                ins.then_inc(dve_order, up(dve_order))
                dve.wait_ge(dve_order, now(dve_order))

            tt, ts, stt = dve.tensor_tensor, dve.tensor_scalar, dve.scalar_tensor_tensor

            def seqs(ap):
                return ap.rearrange("p k (b s) -> p k b s", s=LS)

            def norm(i, m):
                dve.wait_ge(act_drained, at(f"read:ssq{i}"))
                step(dve.reciprocal(rb[:, :], rb[:, :]))
                tt(yT[:, :, :], xT[:, :, :], bc(rb[:, :], 1, KD), ALU.mult).then_inc(
                    x_scaled, up(x_scaled, f"npre{i}"))
                dve.wait_ge(x_scaled, now(x_scaled))
                if m is None:
                    tt(yT[:, :, :], yT[:, :, :], bc(nrm[:, 4, :], 2, T), ALU.mult).then_inc(
                        out_ready, up(out_ready, "out"))
                    dve.wait_ge(out_ready, now(out_ready))
                    return
                step(tt(seqs(hT[:, :, SEQ:T]), seqs(yT[:, :, SEQ:T]), bc(modA[:, m, :, 1:9], 3, LS), ALU.mult))
                tt(seqs(hT[:, :, SEQ:T]), seqs(hT[:, :, SEQ:T]), bc(modT[:, m, 0:KD, 1:9], 3, LS), ALU.add).then_inc(
                    sample_input_ready, up(sample_input_ready, f"hs{i}"))
                dve.wait_ge(sample_input_ready, now(sample_input_ready))

            def residual(k, m, prompt, sample, tmp, label=None, name=None):
                gate = modT[:, m, 16 + k, :]
                for src, c0, n in prompt:
                    step(stt(xT[:, k, c0:c0 + n], src, gate[:, 0:1], xT[:, k, c0:c0 + n], ALU.mult, ALU.add))
                ins = tt(tmp.rearrange("p (b s) -> p b s", s=LS), sample.rearrange("p (b s) -> p b s", s=LS),
                         bc(gate[:, 1:9], 2, LS), ALU.mult)
                if name:
                    ins.then_inc(dve_drained, up(dve_drained, "read:" + name))
                    dve.wait_ge(dve_drained, now(dve_drained))
                else:
                    step(ins)
                tt(xT[:, k, SEQ:T], xT[:, k, SEQ:T], tmp, ALU.add).then_inc(x_ready, up(x_ready, label))
                dve.wait_ge(x_ready, now(x_ready))

            dve.wait_ge(consts_in, book.get("consts", 16))
            dve.wait_ge(dt_ready, at("dt"))
            lr, li, dt = lam[:, 0, :], lam[:, 1, :], lam[:, 2, :]
            step(tt(s5t[:, 0, :], lr, dt, ALU.mult))
            step(tt(s5t[:, 1, :], li, dt, ALU.mult))
            step(ts(s5t[:, 2, :], s5t[:, 1, :], 1.0 / (2.0 * np.pi), MAGIC, ALU.mult, ALU.add))
            step(ts(s5t[:, 2, :], s5t[:, 2, :], MAGIC, None, ALU.subtract))
            step(stt(s5t[:, 1, :], s5t[:, 2, :], -TWO_PI_HI, s5t[:, 1, :], ALU.mult, ALU.add))
            step(stt(s5t[:, 1, :], s5t[:, 2, :], -TWO_PI_LO, s5t[:, 1, :], ALU.mult, ALU.add))
            step(ts(s5t[:, 1, :], s5t[:, 1, :], PI_LIM, -PI_LIM, ALU.min, ALU.max))
            step(ts(s5t[:, 2, :], s5t[:, 1, :], -1.0, None, ALU.mult))
            tt(s5t[:, 2, :], s5t[:, 2, :], s5t[:, 1, :], ALU.max).then_inc(s5_angle_ready, up(s5_angle_ready, "ang"))
            dve.wait_ge(s5_angle_ready, now(s5_angle_ready))
            dve.wait_ge(trig_ready, at("trig"))
            step(dve.memset(pw[:, 0, 0, :], 1.0))
            step(dve.memset(pw[:, 1, 0, :], 0.0))
            ar, ai = pw[:, 0, 1, :], pw[:, 1, 1, :]
            step(tt(ar, s5t[:, 0, :], s5t[:, 4, :], ALU.mult))
            step(tt(ai, s5t[:, 0, :], s5t[:, 3, :], ALU.mult))
            t0, t1, t2 = s5t[:, 5, :], s5t[:, 6, :], s5t[:, 7, :]
            for m in range(1, 8):
                step(tt(t0, pw[:, 0, m, :], ar, ALU.mult))
                step(tt(t1, pw[:, 1, m, :], ai, ALU.mult))
                step(tt(pw[:, 0, m + 1, :], t0, t1, ALU.subtract))
                step(tt(t0, pw[:, 0, m, :], ai, ALU.mult))
                step(tt(t1, pw[:, 1, m, :], ar, ALU.mult))
                step(tt(pw[:, 1, m + 1, :], t0, t1, ALU.add))
            step(tt(t0, lr, lr, ALU.mult))
            step(tt(t1, li, li, ALU.mult))
            step(tt(t2, t0, t1, ALU.add))
            step(dve.reciprocal(t2, t2))
            step(ts(s5t[:, 0, :], ar, 1.0, None, ALU.subtract))
            step(tt(t0, s5t[:, 0, :], lr, ALU.mult))
            step(tt(t1, ai, li, ALU.mult))
            step(tt(t0, t0, t1, ALU.add))
            step(tt(fz[:, 0, :], t0, t2, ALU.mult))
            step(tt(t0, ai, lr, ALU.mult))
            step(tt(t1, s5t[:, 0, :], li, ALU.mult))
            step(tt(t0, t0, t1, ALU.subtract))
            step(tt(fz[:, 1, :], t0, t2, ALU.mult))

            dve.wait_ge(x_in, 16)
            dve.wait_ge(act_drained, at("read:ssq0"))
            step(dve.reciprocal(rb[:, :], rb[:, :]))
            tt(yT[:, :, :], xT[:, :, :], bc(rb[:, :], 1, KD), ALU.mult).then_inc(x_scaled, up(x_scaled, "npre0"))
            dve.wait_ge(x_scaled, now(x_scaled))
            for m in range(4):
                dve.wait_ge(acc_full, filled(f"adaT{m}"))
                tt(modT[:, m], flatbuf(f"adaT{m}", 24, 9), bc(bmod[:, m, :], 2, 9), ALU.add).then_inc(
                    dve_drained, up(dve_drained, f"read:adaT{m}"))
                dve.wait_ge(dve_drained, now(dve_drained))
                step(ts(modA[:, m], modT[:, m, KD:2 * KD, :], 1.0, None, ALU.add))
                tt(modA[:, m], modA[:, m], bc(nrm[:, m, :], 2, 9), ALU.mult).then_inc(
                    mod_ready, up(mod_ready, f"mod{m}"))
                dve.wait_ge(mod_ready, now(mod_ready))
                if m == 0:
                    step(tt(seqs(hT[:, :, SEQ:T]), seqs(yT[:, :, SEQ:T]), bc(modA[:, 0, :, 1:9], 3, LS), ALU.mult))
                    tt(seqs(hT[:, :, SEQ:T]), seqs(hT[:, :, SEQ:T]), bc(modT[:, 0, 0:KD, 1:9], 3, LS),
                              ALU.add).then_inc(sample_input_ready, up(sample_input_ready, "hs0"))
                    dve.wait_ge(sample_input_ready, now(sample_input_ready))
            step(dve.memset(gt[:, :, :, :], 0.0))
            dve.wait_ge(acc_full, filled("ba"))
            for rows, t0_, nt in ((P, 0, 4), (TS, 4, 1)):
                src = buf("ba")[0:rows, 0, 16 * t0_:16 * (t0_ + nt)].rearrange("p (t c) -> p t c", c=16)
                step(dve.tensor_copy(gt[0:rows, BB, t0_:t0_ + nt, :], src[:, :, 0:8]))
                ins = tt(gt[0:rows, BA, t0_:t0_ + nt, :], src[:, :, 8:16], bc(hp[0:rows, 1, :], 1, nt), ALU.add)
                if t0_:
                    ins.then_inc(dve_drained, up(dve_drained, "read:ba"))
                    dve.wait_ge(dve_drained, now(dve_drained))
                else:
                    step(ins)
            step(ts(gt[:, G2], gt[:, BA], -1.0, None, ALU.mult))
            tt(gt[:, G2], gt[:, G2], gt[:, BA], ALU.max).then_inc(gate_args_ready, up(gate_args_ready, "ba"))
            dve.wait_ge(gate_args_ready, now(gate_args_ready))
            dve.wait_ge(softplus_ready, at("splus"))
            step(stt(gt[:, G1], gt[:, BA], 0.0, gt[:, G2], ALU.max, ALU.add))
            step(tt(gt[:, G1], gt[:, G1], bc(hp[:, 0, :], 1, 5), ALU.mult))
            ts(gt[:, GG], gt[:, G1], -1.0, None, ALU.mult).then_inc(g_ready, up(g_ready, "gg"))
            dve.wait_ge(g_ready, now(g_ready))
            dve.wait_ge(conv_in, 32)
            dve.wait_ge(prompt_input_ready, at("h0"))
            for i in range(2):
                step(dve.memset(raw[i][:, 0:3], 0.0))
            for m in range(QKV + 3):
                if m < QKV:
                    dve.wait_ge(act_drained, at(f"read:p{m}"))
                    dst = qkv[:, m, 0:SEQ]
                    sdst = qkv[:, m, SEQ:T].rearrange("p (b s) -> p b s", s=LS)
                    if m == 0:
                        dve.wait_ge(acc_full, filled("adaT3"))
                    step(ts(dst, raw[m % 2][:, 0:SEQ], cw[:, m, 0:1], None, ALU.mult))
                    for j in range(1, CW):
                        step(stt(dst, raw[m % 2][:, j:j + SEQ], cw[:, m, j:j + 1], dst, ALU.mult, ALU.add))
                    dve.wait_ge(history_ready, at(f"cs{m}"))
                    step(ts(sdst, sraw[m % 2][:, :, 0:LS], cw[:, m, 0:1], None, ALU.mult))
                    for j in range(1, CW):
                        ins = stt(sdst, sraw[m % 2][:, :, j:j + LS], cw[:, m, j:j + 1], sdst, ALU.mult, ALU.add)
                        if j < CW - 1:
                            step(ins)
                        else:
                            ins.then_inc(conv_done, up(conv_done, f"conv{m}"))
                            dve.wait_ge(conv_done, now(conv_done))
                if 3 <= m < 19:
                    dve.wait_ge(act_drained, at(f"read:l{m - 3}"))
                    step(dve.reciprocal(ln[(m - 3) % 2], ln[(m - 3) % 2]))
                    tt(qkv[:, m - 3, :], qkv[:, m - 3, :], ln[(m - 3) % 2], ALU.mult).then_inc(
                        l2_done, up(l2_done, f"l2{m - 3}"))
                    dve.wait_ge(l2_done, now(l2_done))
            dve.wait_ge(acc_full, filled("G"))
            for b, dst in ((0, GCOL), (1, GLAST)):
                step(dve.tensor_copy(gt[:, dst, 0:4, :],
                                     buf("G")[:, b, 0:32].rearrange("p (t h) -> p t h", t=4)))
                ins = dve.tensor_copy(gt[0:TS, dst, 4, :], buf("G")[0:TS, b, 32:40])
                if b:
                    ins.then_inc(dve_drained, up(dve_drained, "read:G"))
                    dve.wait_ge(dve_drained, now(dve_drained))
                else:
                    step(ins)
            tt(gt[:, G2], gt[:, GLAST], gt[:, GCOL], ALU.subtract).then_inc(
                log_decay_ready, up(log_decay_ready, "gcol"))
            dve.wait_ge(log_decay_ready, now(log_decay_ready))
            dve.wait_ge(decay_cols_ready, at("ecol"))
            step(stt(gt[:, CKBG], gt[:, G1], -1.0, gt[:, BETA], ALU.mult, ALU.mult))
            step(dve.memset(S[:, :, :], 0.0))
            dve.wait_ge(conv_stored, 32)
            for t, c0, n in tiles:
                dve.wait_ge(acc_full, filled(f"su{t - 1}" if t else "p31"))
                tt(um(M, n), bc(cst[0:n, tri(t), 0:n], 1, H), bc(gt[0:n, GG, t, :], 2, n), ALU.mult).then_inc(
                    row_masks_ready, up(row_masks_ready, f"ru{t}"))
                dve.wait_ge(row_masks_ready, now(row_masks_ready))
                tt(um(MT, n), bc(cst[0:n, IDENT, 0:n], 1, H), bc(gt[0:n, BETA, t, :], 2, n), ALU.mult).then_inc(
                    row_masks_ready, up(row_masks_ready, f"rub{t}"))
                dve.wait_ge(row_masks_ready, now(row_masks_ready))
                dve.wait_ge(decay_rows_ready, at(f"eG{t}"))
                tt(um(EX, n), flatbuf(f"gr{t}", H, n)[0:n], bc(gt[0:n, GCOL, t, :], 2, n), ALU.subtract).then_inc(
                    dve_drained, up(dve_drained, f"read:gr{t}"))
                dve.wait_ge(dve_drained, now(dve_drained))
                ts(um(EX, n), um(EX, n), 0.0, None, ALU.min).then_inc(
                    decay_diff_ready, up(decay_diff_ready, f"diff{t}"))
                dve.wait_ge(decay_diff_ready, now(decay_diff_ready))
                dve.wait_ge(decay_exp_ready, at(f"ex{t}"))
                step(tt(um(EX, n), um(EX, n), bc(cst[0:n, tri(t), 0:n], 1, H), ALU.mult))
                dve.wait_ge(acc_full, filled(f"kk{t}"))
                tt(um(AT, n), flatbuf(f"kk{t}", H, n)[0:n], um(EX, n), ALU.mult).then_inc(
                    dve_drained, up(dve_drained, f"read:kk{t}"))
                dve.wait_ge(dve_drained, now(dve_drained))
                ins = tt(um(AT, n), um(AT, n), flatbuf(f"br{t}", H, n)[0:n], ALU.mult)
                ins.then_inc(dve_drained, up(dve_drained, f"read:br{t}", f"AT{t}"))
                dve.wait_ge(dve_drained, now(dve_drained))
                dve.wait_ge(acc_full, filled(f"qk{t}"))
                tt(um(QKE, n), flatbuf(f"qk{t}", H, n)[0:n], um(EX, n), ALU.mult).then_inc(
                    dve_drained, up(dve_drained, f"read:qk{t}"))
                dve.wait_ge(dve_drained, now(dve_drained))
                tt(qkv[:, 0:H, c0:c0 + n], qkv[:, 0:H, c0:c0 + n], um(EG, n, P), ALU.mult).then_inc(
                    q_decayed, up(q_decayed, f"qdT{t}"))
                dve.wait_ge(q_decayed, now(q_decayed))
                dve.wait_ge(acc_full, filled(f"kt{t}"))
                step(tt(ur(KBGT, n), flatbuf(f"kt{t}", H, P)[0:n], bc(gt[0:n, CKBG, t, :], 2, P), ALU.mult))
                tt(ur(KDECT, n), flatbuf(f"kt{t}", H, P)[0:n], bc(gt[0:n, CKDEC, t, :], 2, P), ALU.mult).then_inc(
                    dve_drained, up(dve_drained, f"read:kt{t}"))
                dve.wait_ge(dve_drained, now(dve_drained))
                dve.wait_ge(acc_full, filled(f"vt{t}"))
                tt(ur(VB, n), flatbuf(f"vt{t}", H, P)[0:n], bc(gt[0:n, BETA, t, :], 2, P), ALU.mult).then_inc(
                    dve_drained, up(dve_drained, f"read:vt{t}"))
                dve.wait_ge(dve_drained, now(dve_drained))
                dve.wait_ge(a_block_ready, at(f"ab{t}_0"))
                dve.wait_ge(acc_full, filled(f"A0{t}"))
                eye = bc(cst[0:n, IDENT, 0:n], 1, H)
                step(tt(um(MT, n), eye, um(AB, n), ALU.subtract))
                tt(um(M, n), eye, flatbuf(f"A0{t}", H, n)[0:n], ALU.subtract).then_inc(
                    dve_drained, up(dve_drained, f"read:A0{t}", f"MT{t}_0"))
                dve.wait_ge(dve_drained, now(dve_drained))
                for l in range(1, levels(t)):
                    if l < levels(t) - 1:
                        dve.wait_ge(acc_full, filled(f"MX{t}_{l}"))
                        tt(um(M, n), um(M, n), flatbuf(f"MX{t}_{l}", H, n)[0:n], ALU.subtract).then_inc(
                            dve_drained, up(dve_drained, f"read:MX{t}_{l}"))
                        dve.wait_ge(dve_drained, now(dve_drained))
                    dve.wait_ge(acc_full, filled(f"MTX{t}_{l}"))
                    ins = tt(um(MT, n), um(MT, n), flatbuf(f"MTX{t}_{l}", H, n)[0:n], ALU.subtract)
                    ins.then_inc(dve_drained, up(dve_drained, f"read:MTX{t}_{l}", f"MT{t}_{l}"))
                    dve.wait_ge(dve_drained, now(dve_drained))
                if t < 4:
                    dve.wait_ge(acc_full, filled(f"su{t}"))
                    step(tt(S[:, :, :], S[:, :, :], bc(um(EG, n, P)[:, :, n - 1], 2, P), ALU.mult))
                    ins = tt(S[:, :, :], S[:, :, :], flatbuf(f"su{t}", H, P), ALU.add)
                    ins.then_inc(dve_drained, up(dve_drained, f"read:su{t}", f"S{t}"))
                    dve.wait_ge(dve_drained, now(dve_drained))
            for h in range(H):
                n = TS
                dve.wait_ge(acc_full, filled(f"suS{h}"))
                if h >= 2:
                    dve.wait_ge(snew_out[h % 2], 16 * (h // 2))
                step(tt(snew[h % 2], s0v[h], bc(um(EG, n, P)[:, h, LS - 1:TS:LS], 2, P), ALU.mult))
                ins = tt(snew[h % 2], snew[h % 2], flatbuf(f"suS{h}", NSEQ, P), ALU.add)
                ins.then_inc(dve_drained, up(dve_drained, f"read:suS{h}", f"snew{h}"))
                dve.wait_ge(dve_drained, now(dve_drained))

            for h in range(H):
                dve.wait_ge(act_drained, at(f"read:on{h}"))
                step(dve.reciprocal(hT[:, h, :], hT[:, h, :]))
                step(tt(yT[:, h, :], yT[:, h, :], hT[:, h, :], ALU.mult))
                stt(yT[:, h, :], yT[:, h, :], onrm[:, 0:1], zT[:, h, :], ALU.mult, ALU.mult).then_inc(
                    o_normed, up(o_normed, "onorm" if h == H - 1 else None))
                dve.wait_ge(o_normed, now(o_normed))
            for m in range(KD):
                dve.wait_ge(acc_full, filled(f"w{m}"))
                ps = buf(f"w{m}")
                residual(m, 0, [(ps[:, 0, 0:HT], 0, HT), (ps[:, 1, 0:SEQ - HT], HT, SEQ - HT)],
                         ps[:, 1, SEQ - HT:HT], rb[:, 0:TS], "x1" if m == KD - 1 else None, f"w{m}")

            def choose(values, width, out):
                step(dve.tensor_reduce(rtv["tm"], values, AX.X, ALU.max))
                step(tt(out, values, bc(rtv["tm"], 2, 4), ALU.is_ge))
                step(tt(out, out, bc(cst[:, MISC, 4:8], 1, 5), ALU.mult))
                step(dve.tensor_reduce(width, out, AX.X, ALU.max))
                step(tt(out, out, bc(width, 2, 4), ALU.is_equal))

            def moe(layer, i, m):
                r = rtv
                step(dve.memset(rt[:, 0:420], 0.0))
                dve.wait_ge(acc_full, filled(f"rt{layer}"))
                for rows, t0, nt in ((P, 0, 4), (TS, 4, 1)):
                    src = buf(f"rt{layer}")[0:rows, 0, 20 * t0:20 * (t0 + nt)].rearrange("p (t c) -> p t c", c=20)
                    ins = tt(r["L"][0:rows, t0:t0 + nt, :], src, bc(br[0:rows, layer, :], 1, nt), ALU.add)
                    if t0:
                        ins.then_inc(dve_drained, up(dve_drained, f"read:rt{layer}"))
                        dve.wait_ge(dve_drained, now(dve_drained))
                    else:
                        step(ins)
                lg, le = r["L"][:, :, 0:4], r["L"][:, :, 4:20].rearrange("p t (g e) -> p t g e", g=4)
                choose(lg, r["gm"], r["ohg"])
                tt(r["ge"], lg, bc(r["tm"], 2, 4), ALU.subtract).then_inc(
                    group_diff_ready, up(group_diff_ready, f"rga{layer}"))
                dve.wait_ge(group_diff_ready, now(group_diff_ready))
                dve.wait_ge(group_exp_ready, at(f"rgb{layer}"))
                step(dve.tensor_reduce(r["pg"], r["ge"], AX.X, ALU.add))
                step(dve.reciprocal(r["pg"], r["pg"]))
                step(tt(r["t16"], le, bc(r["ohg"], 3, 4), ALU.mult))
                step(dve.tensor_reduce(r["sel"], r["t16"].rearrange("p t g e -> p t e g"), AX.X, ALU.add))
                choose(r["sel"], r["gm"], r["oh1"])
                step(dve.tensor_copy(r["m1"], r["tm"]))
                step(stt(r["t4"], r["oh1"], -BIG, r["sel"], ALU.mult, ALU.add))
                choose(r["t4"], r["gm"], r["oh2"])
                tt(r["e2"], r["tm"], r["m1"], ALU.subtract).then_inc(
                    expert_diff_ready, up(expert_diff_ready, f"rea{layer}"))
                dve.wait_ge(expert_diff_ready, now(expert_diff_ready))
                dve.wait_ge(expert_exp_ready, at(f"reb{layer}"))
                step(ts(r["w1"], r["e2"], 1.0, None, ALU.add))
                step(dve.reciprocal(r["w1"], r["w1"]))
                step(tt(r["w1"], r["w1"], r["pg"], ALU.mult))
                step(tt(r["w2"], r["w1"], r["e2"], ALU.mult))
                step(tt(r["oh1"], r["oh1"], bc(r["w1"], 2, 4), ALU.mult))
                step(tt(r["oh2"], r["oh2"], bc(r["w2"], 2, 4), ALU.mult))
                step(tt(r["t4"], r["oh1"], r["oh2"], ALU.add))
                step(tt(r["comb"], bc(r["ohg"], 3, 4), bc(r["t4"], 2, 4), ALU.mult))
                comb = r["comb"].rearrange("p t g e -> p t (g e)")
                if layer == 0:
                    for s in snew_out:
                        dve.wait_ge(s, 16 * (H // 2))
                for n_ in range(12):
                    if n_ < 10:
                        t, g = divmod(n_, 2)
                        _, c0, n = tiles[t]
                        if t:
                            dve.wait_ge(acc_full, filled(f"cb{layer}_{t - 1}_{g}"))
                        tt(RC[g][0:n, 0:8 * n].rearrange("p (e n) -> p e n", n=n),
                                  bc(cst[0:n, IDENT, 0:n], 1, 8), bc(comb[0:n, t, 8 * g:8 * g + 8], 2, n), ALU.mult).then_inc(
                                      route_diag_ready, up(route_diag_ready, f"rc{layer}_{t}_{g}"))
                        dve.wait_ge(route_diag_ready, now(route_diag_ready))
                    if n_ >= 2:
                        t, g = divmod(n_ - 2, 2)
                        _, c0, n = tiles[t]
                        dve.wait_ge(acc_full, filled(f"cb{layer}_{t}_{g}"))
                        dve.tensor_copy(CB[:, 8 * g:8 * g + 8, c0:c0 + n], flatbuf(f"cb{layer}_{t}_{g}", 8, n)).then_inc(
                            dve_drained, up(dve_drained, f"read:cb{layer}_{t}_{g}"))
                        dve.wait_ge(dve_drained, now(dve_drained))
                dve.wait_ge(prompt_input_ready, at(f"h{i}"))
                for b in range(2):
                    dve.memset(yT[:, 4 * b:4 * b + 4, :], 0.0).then_inc(hid_ready, up(hid_ready))
                dve.wait_ge(hid_ready, now(hid_ready))
                n0 = book.get(("moe_first_use", layer), 0)
                a0 = book.get(("moe_a", layer), 0)
                book["moe_v", layer] = now(dve_drained)
                with dve.Fori(0, E // 2) as it:
                    counts.enter(dve_drained, it, 20)
                    counts.enter(hid_ready, it, 4)
                    for e in range(2):
                        for f in range(2):
                            k = 12 * e + 2 * f + 1
                            dve.wait_ge(acc_full, it * 24 + (n0 + k + 1))
                            tt(halves(hid[:, e, f, :]), acc[:, (n0 + k) % NACC, :, 0:HT],
                               halves(CB[:, it * 2 + e, :]), ALU.mult).then_inc(dve_drained, up(dve_drained))
                            dve.wait_ge(dve_drained, now(dve_drained))
                            dve.wait_ge(act_drained, it * 4 + (a0 + 2 * e + f + 1))
                            tt(hid[:, e, f, :], hid[:, e, f, :], s1[:, f, :], ALU.mult).then_inc(
                                hid_ready, up(hid_ready))
                            dve.wait_ge(hid_ready, now(hid_ready))
                        for k_ in range(KD):
                            k = 12 * e + 4 + k_
                            dve.wait_ge(acc_full, it * 24 + (n0 + k + 1))
                            tt(halves(yT[:, k_, :]), halves(yT[:, k_, :]), acc[:, (n0 + k) % NACC, :, 0:HT],
                               ALU.add).then_inc(dve_drained, up(dve_drained))
                            dve.wait_ge(dve_drained, now(dve_drained))
                counts.leave(dve_drained, E // 2)
                counts.leave(hid_ready, E // 2)
                for j in range(8):
                    book["at", f"read:y{layer}_{j}"] = now(dve_drained) - 7 + j
                for k in range(KD):
                    residual(k, m, [(yT[:, k, 0:SEQ], 0, SEQ)], yT[:, k, SEQ:T], rb[:, 0:TS],
                             f"x{i + 1}" if k == KD - 1 else None)

            norm(1, 1)
            moe(0, 1, 1)
            norm(2, 2)

            dve.wait_ge(bc_in, 32)
            e0, e1 = (extra[:, i, :].rearrange("p (q c) -> p q c", q=NPAIR) for i in range(2))
            fr, fi = bc(fz[:, 0, :], 2, 32), bc(fz[:, 1, :], 2, 32)
            step(tt(e0, BC[:, 0], fr, ALU.mult))
            step(tt(e1, BC[:, 1], fi, ALU.mult))
            step(tt(e0, e0, e1, ALU.subtract))
            step(tt(e1, BC[:, 1], fr, ALU.mult))
            step(tt(BC[:, 1], BC[:, 0], fi, ALU.mult))
            step(tt(BC[:, 1], BC[:, 1], e1, ALU.add))
            dve.tensor_copy(BC[:, 0], e0).then_inc(s5_b_ready, up(s5_b_ready, "bb"))
            dve.wait_ge(s5_b_ready, now(s5_b_ready))
            for c in range(KD + 1):
                if c < KD:
                    if c:
                        dve.wait_ge(acc_full, filled(f"zr{c - 1}"))
                    zv, ev = zview(Z[0]), zview(extra[:, 0, :])
                    step(tt(zv, powers(0, 0, 8, c), over_m(BC[:, 0, 4 * c:4 * c + 4, :], 8), ALU.mult))
                    step(tt(ev, powers(1, 0, 8, c), over_m(BC[:, 1, 4 * c:4 * c + 4, :], 8), ALU.mult))
                    tt(zv, zv, ev, ALU.subtract).then_inc(zr_ready, up(zr_ready, f"zr{c}"))
                    dve.wait_ge(zr_ready, now(zr_ready))
                if c:
                    dve.wait_ge(acc_full, filled(f"inc{c - 1}"))
                    dve.tensor_copy(INC[:, :, 4 * c - 4:4 * c, :],
                                          buf(f"inc{c - 1}")[:, :, 0:4 * NCK].rearrange("p r (j c) -> p r j c", j=4)).then_inc(
                                              dve_drained, up(dve_drained, f"read:inc{c - 1}"))
                    dve.wait_ge(dve_drained, now(dve_drained))
            a8r, a8i = pw[:, 0, 8, :], pw[:, 1, 8, :]
            dve.wait_ge(zi_ready, at("zi7"))
            step(ts(BC[:, 1], BC[:, 1], -1.0, None, ALU.mult))
            step(ts(aim[:, 0, :], a8i, -1.0, None, ALU.mult))
            step(dve.tensor_copy(aim[:, 1, :], a8i))
            step(dve.memset(SIN[:, :, :, 0], 0.0))
            with dve.Fori(0, NCP // 8) as it:
                counts.enter(dve_order, it, 40)
                for k in range(8):
                    cur = SIN[:, :, :, it * 8 + k]
                    step(tt(st1, cur, bc(a8r, 1, 2), ALU.mult))
                    step(tt(st2[:, 0, :], SIN[:, 1, :, it * 8 + k], aim[:, 0, :], ALU.mult))
                    step(tt(st2[:, 1, :], SIN[:, 0, :, it * 8 + k], aim[:, 1, :], ALU.mult))
                    step(tt(st1, st1, INC[:, :, :, it * 8 + k], ALU.add))
                    step(tt(SIN[:, :, :, it * 8 + (k + 1)], st1, st2, ALU.add))
            counts.leave(dve_order, NCP // 8)
            step(dve.tensor_copy(fin_p, SIN[:, :, :, NCP]))
            step(dve.tensor_copy(SIN[:, :, :, NCP:NCK], s0ri))
            e0, e1 = (extra[:, i, 0:512].rearrange("p (r q b) -> p r q b", r=2, q=NPAIR) for i in range(2))
            step(tt(e0, s0ri, bc(bc(a8r, 1, 2), 3, NSEQ), ALU.mult))
            for r in range(2):
                step(tt(e1[:, r], s0ri[:, 1 - r], bc(aim[:, r], 2, NSEQ), ALU.mult))
            step(tt(e0, e0, e1, ALU.add))
            tt(fin_s, e0, INC[:, :, :, NCP:NCK], ALU.add).then_inc(s5_fin_ready, up(s5_fin_ready, "s5fin"))
            dve.wait_ge(s5_fin_ready, now(s5_fin_ready))
            ts(SIN[:, 1], SIN[:, 1], -1.0, None, ALU.mult).then_inc(entry_states_ready, up(entry_states_ready, "sin"))
            dve.wait_ge(entry_states_ready, now(entry_states_ready))
            for c in range(KD):
                if c:
                    dve.wait_ge(acc_full, filled(f"yc{c - 1}"))
                step(tt(CA[0], powers(0, 0, 9, c), over_m(BC[:, 2, 4 * c:4 * c + 4, :], 9), ALU.mult))
                step(tt(catmp[0], powers(1, 0, 9, c), over_m(BC[:, 3, 4 * c:4 * c + 4, :], 9), ALU.mult))
                tt(CA[0], CA[0], catmp[0], ALU.subtract).then_inc(ca_re_ready, up(ca_re_ready, f"car{c}"))
                dve.wait_ge(ca_re_ready, now(ca_re_ready))
                dve.wait_ge(acc_full, filled(f"K{c}"))
                if c:
                    dve.wait_ge(acc_full, filled(f"ys{c - 1}"))
                quad = bc(bc(cst[:, MISC, 0:4], 1, 8), 3, 32)
                tt(KB.rearrange("p m (j c) -> p m j c", j=4), bc(flatbuf(f"K{c}", 8, 32), 2, 4), quad,
                         ALU.mult).then_inc(dve_drained, up(dve_drained, f"read:K{c}", f"kb{c}"))
                dve.wait_ge(dve_drained, now(dve_drained))
                dve.wait_ge(acc_full, filled(f"ys{c}"))
                for b in range(2):
                    tc = lambda ap: ap.rearrange("p (c t) -> p t c", t=8)[:, 4 * b:4 * b + 4]
                    ins = stt(tc(yT[:, c, :]), tc(zT[:, c, :]), s5d[:, c:c + 1],
                              buf(f"ys{c}")[:, b, 0:4 * NCK].rearrange("p (t c) -> p t c", t=4), ALU.mult, ALU.add)
                    if b:
                        ins.then_inc(dve_drained, up(dve_drained, f"read:ys{c}", "ysum" if c == KD - 1 else None))
                        dve.wait_ge(dve_drained, now(dve_drained))
                    else:
                        step(ins)
            for m in range(KD):
                dve.wait_ge(acc_full, filled(f"ga{m}"))
                dve.wait_ge(act_drained, at(f"read:gg{m}"))
                t_ = hflat[:, T * (m % 2):T * (m % 2) + T]
                tt(halves(t_), tok(f"ga{m}"), halves(extra[:, m % 2, 0:T]), ALU.mult).then_inc(
                    dve_drained, up(dve_drained, f"read:ga{m}", f"glu{m}"))
                dve.wait_ge(dve_drained, now(dve_drained))
                residual(m, 2, [(t_[:, 0:SEQ], 0, SEQ)], t_[:, SEQ:T], rb[:, 0:TS], "x3" if m == KD - 1 else None)
            norm(3, 3)
            moe(1, 3, 3)
            norm(4, None)

        @block.gpsimd
        def _(pool):
            def step(ins):
                ins.then_inc(pool_order, up(pool_order))
                pool.wait_ge(pool_order, now(pool_order))

            tt = pool.tensor_tensor
            step(pool.memset(small[:, 0:1], EPS))
            step(pool.memset(small[:, 1:2], P * EPS))
            step(pool.memset(small[:, 2:3], float(np.pi / 2)))
            pool.memset(ones[:, :], 1.0).then_inc(ones_ready, up(ones_ready, "ones"))
            pool.wait_ge(ones_ready, now(ones_ready))
            pool.wait_ge(conv_in, 32)
            for m in range(QKV):
                pool.wait_ge(act_drained, at(f"read:p{m}"))
                if m >= 2:
                    pool.wait_ge(conv_done, at(f"conv{m - 2}"))
                r = raw[m % 2][:, 3:3 + T]
                rs = r[:, SEQ:T].rearrange("p (b s) -> p b s", s=LS)
                step(pool.tensor_copy(sraw[m % 2][:, :, 0:3], cs_in[:, m]))
                step(pool.tensor_copy(cs_out[:, m], rs[:, :, LS - 3:LS]))
                step(pool.tensor_copy(cp_out[:, m, :], r[:, SEQ - 3:SEQ]))
                pool.tensor_copy(sraw[m % 2][:, :, 3:11], rs).then_inc(history_ready, up(history_ready, f"cs{m}"))
                pool.wait_ge(history_ready, now(history_ready))
            for t, c0, n in tiles:
                for l in range(levels(t)):
                    if l == 0:
                        pool.wait_ge(dve_drained, at(f"AT{t}"))
                        if t:
                            pool.wait_ge(acc_full, filled(f"su{t - 1}"))
                    elif l == 1:
                        pool.wait_ge(dve_drained, at(f"MT{t}_0"))
                    else:
                        pool.wait_ge(acc_full, filled(f"X{t}_{l - 1}"))
                    tt(um(AB, n), um(AT, n), bc(cst[0:n, LEV + l, 0:n], 1, H), ALU.mult).then_inc(
                        a_block_ready, up(a_block_ready, f"ab{t}_{l}"))
                    pool.wait_ge(a_block_ready, now(a_block_ready))
            pool.wait_ge(act_drained, at("read:vtr"))
            for h in range(H):
                if h >= 2:
                    pool.wait_ge(acc_full, filled(f"suS{h - 2}"))
                tt(vmask[h % 2], bc(ur(AB, TS)[:, h, :], 1, NSEQ), bc(cst[0:TS, ONES8, 0:TS:LS], 2, P),
                          ALU.mult).then_inc(v_masked, up(v_masked, f"vm{h}"))
                pool.wait_ge(v_masked, now(v_masked))
            pool.wait_ge(s5_b_ready, at("bb"))
            for c in range(KD):
                if c:
                    pool.wait_ge(acc_full, filled(f"zi{c - 1}"))
                zv, ev = zview(Z[1]), zview(extra[:, 1, :])
                step(tt(zv, powers(0, 0, 8, c), over_m(BC[:, 1, 4 * c:4 * c + 4, :], 8), ALU.mult))
                step(tt(ev, powers(1, 0, 8, c), over_m(BC[:, 0, 4 * c:4 * c + 4, :], 8), ALU.mult))
                tt(zv, zv, ev, ALU.add).then_inc(zi_ready, up(zi_ready, f"zi{c}"))
                pool.wait_ge(zi_ready, now(zi_ready))
                if c >= 2:
                    pool.wait_ge(acc_full, filled(f"inc{c - 2}"))
                pool.wait_ge(act_drained, at(f"read:u{c}"))
                for j in range(4):
                    ins = pool.tensor_scalar(uM[c % 2][:, j, :], zT[:, c, :], cst[:, MISC, j:j + 1], None, ALU.mult)
                    ins.then_inc(u_masked, up(u_masked, f"um{c}"))
                    pool.wait_ge(u_masked, now(u_masked))
            pool.wait_ge(entry_states_ready, at("sin"))
            for c in range(KD):
                if c:
                    pool.wait_ge(acc_full, filled(f"yc{c - 1}"))
                step(tt(CA[1], powers(0, 0, 9, c), over_m(BC[:, 3, 4 * c:4 * c + 4, :], 9), ALU.mult))
                step(tt(catmp[1], powers(1, 0, 9, c), over_m(BC[:, 2, 4 * c:4 * c + 4, :], 9), ALU.mult))
                tt(CA[1], CA[1], catmp[1], ALU.add).then_inc(ca_im_ready, up(ca_im_ready, f"cai{c}"))
                pool.wait_ge(ca_im_ready, now(ca_im_ready))


def _layouts(x):
    f = lambda n: np.asarray(x[n])
    a = {}
    tokens = np.concatenate([f("x_prompt").reshape(SEQ, D), f("x_sample").reshape(TS, D)], 0)
    a["xT"] = tokens.T.reshape(KD, P, T).transpose(1, 0, 2)
    cc = np.concatenate([f("c_prompt"), f("c_sample")], 0)
    a["cT"] = cc.T.reshape(KD, P, 9).transpose(1, 0, 2)
    a["masks"] = constant_masks()
    col = lambda v: v.reshape(-1, P).T
    a["bmod"] = np.stack([col(f("b_mod_mix")[0]), col(f("b_mod_ffn")[0]), col(f("b_mod_mix")[1]),
                          col(f("b_mod_ffn")[1])], 1)
    a["nrm"] = np.stack([col(f("norm_mix")[0]), col(f("norm_ffn")[0]), col(f("norm_mix")[1]),
                         col(f("norm_ffn")[1]), col(f("norm_final"))], 1)
    for n in ("w_mod_mix", "w_mod_ffn"):
        a[n] = f(n).reshape(2, 2, 4, P, 6, 512).transpose(0, 4, 1, 3, 2, 5).reshape(2, 12, P, UNIT)

    def pairs(w):
        k, m = w.shape
        return w.reshape(k // P, P, m // 256, 2, P).transpose(2, 1, 3, 0, 4).reshape(m // 256, P, UNIT)

    w_in = f("gdn_w_in")[0]
    a["w_in"] = pairs(w_in[:, 0:4 * D])
    a["w_ba"] = w_in[:, 4 * D:].reshape(KD, P, 16).transpose(1, 0, 2)
    a["w_out"] = pairs(f("gdn_w_out")[0])
    a["s5in"] = pairs(f("s5_w_in")[0])
    a["glu"] = f("s5_w_glu")[0].reshape(KD, P, 2, KD, P).transpose(3, 1, 2, 0, 4).reshape(KD, P, UNIT)
    for n, s in (("w1", "moe_w1"), ("w3", "moe_w3")):
        a[n] = f(s).reshape(2, E, KD, P, 2, P).transpose(0, 1, 3, 4, 2, 5).reshape(2, E, P, UNIT)
    a["w2"] = f("moe_w2").reshape(2, E, 2, P, KD, P).transpose(0, 1, 3, 4, 2, 5).reshape(2, E, P, UNIT)
    a["wr"] = np.concatenate([f("moe_w_rg"), f("moe_w_re")], 2).reshape(2, KD, P, 20).transpose(2, 0, 1, 3)
    a["br"] = np.concatenate([f("moe_b_rg"), f("moe_b_re")], 1)
    a["conv"] = f("state_conv")[0].reshape(NSEQ, 3, QKV, P).transpose(3, 2, 0, 1)
    a["cw"] = f("gdn_conv_w")[0].reshape(CW, QKV, P).transpose(2, 1, 0)
    a["a_log"], a["dt_bias"] = f("gdn_a_log")[0], f("gdn_dt_bias")[0]
    a["onrm"] = f("gdn_o_norm")[0].reshape(P, 1)
    a["s0"] = f("state_delta")[0].transpose(1, 2, 0, 3)
    states = lambda v: v.reshape(NPAIR, 2, 64).transpose(1, 2, 0).reshape(P, NPAIR)
    a["lam"] = np.stack([states(f("s5_lam_re")[0]), states(f("s5_lam_im")[0])], 1)
    a["log_dt"] = f("s5_log_dt")[0].reshape(NPAIR, 2).T
    a["s5d"] = f("s5_d")[0].reshape(KD, P).T
    bcs = np.zeros((2, 64, 4, NPAIR, 2, 16), np.float32)
    for k, n in enumerate(("s5_b_re", "s5_b_im", "s5_c_re", "s5_c_im")):
        v = f(n)[0].reshape(NPAIR, 2, *f(n).shape[2:])
        v = v.transpose(1, 2, 0, 3) if k < 2 else v.transpose(1, 3, 0, 2)
        for g in range(2):
            bcs[g, :, k, :, g, :] = v[g]
    a["bc"] = bcs.reshape(P, 4, NPAIR, 32)
    s0 = np.stack([f("state_ssm_re")[0], f("state_ssm_im")[0]], 0).reshape(2, NSEQ, NPAIR, 2, 64)
    a["s0ri"] = s0.transpose(3, 4, 0, 2, 1).reshape(P, 2, NPAIR, NSEQ)
    return {n: np.ascontiguousarray(v) for n, v in a.items()}


_OUTS = {"y": (P, KD, T), "p_delta": (P, H, P), "p_conv": (P, QKV, 3), "s_conv": (P, QKV, NSEQ, 3),
         "s_delta": (H, P, NSEQ, P), "p_ssm": (P, 2, NPAIR), "s_ssm": (P, 2, NPAIR, NSEQ)}


def _build(arrays, bacc, book):
    nc = bacc.Bacc("TRN2", target_bir_lowering=False, num_devices=1)
    d = {n: nc.dram_tensor(f"in_{n}", v.shape, F32, kind="ExternalInput").ap() for n, v in arrays.items()}
    o = {n: nc.dram_tensor(f"out_{n}", s, F32, kind="ExternalOutput").ap() for n, s in _OUTS.items()}
    trunk(nc, d, o, book)
    return nc


def kernel(**inputs):
    import concourse.bacc as bacc
    from concourse.bass_utils import run_bass_kernel_spmd as run

    arrays = _layouts(inputs)
    book = {}
    _build(arrays, bacc, book)
    nc = _build(arrays, bacc, book)
    r = run(nc, [{f"in_{n}": v for n, v in arrays.items()}], core_ids=[0]).results[0]
    g = {n: r[f"out_{n}"] for n in _OUTS}
    y = g["y"].transpose(2, 1, 0).reshape(T, D)
    states = lambda v: v.reshape(2, 64, NPAIR).transpose(2, 0, 1).reshape(1, 1, 64, 64)
    sstates = lambda v: v.reshape(2, 64, NPAIR, NSEQ).transpose(3, 2, 0, 1).reshape(1, NSEQ, 64, 64)
    c = np.ascontiguousarray
    return (c(y[0:SEQ].reshape(1, SEQ, D)), c(y[SEQ:].reshape(NSEQ, LS, D)),
            c(g["p_delta"].transpose(1, 0, 2).reshape(1, 1, H, P, P)),
            c(g["p_conv"].transpose(2, 1, 0).reshape(1, 1, 3, QKV * P)),
            c(states(g["p_ssm"][:, 0])), c(states(g["p_ssm"][:, 1])),
            c(g["s_delta"].transpose(2, 0, 1, 3).reshape(1, NSEQ, H, P, P)),
            c(g["s_conv"].transpose(2, 3, 1, 0).reshape(1, NSEQ, 3, QKV * P)),
            c(sstates(g["s_ssm"][:, 0])), c(sstates(g["s_ssm"][:, 1])))
```

```python
from contextlib import ExitStack

import numpy as np
import concourse.bass as bass
from concourse import mybir

F32 = mybir.dt.float32
I32 = mybir.dt.int32
ALU = mybir.AluOpType
ACT = mybir.ActivationFunctionType
AX = mybir.AxisListType

P = 128
D = 1024
KD = D // P
SEQ, NSEQ, LS = 512, 8, 8
TS = NSEQ * LS
T = SEQ + TS
HT = T // 2
H = 8
NCK = T // 8
NCP = SEQ // 8
NPAIR = 32
E, NG, EG = 16, 4, 4
TOP = 2
NOVER = (TOP * T) // P - 1
CHUNKS = E + NOVER
EPS = 1e-6
NSLOT = 6
UNIT = 2048
NACC = 4
XT_ACC, H_ACC, Y_ACC = 0, 1, 2
CW = 4
QKV = 24
NLEV = 7
IDENT, TRIU, TRIU8, ONES8, MISC, LEV = 0, 1, 2, 3, 4, 5
N_CONST = LEV + NLEV
MAGIC = 12582912.0
TWO_PI_HI = 6.28125
TWO_PI_LO = 0.0019353071795864769
BIG = 1e30
PI_LIM = 3.1415925
READ_BY_SCALAR = {"ssq", "ada", "l", "p", "X", "wT", "vn", "o", "vnT", "vtr", "oS", "on", "u", "zr", "zi", "yc", "gg",
                  "tm"}


def constant_masks():
    j, i = np.meshgrid(np.arange(P), np.arange(P), indexing="ij")
    same = (i // LS) == (j // LS)
    misc = np.where(i < 4, j // 32 == i, np.where(i < 8, 8 - i, 0))
    misc = np.where((i >= 8) & (i < 24), P * (i - 8) - 1, misc)
    misc = np.where((i >= 24) & (i < 40), P * (E - 1) - P * (i - 24), misc)
    misc = np.where((i >= 40) & (i < 48), i - 40, misc)
    m = [i == j, i >= j, (i >= j) & same, same, misc]
    for l in range(NLEV):
        b = 1 << l
        m.append((i // (2 * b) == j // (2 * b)) & ((i // b) % 2 == 1) & ((j // b) % 2 == 0))
    return np.ascontiguousarray(np.stack(m, 1).astype(np.float32))


class Counts:

    def __init__(self, book):
        self.book, self.n, self.loop = book, {}, {}

    def up(self, sem, *labels, by=1):
        self.n[id(sem)] = self.n.get(id(sem), 0) + by
        for label in labels:
            if label is not None:
                self.book["at", label] = self.n[id(sem)]
        return by

    def now(self, sem):
        n = self.n.get(id(sem), 0)
        if id(sem) in self.loop:
            i, per, _ = self.loop[id(sem)]
            return i * per + n
        return n

    def enter(self, sem, i, per):
        self.loop[id(sem)] = i, per, self.n.get(id(sem), 0)

    def leave(self, sem, times):
        _, per, base = self.loop.pop(id(sem))
        assert self.n[id(sem)] - base == per
        self.n[id(sem)] = base + times * per


def levels(t):
    return NLEV if t < 4 else 3


def ring_units():
    out = [("mod", m, u) for m in range(4) for u in range(12)]
    out += [("w_in", 0, u) for u in range(16)] + [("w_out", 0, u) for u in range(4)]
    out += [("moe", 0, u) for u in range(3 * E)]
    out += [("s5in", 0, u) for u in range(4)] + [("glu", 0, u) for u in range(8)]
    out += [("moe", 1, u) for u in range(3 * E)]
    return out



def trunk(nc, d, o, book):
    units = ring_units()
    unit_no = {u: n for n, u in enumerate(units)}
    with ExitStack() as ctx:
        def sb(name, shape):
            return ctx.enter_context(nc.sbuf_tensor(name, shape, F32))

        def sem(name):
            return ctx.enter_context(nc.semaphore(name))

        counts = Counts(book)
        up, now = counts.up, counts.now

        xT = sb("xT", [P, KD, T])
        hT = sb("hT", [P, KD, T])
        yT = sb("yT", [P, KD, T])
        zT = sb("zT", [P, KD, T])
        big = sb("big", [P, QKV * T])
        ring = sb("ring", [P, NSLOT, UNIT])
        modT = sb("modT", [P, 4, 24, 9])
        modA = sb("modA", [P, 4, KD, 9])
        rb = sb("rb", [P, T])
        extra = sb("extra", [P, 2, 1024])
        cst = sb("cst", [P, N_CONST, P])
        small = sb("small", [P, 4])
        ones = sb("ones", [P, P])
        cT = sb("cT", [P, KD, 9])
        bmod = sb("bmod", [P, 4, 24])
        nrm = sb("nrm", [P, 5, KD])
        w_ba = sb("w_ba", [P, KD, 16])
        hp = sb("hp", [P, 2, H])
        onrm = sb("onrm", [P, 1])
        lam = sb("lam", [P, 3, NPAIR])
        pw = sb("pw", [P, 2, 9, NPAIR])
        fz = sb("fz", [P, 2, NPAIR])
        s5t = sb("s5t", [P, 8, NPAIR])
        s5d = sb("s5d", [P, KD])
        wr = sb("wr", [P, 2, KD, 20])
        br = sb("br", [P, 2, 20])
        gt = sb("gt", [P, 10, 5, H])
        row_of = ctx.enter_context(nc.sbuf_tensor("row_of", [P, TOP, 5], I32))
        over = ctx.enter_context(nc.sbuf_tensor("over", [P, 9], I32))
        S = sb("S", [P, H, P])
        acc = ctx.enter_context(nc.psum_tensor("acc", [P, NACC, 2, 512], F32))

        hflat = hT[:, :, :].rearrange("p k t -> p (k t)")
        yflat = yT[:, :, :].rearrange("p k t -> p (k t)")
        m_sb = big[0:9, 0:2 * 3072].rearrange("p (b n) -> p b n", b=2)
        qkv = big[:, :].rearrange("p (m t) -> p m t", t=T)
        unit = [hflat[:, 1024 * i:1024 * (i + 1)] for i in range(4)]
        unit += [ring[:, s, 1024 * j:1024 * (j + 1)] for s in (2, 3) for j in range(2)]
        unit += [extra[:, j, :] for j in range(2)]
        EG, EX, AT, AB, M, MT, KBGT, KDECT, VB, QKE = range(10)
        raw = [yflat[:, 640 * i:640 * i + T + 3] for i in range(2)]
        sraw = [yflat[:, 1280 + 88 * i:1280 + 88 * (i + 1)].rearrange("p (b s) -> p b s", s=11) for i in range(2)]
        sq = [yflat[:, 1536 + T * i:1536 + T * (i + 1)] for i in range(2)]
        ln = [yflat[:, 2688 + T * i:2688 + T * (i + 1)] for i in range(2)]
        cs_in = extra[:, 0, 0:QKV * 24].rearrange("p (m b s) -> p m b s", b=NSEQ, s=3)
        cs_out = extra[:, 1, 0:QKV * 24].rearrange("p (m b s) -> p m b s", b=NSEQ, s=3)
        cp_out = extra[:, 1, 600:600 + QKV * 3].rearrange("p (m s) -> p m s", s=3)
        cw = extra[:, 1, 700:700 + QKV * CW].rearrange("p (m s) -> p m s", s=CW)
        BA, BB, BETA, GG, G1, G2, GCOL, GLAST, CKBG, CKDEC = range(10)
        s0v = [qkv[:, 8 * (h // 4):8 * (h // 4) + 8, P * (h % 4):P * (h % 4) + P] for h in range(H)]
        snew = [qkv[:, 16:24, P * i:P * i + P] for i in range(2)]
        vmask = [qkv[0:TS, 16:24, 256 + P * i:256 + P * i + P] for i in range(2)]
        half = 2 * NPAIR * NCK
        INC = big[:, 0:half].rearrange("p (r q c) -> p r q c", r=2, q=NPAIR)
        SIN = big[:, half:2 * half].rearrange("p (r q c) -> p r q c", r=2, q=NPAIR)
        Z = [big[:, half + 1024 * i:half + 1024 * (i + 1)] for i in range(2)]
        ZT = big[:, half + 2048:half + 4096].rearrange("p (r m n) -> p r m n", r=2, m=8)
        uM = [big[:, 2 * half + 4 * T * i:2 * half + 4 * T * (i + 1)].rearrange("p (j t) -> p j t", j=4)
              for i in range(2)]
        CA = [big[:, 2 * half + 1152 * i:2 * half + 1152 * (i + 1)].rearrange("p (m q c) -> p m q c", m=9, q=4)
              for i in range(2)]
        KB = big[:, 2 * half + 2304:2 * half + 3328].rearrange("p (m n) -> p m n", m=8)
        YS = big[0:NCK, 2 * half + 3328:2 * half + 4352].rearrange("p (t n) -> p t n", t=8)
        catmp = [big[:, 1152 * i:1152 * (i + 1)].rearrange("p (m q c) -> p m q c", m=9, q=4) for i in range(2)]
        BC = hflat[:, 0:4096].rearrange("p (k q c) -> p k q c", k=4, q=NPAIR)
        s0ri = hflat[:, 4096:4608].rearrange("p (r q b) -> p r q b", r=2, q=NPAIR)
        sflat = S[:, :, :].rearrange("p h n -> p (h n)")
        fin_p = sflat[:, 0:64].rearrange("p (r q) -> p r q", r=2)
        fin_s = sflat[:, 64:576].rearrange("p (r q b) -> p r q b", r=2, q=NPAIR)
        st1 = sflat[:, 576:640].rearrange("p (r q) -> p r q", r=2)
        st2 = sflat[:, 640:704].rearrange("p (r q) -> p r q", r=2)
        aim = sflat[:, 704:768].rearrange("p (r q) -> p r q", r=2)
        htok = [big[:, D * t:D * (t + 1)] for t in range(5)]
        got = [[big[:, D * (5 + 2 * i + k):D * (6 + 2 * i + k)] for k in range(TOP)] for i in range(2)]
        otok = [big[:, D * (9 + i):D * (10 + i)] for i in range(2)]
        xtmp = big[:, D * 11:D * 12]
        xc = [yflat[:, D * i:D * (i + 1)] for i in range(2)]
        yc = [yflat[:, D * (2 + i):D * (3 + i)] for i in range(2)]
        zflat = zT[:, :, :].rearrange("p k t -> p (k t)")
        xcT = [zflat[:, D * i:D * (i + 1)].rearrange("p (k n) -> p k n", n=P) for i in range(2)]
        hid = [zflat[:, 2 * D + 2 * P * i:2 * D + 2 * P * (i + 1)] for i in range(2)]
        s1 = [zflat[:, 2 * D + 2 * P * (2 + i):2 * D + 2 * P * (3 + i)] for i in range(2)]
        rt = extra[:, 0, :]
        rx = extra[:, 1, :]

        xs, ys = d["xs"], d["ys"]
        xs_chunks, ys_chunks = (v.rearrange("(c p) n -> c p n", p=P) for v in (xs, ys))

        acc_full = sem("acc_full")
        dve_drained = sem("dve_drained")
        act_drained = sem("act_drained")
        slot_loaded = [sem(f"slot{i}_loaded") for i in range(NSLOT)]
        consts_in, x_in, conv_in, s0_in, bc_in = (sem(n) for n in ("consts_in", "x_in", "conv_in", "s0_in", "bc_in"))
        snew_out = [sem("snew_out0"), sem("snew_out1")]
        stored, conv_stored = sem("stored"), sem("conv_stored")
        dve_order, act_order, pool_order = sem("dve_order"), sem("act_order"), sem("pool_order")
        zero_ready, zeros_stored = sem("zero_ready"), sem("zeros_stored")
        one_hots_ready = sem("one_hots_ready")
        routed = sem("routed")
        scattered = sem("scattered")
        xc_loaded = [sem("xc_loaded0"), sem("xc_loaded1")]
        xt_full, xt_out = sem("xt_full"), sem("xt_out")
        h_full, s1_ready, hid_ready = sem("h_full"), sem("s1_ready"), sem("hid_ready")
        y_full, yc_ready = sem("y_full"), sem("yc_ready")
        ys_stored = [sem("ys_stored0"), sem("ys_stored1")]
        gathered = [sem("gathered0"), sem("gathered1")]
        combined = sem("combined")
        (over_loaded, over_xt_full, over_xt_out, over_h_full, over_s1_ready, over_hid_ready, over_y_full,
         over_yc_ready, over_stored) = (
            [sem(f"over_{n}{l}") for l in range(2)] for n in (
                "loaded", "xt_full", "xt_out", "h_full", "s1_ready", "hid_ready", "y_full", "yc_ready", "stored"))
        s5_angle_ready = sem("s5_angle_ready")
        gate_args_ready = sem("gate_args_ready")
        s5_b_ready = sem("s5_b_ready")
        ca_re_ready = sem("ca_re_ready")
        conv_done = sem("conv_done")
        decay_diff_ready = sem("decay_diff_ready")
        log_decay_ready = sem("log_decay_ready")
        g_ready = sem("g_ready")
        sample_input_ready = sem("sample_input_ready")
        l2_done = sem("l2_done")
        mod_ready = sem("mod_ready")
        x_scaled = sem("x_scaled")
        o_normed = sem("o_normed")
        out_ready = sem("out_ready")
        q_decayed = sem("q_decayed")
        expert_diff_ready = sem("expert_diff_ready")
        group_diff_ready = sem("group_diff_ready")
        row_masks_ready = sem("row_masks_ready")
        s5_fin_ready = sem("s5_fin_ready")
        entry_states_ready = sem("entry_states_ready")
        x_ready = sem("x_ready")
        zr_ready = sem("zr_ready")
        qkv_silu_done = sem("qkv_silu_done")
        dt_ready = sem("dt_ready")
        decay_rows_ready = sem("decay_rows_ready")
        decay_cols_ready = sem("decay_cols_ready")
        decay_exp_ready = sem("decay_exp_ready")
        gelu_done = sem("gelu_done")
        prompt_input_ready = sem("prompt_input_ready")
        l2_squares_ready = sem("l2_squares_ready")
        squares_ready = sem("squares_ready")
        o_squares_ready = sem("o_squares_ready")
        expert_exp_ready = sem("expert_exp_ready")
        group_exp_ready = sem("group_exp_ready")
        silu_c_ready = sem("silu_c_ready")
        softplus_ready = sem("softplus_ready")
        trig_ready = sem("trig_ready")
        a_block_ready = sem("a_block_ready")
        ca_im_ready = sem("ca_im_ready")
        history_ready = sem("history_ready")
        ones_ready = sem("ones_ready")
        u_masked = sem("u_masked")
        v_masked = sem("v_masked")
        zi_ready = sem("zi_ready")

        def at(label):
            return book.get(("at", label), 1)

        def reader(name):
            stem = name[:min(name.find(c) for c in name if c.isdigit())] if any(c.isdigit() for c in name) else name
            return act_drained if stem in READ_BY_SCALAR else dve_drained

        def filled(name):
            return use(name) + 1

        def use(name):
            return book.get(("use", name), 0)

        def buf(name):
            return acc[:, use(name) % NACC, :, :]

        def flatbuf(name, n, w):
            return buf(name).rearrange("p b c -> p (b c)")[:, 0:n * w].rearrange("p (n w) -> p n w", w=w)

        def tok(name):
            return buf(name)[:, :, 0:HT]

        def halves(ap):
            return ap.rearrange("p (b t) -> p b t", b=2)

        def bc(ap, axis, n):
            x = ap.unsqueeze(axis)
            return x.broadcast_to([n if i == axis else s for i, s in enumerate(x.shape)])

        def um(k, n, rows=None):
            rows = n if rows is None else rows
            return unit[k][0:rows, 0:H * n].rearrange("p (h n) -> p h n", n=n)

        def ur(k, n):
            return unit[k][0:n, 0:H * P].rearrange("p (h n) -> p h n", n=P)

        tiles = [(t, P * t, P if t < 4 else TS) for t in range(5)]
        tri = lambda t: TRIU if t < 4 else TRIU8
        block = ctx.enter_context(nc.Block())

        rtv = {"L": rt[:, 0:100].rearrange("p (t c) -> p t c", t=5),
               "ge": rt[:, 100:120].rearrange("p (t c) -> p t c", t=5),
               "ohg": rt[:, 120:140].rearrange("p (t c) -> p t c", t=5),
               "t4": rt[:, 140:160].rearrange("p (t c) -> p t c", t=5),
               "t16": rt[:, 160:240].rearrange("p (t g e) -> p t g e", t=5, g=4),
               "sel": rt[:, 240:260].rearrange("p (t c) -> p t c", t=5),
               "oh1": rt[:, 260:280].rearrange("p (t c) -> p t c", t=5),
               "oh2": rt[:, 280:300].rearrange("p (t c) -> p t c", t=5),
               "gm": rt[:, 300:305], "pg": rt[:, 305:310], "m1": rt[:, 310:315], "m2": rt[:, 315:320],
               "e2": rt[:, 320:325], "w1": rt[:, 325:330], "w2": rt[:, 330:335], "tm": rt[:, 335:340],
               "rank": rx[:, 240:320].rearrange("p (t e) -> p t e", t=5),
               "pos": rx[:, 320:400].rearrange("p (t e) -> p t e", t=5),
               "po": rx[:, 400:480].rearrange("p (t e) -> p t e", t=5),
               "tot": rx[:, 480:496], "chunks": rx[:, 496:512], "cum": rx[:, 512:528], "far": rx[:, 528:544],
               "le": rx[:, 544:672].rearrange("p (j e) -> p j e", e=E), "over": rx[:, 672:681],
               "row": rx[:, 681:691].rearrange("p (k t) -> p k t", k=TOP), "one": rx[:, 691:707]}
        choice = [rx[:, 80 * i:80 * (i + 1)].rearrange("p (t g e) -> p t g e", t=5, g=4) for i in range(3)]
        chosen = [rx[:, 80 * i:80 * (i + 1)].rearrange("p (t e) -> p t e", t=5) for i in range(3)]

        def zview(ap):
            return ap.rearrange("p (m q c) -> p m q c", m=8, q=4)

        def powers(r, m0, m1, c):
            return bc(pw[:, r, m0:m1, 4 * c:4 * c + 4], 3, 32)

        def over_m(ap, n):
            return bc(ap, 1, n)

        def unit_source(kind, a, u):
            if kind == "mod":
                return d["w_mod_mix" if a % 2 == 0 else "w_mod_ffn"][a // 2, u]
            if kind == "moe":
                return d[("w1", "w3", "w2")[u % 3]][a, u // 3]
            return d[kind][u]

        @block.sync
        def _(sp):
            def consts(dst, src):
                sp.dma_start(dst, src).then_inc(consts_in, up(consts_in, by=16))

            sp.dma_start(xT[:, :, :], d["xT"]).then_inc(x_in, 16)
            consts(cT[:, :, :], d["cT"])
            for dst, src in ((cst[:, :, :], "masks"), (bmod[:, :, :], "bmod"), (nrm[:, :, :], "nrm"),
                             (w_ba[:, :, :], "w_ba"), (onrm[:, :], "onrm"), (s5d[:, :], "s5d"),
                             (wr[:, :, :, :], "wr")):
                consts(dst, d[src])
            for i, src in enumerate(("a_log", "dt_bias")):
                consts(hp[:, i, :], d[src].partition_broadcast(P))
            for l in range(2):
                consts(br[:, l, :], d["br"][l].partition_broadcast(P))
            consts(lam[:, 0:2, :], d["lam"])
            for g in range(2):
                consts(lam[64 * g:64 * g + 64, 2, :], d["log_dt"][g].partition_broadcast(64))
            book["consts"] = now(consts_in)

            def load(n):
                if n >= NSLOT:
                    sp.wait_ge(acc_full, book.get(("unit_read", n - NSLOT), 1))
                loaded = slot_loaded[n % NSLOT]
                sp.dma_start(ring[:, n % NSLOT, :], unit_source(*units[n])).then_inc(
                    loaded, up(loaded, ("unit", n), by=16))

            def moe_loads(layer):
                first = unit_no["moe", layer, 0]
                done = E * layer
                for j in range(6):
                    load(first + j)
                sp.wait_ge(scattered, 16 * TOP * 5 * (layer + 1))
                for j in range(2):
                    sp.dma_start(xc[j], xs_chunks[j]).then_inc(xc_loaded[j], 16)
                for s in slot_loaded:
                    counts.enter(s, None, 16)

                def turn(i, last=False):
                    for j in range(2):
                        slots = [(first + 3 * j + x) % NSLOT for x in range(3)]
                        if not last:
                            sp.wait_ge(xt_full, i * 2 + (done + j + 1))
                            sp.dma_start(xc[j], xs_chunks[i * 2 + (2 + j)]).then_inc(xc_loaded[j], 16)
                            sp.wait_ge(h_full, i * 2 + (done + j + 1))
                            sp.dma_start(ring[:, slots[0], :], d["w1"][layer][i * 2 + (2 + j)]).then_inc(
                                slot_loaded[slots[0]], up(slot_loaded[slots[0]], by=16))
                            sp.dma_start(ring[:, slots[1], :], d["w3"][layer][i * 2 + (2 + j)]).then_inc(
                                slot_loaded[slots[1]], up(slot_loaded[slots[1]], by=16))
                            sp.wait_ge(y_full, i * 2 + (done + j + 1))
                            sp.dma_start(ring[:, slots[2], :], d["w2"][layer][i * 2 + (2 + j)]).then_inc(
                                slot_loaded[slots[2]], up(slot_loaded[slots[2]], by=16))
                        sp.wait_ge(yc_ready, i * 2 + (done + j + 1))
                        sp.dma_start(ys_chunks[i * 2 + j], yc[j]).then_inc(ys_stored[j], 16)

                with sp.Fori(0, E // 2 - 1) as i:
                    turn(i)
                for s in slot_loaded:
                    counts.leave(s, E // 2 - 1)
                turn(E // 2 - 1, last=True)
                for s in ys_stored:
                    sp.wait_ge(s, 16 * (E // 2) * (layer + 1))
                sp.wait_ge(routed, layer + 1)
                n_over = sp.value_load(over[0:1, 8:9], min_val=0, max_val=NOVER)
                with sp.Fori(0, NOVER) as j:
                    with sp.If(n_over > j):
                        e = sp.value_load(over[0:1, bass.ds(j, 1)], min_val=0, max_val=E - 1)
                        for x, w in enumerate(("w1", "w3", "w2")):
                            sp.dma_start(ring[:, x, :].unsqueeze(1),
                                         d[w][layer][bass.ds(e, 1)].rearrange("e p n -> p e n")).then_inc(
                                over_loaded[layer], 16)
                        sp.wait_ge(over_stored[layer], j * 16 + 16)
                        sp.dma_start(xc[0], xs_chunks[j + E]).then_inc(over_loaded[layer], 16)
                        sp.wait_ge(over_yc_ready[layer], j + 1)
                        sp.dma_start(ys_chunks[j + E], yc[0]).then_inc(over_stored[layer], 16)

            for n in range(unit_no["w_in", 0, 0]):
                load(n)
            sp.dma_start(cs_in, d["conv"]).then_inc(conv_in, up(conv_in, by=16))
            sp.dma_start(cw, d["cw"]).then_inc(conv_in, up(conv_in, by=16))
            for n in range(unit_no["w_in", 0, 0], unit_no["w_out", 0, 0]):
                load(n)
            sp.wait_ge(zero_ready, 1)
            zero = S[:, :, :].rearrange("p h n -> p (h n)").unsqueeze(1).broadcast_to([P, CHUNKS // 3, D])
            for c in range(3):
                rows = xs.rearrange("(c p) n -> p c n", p=P)[:, CHUNKS // 3 * c:CHUNKS // 3 * (c + 1), :]
                sp.dma_start(rows, zero).then_inc(zeros_stored, up(zeros_stored, by=16))
            for l in range(2):
                rows = ys.rearrange("(c p) n -> p c n", p=P)[:, E + NOVER // 2 * l:E + NOVER // 2 * (l + 1), :]
                sp.dma_start(rows, zero[:, 0:NOVER // 2, :]).then_inc(over_stored[l], 16)
            for n in range(unit_no["w_out", 0, 0], unit_no["moe", 0, 0]):
                load(n)
            sp.wait_ge(history_ready, at(f"cs{QKV - 1}"))
            sp.dma_start(o["s_conv"], cs_out).then_inc(conv_stored, up(conv_stored, by=16))
            sp.dma_start(o["p_conv"], cp_out).then_inc(conv_stored, up(conv_stored, by=16))
            sp.wait_ge(acc_full, filled("o3"))
            for h in range(H):
                sp.dma_start(s0v[h], d["s0"][h]).then_inc(s0_in, up(s0_in, by=16))
            sp.wait_ge(dve_drained, at("S3"))
            sp.dma_start(o["p_delta"], S[:, :, :]).then_inc(stored, up(stored, by=16))
            for h in range(H):
                sp.wait_ge(dve_drained, at(f"snew{h}"))
                sp.dma_start(o["s_delta"][h], snew[h % 2]).then_inc(snew_out[h % 2], up(snew_out[h % 2], by=16))
            sp.wait_ge(acc_full, filled("suS7"))
            moe_loads(0)
            for n in range(unit_no["s5in", 0, 0], unit_no["glu", 0, 0]):
                load(n)
            sp.wait_ge(acc_full, filled("u7"))
            sp.dma_start(BC, d["bc"]).then_inc(bc_in, up(bc_in, by=16))
            sp.dma_start(s0ri, d["s0ri"]).then_inc(bc_in, up(bc_in, by=16))
            for n in range(unit_no["glu", 0, 0], unit_no["moe", 1, 0]):
                load(n)
            sp.wait_ge(s5_fin_ready, at("s5fin"))
            sp.dma_start(o["p_ssm"], fin_p).then_inc(stored, up(stored, by=16))
            sp.dma_start(o["s_ssm"], fin_s).then_inc(stored, up(stored, by=16))
            moe_loads(1)
            sp.wait_ge(out_ready, at("out"))
            sp.dma_start(o["y"], yT[:, :, :]).then_inc(stored, up(stored, by=16))
            sp.wait_ge(stored, now(stored))
            sp.wait_ge(conv_stored, now(conv_stored))
            for s in snew_out:
                sp.wait_ge(s, now(s))

        @block.tensor
        def _(pe):
            state = {"n": 0}

            def begin(name):
                n = state["n"]
                book["use", name] = n
                book["name", n] = name
                if n >= NACC:
                    last = book["name", n - NACC]
                    pe.wait_ge(reader(last), at("read:" + last))
                state["n"] += 1
                return acc[:, n % NACC, :, :]

            def weights(n):
                pe.wait_ge(slot_loaded[n % NSLOT], at(("unit", n)))
                return ring[:, n % NSLOT, :]

            def project(name, w, rhs):
                ps = begin(name)
                for b in range(2):
                    for k in range(KD):
                        mm = pe.matmul(ps[:, b, 0:HT], w[:, k, :], rhs[:, k, HT * b:HT * b + HT],
                                       start=(k == 0), stop=(k == KD - 1))
                mm.then_inc(acc_full, 1)

            def norm_sums(i):
                pe.wait_ge(squares_ready, at(f"nsq{i}"))
                ps = begin(f"ssq{i}")
                for b in range(2):
                    for k in range(KD):
                        mm = pe.matmul(ps[:, b, 0:HT], ones[:, :], yT[:, k, HT * b:HT * b + HT],
                                       start=(k == 0), stop=(k == KD - 1))
                mm.then_inc(acc_full, 1)

            def await_input(i):
                pe.wait_ge(prompt_input_ready, at(f"h{i}"))
                pe.wait_ge(sample_input_ready, at(f"hs{i}"))

            def heads(name, lhsT, rhs, out=None):
                begin(name)
                for h in range(H):
                    mm = pe.matmul(out[:, h, :], lhsT(h), rhs(h), start=True, stop=True, skip_group_check=True)
                mm.then_inc(acc_full, 1)

            def adaln(m):
                for nb in range(6):
                    ps = begin(f"ada{m}_{nb}")
                    for kh in range(2):
                        n = unit_no["mod", m, 2 * nb + kh]
                        w = weights(n).rearrange("p (k c) -> p k c", k=4)
                        for k in range(4):
                            mm = pe.matmul(ps[0:9, 0, :], cT[:, 4 * kh + k, :], w[:, k, :],
                                           start=(kh + k == 0), stop=(kh + k == 4))
                        book["unit_read", n] = state["n"]
                    mm.then_inc(acc_full, 1)

            def adaln_turn(m):
                begin(f"adaT{m}")
                pe.wait_ge(act_drained, at(f"read:ada{m}_5"))
                out = flatbuf(f"adaT{m}", 24, 9)
                for j in range(24):
                    mm = pe.transpose(out[:, j, :], m_sb[:, m % 2, P * j:P * j + P], cst[0:9, IDENT, 0:9])
                mm.then_inc(acc_full, 1)

            def delta_tile(t, c0, n):
                k_ = lambda h: qkv[:, 8 + h, c0:c0 + n]
                q_ = lambda h: qkv[:, h, c0:c0 + n]
                v_ = lambda h: qkv[:, 16 + h, c0:c0 + n]
                for name, u, ready in ((f"gr{t}", M, f"ru{t}"), (f"br{t}", MT, f"rub{t}")):
                    pe.wait_ge(row_masks_ready, at(ready))
                    ps = begin(name)
                    w = min(512, H * n)
                    for b in range(H * n // w):
                        mm = pe.matmul(ps[:, b, 0:w], ones[0:n, :], unit[u][0:n, w * b:w * b + w],
                                       start=True, stop=True)
                    mm.then_inc(acc_full, 1)
                heads(f"kk{t}", k_, k_, flatbuf(f"kk{t}", H, n)[0:n])
                heads(f"qk{t}", k_, q_, flatbuf(f"qk{t}", H, n)[0:n])
                for name, src in ((f"kt{t}", k_), (f"vt{t}", v_)):
                    begin(name)
                    out = flatbuf(name, H, P)[0:n]
                    for h in range(H):
                        mm = pe.transpose(out[:, h, :], src(h), cst[:, IDENT, :])
                    mm.then_inc(acc_full, 1)
                pe.wait_ge(a_block_ready, at(f"ab{t}_0"))
                begin(f"A0{t}")
                out = flatbuf(f"A0{t}", H, n)[0:n]
                for h in range(H):
                    mm = pe.transpose(out[:, h, :], um(AB, n)[:, h, :], cst[0:n, IDENT, 0:n])
                mm.then_inc(acc_full, 1)
                for l in range(1, levels(t)):
                    pe.wait_ge(dve_drained, at(f"MT{t}_{l - 1}"))
                    pe.wait_ge(a_block_ready, at(f"ab{t}_{l}"))
                    heads(f"X{t}_{l}", lambda h: um(AB, n)[:, h, :], lambda h: um(M, n)[:, h, :],
                          flatbuf(f"X{t}_{l}", H, n)[0:n])
                    pe.wait_ge(act_drained, at(f"read:X{t}_{l}"))
                    if l < levels(t) - 1:
                        heads(f"MX{t}_{l}", lambda h: um(MT, n)[:, h, :], lambda h: um(EX, n)[:, h, :],
                              flatbuf(f"MX{t}_{l}", H, n)[0:n])
                    heads(f"MTX{t}_{l}", lambda h: um(EX, n)[:, h, :], lambda h: um(MT, n)[:, h, :],
                          flatbuf(f"MTX{t}_{l}", H, n)[0:n])
                pe.wait_ge(dve_drained, at(f"MT{t}_{levels(t) - 1}"))
                pe.wait_ge(dve_drained, at(f"read:kt{t}"))
                pe.wait_ge(dve_drained, at(f"read:vt{t}"))
                heads(f"wT{t}", lambda h: ur(KBGT, n)[:, h, :], lambda h: um(MT, n)[:, h, :],
                      flatbuf(f"wT{t}", H, n))
                pe.wait_ge(act_drained, at(f"read:wT{t}"))
                if t < 4:
                    if t:
                        pe.wait_ge(dve_drained, at(f"S{t - 1}"))
                    begin(f"vn{t}")
                    out = flatbuf(f"vn{t}", H, P)
                    for h in range(H):
                        pe.matmul(out[:, h, :], um(MT, n)[:, h, :], ur(VB, n)[:, h, :], start=True, stop=False,
                                  skip_group_check=True)
                        mm = pe.matmul(out[:, h, :], um(EX, n, P)[:, h, :], S[:, h, :], start=False, stop=True,
                                       skip_group_check=True)
                    mm.then_inc(acc_full, 1)
                    pe.wait_ge(act_drained, at(f"read:vn{t}"))
                    pe.wait_ge(q_decayed, at(f"qdT{t}"))
                    begin(f"o{t}")
                    out = flatbuf(f"o{t}", H, n)
                    for h in range(H):
                        pe.matmul(out[:, h, :], S[:, h, :], q_(h), start=True, stop=False, skip_group_check=True)
                        mm = pe.matmul(out[:, h, :], ur(AB, n)[:, h, :], um(QKE, n)[:, h, :], start=False,
                                       stop=True, skip_group_check=True)
                    mm.then_inc(acc_full, 1)
                    heads(f"su{t}", lambda h: ur(KDECT, n)[:, h, :], lambda h: ur(AB, n)[:, h, :],
                          flatbuf(f"su{t}", H, P))
                    return
                pe.wait_ge(s0_in, 16 * H)
                begin("vnT")
                out = flatbuf("vnT", H, n)
                for h in range(H):
                    pe.matmul(out[:, h, :], ur(VB, n)[:, h, :], um(MT, n)[:, h, :], start=True, stop=False,
                              skip_group_check=True)
                    for b in range(NSEQ):
                        mm = pe.matmul(out[:, h, LS * b:LS * b + LS], s0v[h][:, b, :],
                                       um(EX, n, P)[:, h, LS * b:LS * b + LS], start=False, stop=(b == NSEQ - 1),
                                       skip_group_check=True)
                mm.then_inc(acc_full, 1)
                pe.wait_ge(act_drained, at("read:vnT"))
                begin("vtr")
                out = flatbuf("vtr", H, P)[0:n]
                for h in range(H):
                    mm = pe.transpose(out[:, h, :], um(M, n, P)[:, h, :], cst[:, IDENT, :])
                mm.then_inc(acc_full, 1)
                pe.wait_ge(act_drained, at("read:vtr"))
                pe.wait_ge(q_decayed, at(f"qdT{t}"))
                begin("oS")
                out = flatbuf("oS", H, n)
                for h in range(H):
                    pe.matmul(out[:, h, :], ur(AB, n)[:, h, :], um(QKE, n)[:, h, :], start=True, stop=False,
                              skip_group_check=True)
                    for b in range(NSEQ):
                        mm = pe.matmul(out[:, h, LS * b:LS * b + LS], s0v[h][:, b, :],
                                       q_(h)[:, LS * b:LS * b + LS], start=False, stop=(b == NSEQ - 1),
                                       skip_group_check=True)
                mm.then_inc(acc_full, 1)
                for h in range(H):
                    pe.wait_ge(v_masked, at(f"vm{h}"))
                    ps = begin(f"suS{h}")
                    for b in range(2):
                        mm = pe.matmul(ps[:, b, :], ur(KDECT, n)[:, h, :], vmask[h % 2][:, 4 * b:4 * b + 4, :],
                                       start=True, stop=True)
                    mm.then_inc(acc_full, 1)

            def route(layer, i):
                await_input(i)
                ps = begin(f"rt{layer}")
                for t, c0, n in tiles:
                    for k in range(KD):
                        mm = pe.matmul(ps[0:n, 0, 20 * t:20 * t + 20], hT[:, k, c0:c0 + n], wr[:, layer, k, :],
                                       start=(k == 0), stop=(k == KD - 1), skip_group_check=True)
                mm.then_inc(acc_full, 1)
                for t, c0, n in tiles:
                    out = flatbuf(f"tm{layer}_{t}", KD, P)
                    begin(f"tm{layer}_{t}")
                    for k in range(KD):
                        mm = pe.transpose(out[0:n, k, :], hT[:, k, c0:c0 + n], cst[:, IDENT, :])
                    mm.then_inc(acc_full, 1)
                pe.wait_ge(one_hots_ready, layer + 1)
                ps = begin(f"rk{layer}")
                for t, c0, n in tiles:
                    for b in range(t + 1):
                        before = ones[:, 0:n] if b < t else cst[0:n, TRIU, 0:n]
                        pe.matmul(ps[0:n, 0, E * t:E * (t + 1)], before, chosen[2][0:P if b < t else n, b, :],
                                  start=(b == 0), stop=(b == t), skip_group_check=True)
                for t, c0, n in tiles:
                    mm = pe.matmul(ps[:, 1, 0:E], ones[0:n, :], chosen[2][0:n, t, :], start=(t == 0), stop=(t == 4))
                mm.then_inc(acc_full, 1)

            def turn_rows(x, xt):
                for k in range(KD):
                    mm = pe.transpose(xt[:, k, :], x[:, P * k:P * (k + 1)], cst[:, IDENT, :])
                return mm

            def hidden(w1, w3, xt):
                for x, w in ((0, w1), (1, w3)):
                    wv = w.rearrange("p (m k c) -> p m k c", m=2, k=KD)
                    for f in range(2):
                        for k in range(KD):
                            mm = pe.matmul(acc[:, H_ACC, x, P * f:P * (f + 1)], wv[:, f, k, :], xt[:, k, :],
                                           start=(k == 0), stop=(k == KD - 1), skip_group_check=True)
                return mm

            def outputs(y, hd, w2):
                for b in range(2):
                    for f in range(2):
                        mm = pe.matmul(y[:, b, :], hd[:, P * f:P * (f + 1)], w2[:, D * f + 512 * b:D * f + 512 * (b + 1)],
                                       start=(f == 0), stop=(f == 1))
                return mm

            def moe(layer):
                for n in range(state["n"] - NACC, state["n"]):
                    last = book["name", n]
                    pe.wait_ge(reader(last), at("read:" + last))
                first = unit_no["moe", layer, 0]
                done = E * layer
                xt_acc = acc[:, XT_ACC].rearrange("p b c -> p (b c)").rearrange("p (k n) -> p k n", n=P)
                pe.wait_ge(xc_loaded[0], 16 * (E // 2) * layer + 16)
                turn_rows(xc[0], xt_acc).then_inc(xt_full, 1)

                def turn(i, last=False):
                    for j in range(2):
                        slots = [(first + 3 * j + x) % NSLOT for x in range(3)]
                        w1, w3, w2 = (ring[:, s, :] for s in slots)
                        loaded = [at(("unit", first + 3 * j + x)) for x in range(3)]
                        pe.wait_ge(slot_loaded[slots[0]], i * 16 + loaded[0])
                        pe.wait_ge(slot_loaded[slots[1]], i * 16 + loaded[1])
                        pe.wait_ge(xt_out, i * 2 + (done + j + 1))
                        hidden(w1, w3, xcT[j]).then_inc(h_full, 1)
                        if not (last and j == 1):
                            pe.wait_ge(xc_loaded[1 - j], i * 16 + (16 * (E // 2) * layer + 16 + 16 * j))
                            turn_rows(xc[1 - j], xt_acc).then_inc(xt_full, 1)
                        pe.wait_ge(slot_loaded[slots[2]], i * 16 + loaded[2])
                        pe.wait_ge(hid_ready, i * 2 + (done + j + 1))
                        outputs(acc[:, Y_ACC + j], hid[j], w2).then_inc(y_full, 1)

                with pe.Fori(0, E // 2 - 1) as i:
                    turn(i)
                turn(E // 2 - 1, last=True)
                for j in range(6):
                    book["unit_read", first + 3 * E - 6 + j] = state["n"]
                n_over = pe.value_load(over[0:1, 8:9], min_val=0, max_val=NOVER)
                with pe.Fori(0, NOVER) as j:
                    with pe.If(n_over > j):
                        pe.wait_ge(over_loaded[layer], j * 64 + 64)
                        turn_rows(xc[0], xt_acc).then_inc(over_xt_full[layer], 1)
                        pe.wait_ge(over_xt_out[layer], j + 1)
                        hidden(ring[:, 0, :], ring[:, 1, :], xcT[0]).then_inc(over_h_full[layer], 1)
                        pe.wait_ge(over_hid_ready[layer], j + 1)
                        outputs(acc[:, Y_ACC], hid[0], ring[:, 2, :]).then_inc(over_y_full[layer], 1)
                for t, c0, n in tiles:
                    pe.wait_ge(combined, at(f"o{layer}_{t}"))
                    out = flatbuf(f"ot{layer}_{t}", KD, n)
                    begin(f"ot{layer}_{t}")
                    for k in range(KD):
                        mm = pe.transpose(out[:, k, :], otok[t % 2][0:n, P * k:P * (k + 1)], cst[0:n, IDENT, 0:n])
                    mm.then_inc(acc_full, 1)

            def s5():
                await_input(2)
                for m in range(KD):
                    n = unit_no["s5in", 0, m // 2]
                    w = weights(n).rearrange("p (m k c) -> p m k c", m=2, k=KD)
                    project(f"u{m}", w[:, m % 2], hT)
                    book["unit_read", n] = state["n"]
                for c in range(KD):
                    for r, name in enumerate(("zr", "zi")):
                        if r == 0:
                            pe.wait_ge(zr_ready, at(f"zr{c}"))
                        else:
                            pe.wait_ge(zi_ready, at(f"zi{c}"))
                        begin(f"{name}{c}")
                        out = flatbuf(f"{name}{c}", 8, P)
                        for m in range(8):
                            mm = pe.transpose(out[:, m, :], Z[r][:, P * m:P * m + P], cst[:, IDENT, :])
                        mm.then_inc(acc_full, 1)
                    pe.wait_ge(act_drained, at(f"read:zi{c}"))
                    pe.wait_ge(u_masked, at(f"um{c}"))
                    ps = begin(f"inc{c}")
                    uv = uM[c % 2].rearrange("p j (c t) -> p t j c", t=8)
                    for r in range(2):
                        for tau in range(8):
                            mm = pe.matmul(ps[:, r, 0:4 * NCK].rearrange("p (j c) -> p j c", j=4),
                                           ZT[:, r, 7 - tau, :], uv[:, tau], start=(tau == 0), stop=(tau == 7))
                    mm.then_inc(acc_full, 1)
                pe.wait_ge(entry_states_ready, at("sin"))
                for c in range(KD):
                    pe.wait_ge(ca_re_ready, at(f"car{c}"))
                    pe.wait_ge(ca_im_ready, at(f"cai{c}"))
                    ps = begin(f"K{c}")
                    for j in range(4):
                        q = 4 * c + j
                        for r in range(2):
                            mm = pe.matmul(ps[32 * j:32 * j + 32, 0, 0:256].rearrange("p (m c) -> p m c", m=8),
                                           BC[:, r, q, :], CA[r][:, 0:8, j, :], start=(r == 0), stop=(r == 1),
                                           skip_group_check=True)
                    mm.then_inc(acc_full, 1)
                    ps = begin(f"yc{c}")
                    for j in range(4):
                        q = 4 * c + j
                        for r in range(2):
                            mm = pe.matmul(ps[0:NCK, j // 2, 256 * (j % 2):256 * (j % 2) + 256].rearrange(
                                               "p (m c) -> p m c", m=8),
                                           SIN[:, r, q, :], CA[r][:, 1:9, j, :], start=(r == 0), stop=(r == 1),
                                           skip_group_check=True)
                    mm.then_inc(acc_full, 1)
                    pe.wait_ge(dve_drained, at(f"kb{c}"))
                    pe.wait_ge(act_drained, at(f"read:yc{c}"))
                    ps = begin(f"ys{c}")
                    uv = zT[:, c, :].rearrange("p (c t) -> p t c", t=8)
                    for b in range(2):
                        ov = ps[:, b, 0:4 * NCK].rearrange("p (t c) -> p t c", t=4)
                        for lag in range(8):
                            lo, hi = max(4 * b, lag), 4 * b + 4
                            if lo >= hi:
                                continue
                            pe.matmul(ov[:, lo - 4 * b:4], KB[:, lag, :], uv[:, lo - lag:hi - lag],
                                      start=(lag == 0), stop=False, skip_group_check=True)
                        for tau in range(4):
                            mm = pe.matmul(ov[:, tau, :], YS[:, 4 * b + tau, :], cst[0:NCK, IDENT, 0:NCK],
                                           start=False, stop=(tau == 3), skip_group_check=True)
                    mm.then_inc(acc_full, 1)
                pe.wait_ge(gelu_done, at("gelu"))
                for m in range(KD):
                    n = unit_no["glu", 0, m]
                    w = weights(n).rearrange("p (m k c) -> p m k c", m=2, k=KD)
                    project(f"ga{m}", w[:, 0], yT)
                    project(f"gg{m}", w[:, 1], yT)
                    book["unit_read", n] = state["n"]

            pe.wait_ge(consts_in, book.get("consts", 16))
            pe.wait_ge(ones_ready, at("ones"))
            norm_sums(0)
            pe.wait_ge(silu_c_ready, at("silu_c"))
            for m in range(4):
                adaln(m)
                if m:
                    adaln_turn(m - 1)
            adaln_turn(3)
            await_input(0)
            ps = begin("ba")
            for t, c0, n in tiles:
                for k in range(KD):
                    mm = pe.matmul(ps[0:n, 0, 16 * t:16 * t + 16], hT[:, k, c0:c0 + n], w_ba[:, k, :],
                                   start=(k == 0), stop=(k == KD - 1), skip_group_check=True)
            mm.then_inc(acc_full, 1)
            for m in range(32):
                n = unit_no["w_in", 0, m // 2]
                w = weights(n).rearrange("p (m k c) -> p m k c", m=2, k=KD)
                project(f"p{m}", w[:, m % 2], hT)
                book["unit_read", n] = state["n"]
                if 2 <= m < 18:
                    pe.wait_ge(l2_squares_ready, at(f"l2sq{m - 2}"))
                    ps = begin(f"l{m - 2}")
                    for b in range(2):
                        mm = pe.matmul(ps[:, b, 0:HT], ones[:, :], sq[m % 2][:, HT * b:HT * b + HT],
                                       start=True, stop=True)
                    mm.then_inc(acc_full, 1)
            pe.wait_ge(g_ready, at("gg"))
            ps = begin("G")
            for t, c0, n in tiles:
                for b, mask in ((0, cst[0:n, tri(t), 0:n]), (1, ones[0:n, 0:n] if t < 4 else cst[0:n, ONES8, 0:n])):
                    mm = pe.matmul(ps[0:n, b, 8 * t:8 * t + 8], mask, gt[0:n, GG, t, :], start=True, stop=True,
                                   skip_group_check=True)
            mm.then_inc(acc_full, 1)
            pe.wait_ge(l2_done, at("l215"))
            pe.wait_ge(qkv_silu_done, at("act23"))
            for t, c0, n in tiles:
                delta_tile(t, c0, n)
            pe.wait_ge(o_squares_ready, at("osq"))
            for h in range(H):
                ps = begin(f"on{h}")
                for b in range(2):
                    mm = pe.matmul(ps[:, b, 0:HT], ones[:, :], hT[:, h, HT * b:HT * b + HT], start=True, stop=True)
                mm.then_inc(acc_full, 1)
            pe.wait_ge(o_normed, at("onorm"))
            for m in range(KD):
                n = unit_no["w_out", 0, m // 2]
                w = weights(n).rearrange("p (m k c) -> p m k c", m=2, k=KD)
                project(f"w{m}", w[:, m % 2], yT)
                book["unit_read", n] = state["n"]
            norm_sums(1)
            route(0, 1)
            moe(0)
            norm_sums(2)
            s5()
            norm_sums(3)
            route(1, 3)
            moe(1)
            norm_sums(4)

        @block.scalar
        def _(act):
            def step(ins):
                ins.then_inc(act_order, up(act_order))
                act.wait_ge(act_order, now(act_order))

            def norm(i, m):
                act.wait_ge(x_ready, at(f"x{i}"))
                act.activation(yT[:, :, :], xT[:, :, :], ACT.Square).then_inc(
                    squares_ready, up(squares_ready, f"nsq{i}"))
                act.wait_ge(squares_ready, now(squares_ready))
                act.wait_ge(acc_full, filled(f"ssq{i}"))
                act.activation(halves(rb[:, :]), tok(f"ssq{i}"), ACT.Sqrt, bias=small[:, 0:1], scale=1.0 / D).then_inc(
                    act_drained, up(act_drained, f"read:ssq{i}"))
                act.wait_ge(act_drained, now(act_drained))
                if m is None:
                    return
                act.wait_ge(x_scaled, at(f"npre{i}"))
                act.wait_ge(mod_ready, at(f"mod{m}"))
                for k in range(KD):
                    ins = act.activation(hT[:, k, 0:SEQ], yT[:, k, 0:SEQ], ACT.Identity,
                                         bias=modT[:, m, k, 0:1], scale=modA[:, m, k, 0:1])
                    if k < KD - 1:
                        ins.then_inc(act_order, up(act_order))
                act.wait_ge(act_order, now(act_order))
                ins.then_inc(prompt_input_ready, up(prompt_input_ready, f"h{i}"))
                act.wait_ge(prompt_input_ready, now(prompt_input_ready))

            def rows_out(layer):
                if layer == 0:
                    for s in snew_out:
                        act.wait_ge(s, 16 * (H // 2))
                for t, c0, n in tiles:
                    act.wait_ge(acc_full, filled(f"tm{layer}_{t}"))
                    act.activation(htok[t][0:n, :], flatbuf(f"tm{layer}_{t}", 1, D)[0:n, 0, :], ACT.Copy).then_inc(
                        act_drained, up(act_drained, f"read:tm{layer}_{t}"))
                    act.wait_ge(act_drained, now(act_drained))

            def moe(layer):
                done = E * layer
                xt_acc = acc[:, XT_ACC].rearrange("p b c -> p (b c)").rearrange("p (k n) -> p k n", n=P)
                act.wait_ge(xt_full, done + 1)
                act.activation(xcT[0], xt_acc, ACT.Copy).then_inc(xt_out, 1)

                def turn(i, last=False):
                    for j in range(2):
                        act.wait_ge(h_full, i * 2 + (done + j + 1))
                        act.activation(s1[j], acc[:, H_ACC, 0, 0:2 * P], ACT.Silu).then_inc(s1_ready, 1)
                        if not (last and j == 1):
                            act.wait_ge(xt_full, i * 2 + (done + j + 2))
                            act.activation(xcT[1 - j], xt_acc, ACT.Copy).then_inc(xt_out, 1)

                with act.Fori(0, E // 2 - 1) as i:
                    turn(i)
                turn(E // 2 - 1, last=True)
                act.wait_ge(routed, layer + 1)
                n_over = act.value_load(over[0:1, 8:9], min_val=0, max_val=NOVER)
                with act.Fori(0, NOVER) as j:
                    with act.If(n_over > j):
                        act.wait_ge(over_xt_full[layer], j + 1)
                        act.activation(xcT[0], xt_acc, ACT.Copy).then_inc(over_xt_out[layer], 1)
                        act.wait_ge(over_h_full[layer], j + 1)
                        act.activation(s1[0], acc[:, H_ACC, 0, 0:2 * P], ACT.Silu).then_inc(over_s1_ready[layer], 1)

            act.wait_ge(consts_in, book.get("consts", 16))
            act.wait_ge(ones_ready, at("ones"))
            act.activation(cT[:, :, :], cT[:, :, :], ACT.Silu).then_inc(silu_c_ready, up(silu_c_ready, "silu_c"))
            act.wait_ge(silu_c_ready, now(silu_c_ready))
            step(act.activation(lam[:, 2, :], lam[:, 2, :], ACT.Exp))
            act.activation(hp[:, 0, :], hp[:, 0, :], ACT.Exp).then_inc(dt_ready, up(dt_ready, "dt"))
            act.wait_ge(dt_ready, now(dt_ready))
            act.wait_ge(s5_angle_ready, at("ang"))
            step(act.activation(s5t[:, 0, :], s5t[:, 0, :], ACT.Exp))
            step(act.activation(s5t[:, 3, :], s5t[:, 1, :], ACT.Sin))
            act.activation(s5t[:, 4, :], s5t[:, 2, :], ACT.Sin, bias=small[:, 2:3], scale=-1.0).then_inc(
                trig_ready, up(trig_ready, "trig"))
            act.wait_ge(trig_ready, now(trig_ready))
            act.wait_ge(x_in, 16)
            act.activation(yT[:, :, :], xT[:, :, :], ACT.Square).then_inc(squares_ready, up(squares_ready, "nsq0"))
            act.wait_ge(squares_ready, now(squares_ready))
            act.wait_ge(acc_full, filled("ssq0"))
            act.activation(halves(rb[:, :]), tok("ssq0"), ACT.Sqrt, bias=small[:, 0:1], scale=1.0 / D).then_inc(
                act_drained, up(act_drained, "read:ssq0"))
            act.wait_ge(act_drained, now(act_drained))
            for m in range(4):
                for nb in range(6):
                    act.wait_ge(acc_full, filled(f"ada{m}_{nb}"))
                    if m >= 2 and nb == 0:
                        act.wait_ge(acc_full, filled(f"adaT{m - 2}"))
                    act.activation(m_sb[:, m % 2, 512 * nb:512 * nb + 512], buf(f"ada{m}_{nb}")[0:9, 0, :],
                                         ACT.Copy).then_inc(act_drained, up(act_drained, f"read:ada{m}_{nb}"))
                    act.wait_ge(act_drained, now(act_drained))
            act.wait_ge(x_scaled, at("npre0"))
            act.wait_ge(mod_ready, at("mod0"))
            for k in range(KD):
                ins = act.activation(hT[:, k, 0:SEQ], yT[:, k, 0:SEQ], ACT.Identity,
                                     bias=modT[:, 0, k, 0:1], scale=modA[:, 0, k, 0:1])
                if k < KD - 1:
                    ins.then_inc(act_order, up(act_order))
            act.wait_ge(act_order, now(act_order))
            ins.then_inc(prompt_input_ready, up(prompt_input_ready, "h0"))
            act.wait_ge(prompt_input_ready, now(prompt_input_ready))
            act.wait_ge(gate_args_ready, at("ba"))
            step(act.activation(gt[:, BETA], gt[:, BB], ACT.Sigmoid))
            step(act.activation(gt[:, G1], gt[:, G2], ACT.Exp, scale=-1.0))
            act.activation(gt[:, G2], gt[:, G1], ACT.Ln, bias=1.0).then_inc(
                softplus_ready, up(softplus_ready, "splus"))
            act.wait_ge(softplus_ready, now(softplus_ready))
            for m in range(32 + 3):
                if m < QKV:
                    act.wait_ge(acc_full, filled(f"p{m}"))
                    if m >= 2:
                        act.wait_ge(conv_done, at(f"conv{m - 2}"))
                        act.wait_ge(history_ready, at(f"cs{m - 2}"))
                    act.activation(halves(raw[m % 2][:, 3:3 + T]), tok(f"p{m}"), ACT.Copy).then_inc(
                        act_drained, up(act_drained, f"read:p{m}"))
                    act.wait_ge(act_drained, now(act_drained))
                elif m < 32:
                    act.wait_ge(acc_full, filled(f"p{m}"))
                    act.activation(halves(zT[:, m - QKV, :]), tok(f"p{m}"), ACT.Silu).then_inc(
                        act_drained, up(act_drained, f"read:p{m}"))
                    act.wait_ge(act_drained, now(act_drained))
                if 1 <= m <= QKV:
                    act.wait_ge(conv_done, at(f"conv{m - 1}"))
                    act.activation(qkv[:, m - 1, :], qkv[:, m - 1, :], ACT.Silu).then_inc(
                        qkv_silu_done, up(qkv_silu_done, f"act{m - 1}"))
                    act.wait_ge(qkv_silu_done, now(qkv_silu_done))
                if 1 <= m <= 16:
                    if m >= 3:
                        act.wait_ge(acc_full, filled(f"l{m - 3}"))
                    act.activation(sq[(m - 1) % 2], qkv[:, m - 1, :], ACT.Square).then_inc(
                        l2_squares_ready, up(l2_squares_ready, f"l2sq{m - 1}"))
                    act.wait_ge(l2_squares_ready, now(l2_squares_ready))
                if 2 <= m < 18:
                    act.wait_ge(acc_full, filled(f"l{m - 2}"))
                    if m >= 4:
                        act.wait_ge(l2_done, at(f"l2{m - 4}"))
                    is_q = m - 2 < 8
                    act.activation(halves(ln[m % 2]), tok(f"l{m - 2}"), ACT.Sqrt,
                                         bias=small[:, 1:2] if is_q else small[:, 0:1],
                                         scale=float(P) if is_q else 1.0).then_inc(
                                             act_drained, up(act_drained, f"read:l{m - 2}"))
                    act.wait_ge(act_drained, now(act_drained))
            act.wait_ge(log_decay_ready, at("gcol"))
            step(act.activation(gt[:, G1], gt[:, GCOL], ACT.Exp))
            act.activation(gt[:, CKDEC], gt[:, G2], ACT.Exp).then_inc(decay_cols_ready, up(decay_cols_ready, "ecol"))
            act.wait_ge(decay_cols_ready, now(decay_cols_ready))
            for t, c0, n in tiles:
                act.wait_ge(acc_full, filled(f"gr{t}"))
                if t:
                    act.wait_ge(dve_drained, at(f"S{t - 1}"))
                act.activation(um(EG, n, P), flatbuf(f"gr{t}", H, n), ACT.Exp).then_inc(
                    decay_rows_ready, up(decay_rows_ready, f"eG{t}"))
                act.wait_ge(decay_rows_ready, now(decay_rows_ready))
                act.wait_ge(decay_diff_ready, at(f"diff{t}"))
                act.activation(um(EX, n), um(EX, n), ACT.Exp).then_inc(decay_exp_ready, up(decay_exp_ready, f"ex{t}"))
                act.wait_ge(decay_exp_ready, now(decay_exp_ready))
                for l in range(1, levels(t)):
                    act.wait_ge(acc_full, filled(f"X{t}_{l}"))
                    if l == 1:
                        act.wait_ge(dve_drained, at(f"read:qk{t}"))
                    else:
                        act.wait_ge(acc_full, filled(f"MTX{t}_{l - 1}"))
                    act.activation(um(EX, n), flatbuf(f"X{t}_{l}", H, n)[0:n], ACT.Copy).then_inc(
                        act_drained, up(act_drained, f"read:X{t}_{l}"))
                    act.wait_ge(act_drained, now(act_drained))
                act.wait_ge(acc_full, filled(f"wT{t}"))
                act.activation(um(EX, n, P), flatbuf(f"wT{t}", H, n), ACT.Copy).then_inc(
                    act_drained, up(act_drained, f"read:wT{t}"))
                act.wait_ge(act_drained, now(act_drained))
                if t < 4:
                    act.wait_ge(acc_full, filled(f"vn{t}"))
                    act.activation(ur(AB, n), flatbuf(f"vn{t}", H, P), ACT.Copy).then_inc(
                        act_drained, up(act_drained, f"read:vn{t}"))
                    act.wait_ge(act_drained, now(act_drained))
                    act.wait_ge(acc_full, filled(f"o{t}"))
                    act.activation(yT[:, :, c0:c0 + n], flatbuf(f"o{t}", H, n), ACT.Copy).then_inc(
                        act_drained, up(act_drained, f"read:o{t}"))
                    act.wait_ge(act_drained, now(act_drained))
                else:
                    act.wait_ge(acc_full, filled("vnT"))
                    act.activation(um(M, n, P), flatbuf("vnT", H, n), ACT.Copy).then_inc(
                        act_drained, up(act_drained, "read:vnT"))
                    act.wait_ge(act_drained, now(act_drained))
                    act.wait_ge(acc_full, filled("vtr"))
                    act.activation(ur(AB, n), flatbuf("vtr", H, P)[0:n], ACT.Copy).then_inc(
                        act_drained, up(act_drained, "read:vtr"))
                    act.wait_ge(act_drained, now(act_drained))
                    act.wait_ge(acc_full, filled("oS"))
                    act.activation(yT[:, :, c0:c0 + n], flatbuf("oS", H, n), ACT.Copy).then_inc(
                        act_drained, up(act_drained, "read:oS"))
                    act.wait_ge(act_drained, now(act_drained))
            act.wait_ge(dve_drained, at("snew7"))
            act.activation(hT[:, :, :], yT[:, :, :], ACT.Square).then_inc(o_squares_ready, up(o_squares_ready, "osq"))
            act.wait_ge(o_squares_ready, now(o_squares_ready))
            for h in range(H):
                act.wait_ge(acc_full, filled(f"on{h}"))
                act.activation(halves(hT[:, h, :]), tok(f"on{h}"), ACT.Sqrt, bias=small[:, 0:1],
                                     scale=1.0 / P).then_inc(act_drained, up(act_drained, f"read:on{h}"))
                act.wait_ge(act_drained, now(act_drained))
            norm(1, 1)

            def route(layer):
                act.wait_ge(group_diff_ready, at(f"rga{layer}"))
                act.activation(rtv["ge"], rtv["ge"], ACT.Exp).then_inc(
                    group_exp_ready, up(group_exp_ready, f"rgb{layer}"))
                act.wait_ge(group_exp_ready, now(group_exp_ready))
                act.wait_ge(expert_diff_ready, at(f"rea{layer}"))
                act.activation(rtv["e2"], rtv["e2"], ACT.Exp).then_inc(
                    expert_exp_ready, up(expert_exp_ready, f"reb{layer}"))
                act.wait_ge(expert_exp_ready, now(expert_exp_ready))

            rows_out(0)
            route(0)
            moe(0)
            norm(2, 2)
            for m in range(KD):
                act.wait_ge(acc_full, filled(f"u{m}"))
                act.activation(halves(zT[:, m, :]), tok(f"u{m}"), ACT.Copy).then_inc(
                    act_drained, up(act_drained, f"read:u{m}"))
                act.wait_ge(act_drained, now(act_drained))
            for c in range(KD):
                for r, name in enumerate(("zr", "zi")):
                    act.wait_ge(acc_full, filled(f"{name}{c}"))
                    if c and r == 0:
                        act.wait_ge(acc_full, filled(f"inc{c - 1}"))
                    act.activation(ZT[:, r], flatbuf(f"{name}{c}", 8, P), ACT.Copy).then_inc(
                        act_drained, up(act_drained, f"read:{name}{c}"))
                    act.wait_ge(act_drained, now(act_drained))
            for c in range(KD):
                act.wait_ge(acc_full, filled(f"yc{c}"))
                if c:
                    act.wait_ge(acc_full, filled(f"ys{c - 1}"))
                else:
                    act.wait_ge(entry_states_ready, at("sin"))
                act.activation(YS.rearrange("p t (j c) -> p j t c", j=4),
                                     flatbuf(f"yc{c}", 4, 256)[0:NCK].rearrange("p j (t c) -> p j t c", t=8),
                                     ACT.Copy).then_inc(act_drained, up(act_drained, f"read:yc{c}"))
                act.wait_ge(act_drained, now(act_drained))
            act.wait_ge(dve_drained, at("ysum"))
            act.activation(yT[:, :, :], yT[:, :, :], ACT.Gelu_apprx_tanh).then_inc(gelu_done, up(gelu_done, "gelu"))
            act.wait_ge(gelu_done, now(gelu_done))
            for m in range(KD):
                act.wait_ge(acc_full, filled(f"gg{m}"))
                if m >= 2:
                    act.wait_ge(dve_drained, at(f"glu{m - 2}"))
                act.activation(halves(extra[:, m % 2, 0:T]), tok(f"gg{m}"), ACT.Sigmoid).then_inc(
                    act_drained, up(act_drained, f"read:gg{m}"))
                act.wait_ge(act_drained, now(act_drained))
            norm(3, 3)
            rows_out(1)
            route(1)
            moe(1)
            norm(4, None)

        @block.vector
        def _(dve):
            def step(ins):
                ins.then_inc(dve_order, up(dve_order))
                dve.wait_ge(dve_order, now(dve_order))

            tt, ts, stt = dve.tensor_tensor, dve.tensor_scalar, dve.scalar_tensor_tensor

            def seqs(ap):
                return ap.rearrange("p k (b s) -> p k b s", s=LS)

            def norm(i, m):
                dve.wait_ge(act_drained, at(f"read:ssq{i}"))
                step(dve.reciprocal(rb[:, :], rb[:, :]))
                tt(yT[:, :, :], xT[:, :, :], bc(rb[:, :], 1, KD), ALU.mult).then_inc(
                    x_scaled, up(x_scaled, f"npre{i}"))
                dve.wait_ge(x_scaled, now(x_scaled))
                if m is None:
                    tt(yT[:, :, :], yT[:, :, :], bc(nrm[:, 4, :], 2, T), ALU.mult).then_inc(
                        out_ready, up(out_ready, "out"))
                    dve.wait_ge(out_ready, now(out_ready))
                    return
                step(tt(seqs(hT[:, :, SEQ:T]), seqs(yT[:, :, SEQ:T]), bc(modA[:, m, :, 1:9], 3, LS), ALU.mult))
                tt(seqs(hT[:, :, SEQ:T]), seqs(hT[:, :, SEQ:T]), bc(modT[:, m, 0:KD, 1:9], 3, LS), ALU.add).then_inc(
                    sample_input_ready, up(sample_input_ready, f"hs{i}"))
                dve.wait_ge(sample_input_ready, now(sample_input_ready))

            def residual(k, m, prompt, sample, tmp, label=None, name=None):
                gate = modT[:, m, 16 + k, :]
                for src, c0, n in prompt:
                    step(stt(xT[:, k, c0:c0 + n], src, gate[:, 0:1], xT[:, k, c0:c0 + n], ALU.mult, ALU.add))
                ins = tt(tmp.rearrange("p (b s) -> p b s", s=LS), sample.rearrange("p (b s) -> p b s", s=LS),
                         bc(gate[:, 1:9], 2, LS), ALU.mult)
                if name:
                    ins.then_inc(dve_drained, up(dve_drained, "read:" + name))
                    dve.wait_ge(dve_drained, now(dve_drained))
                else:
                    step(ins)
                tt(xT[:, k, SEQ:T], xT[:, k, SEQ:T], tmp, ALU.add).then_inc(x_ready, up(x_ready, label))
                dve.wait_ge(x_ready, now(x_ready))

            dve.memset(S[:, :, :], 0.0).then_inc(zero_ready, 1)
            dve.wait_ge(zero_ready, 1)
            dve.wait_ge(consts_in, book.get("consts", 16))
            dve.wait_ge(dt_ready, at("dt"))
            lr, li, dt = lam[:, 0, :], lam[:, 1, :], lam[:, 2, :]
            step(tt(s5t[:, 0, :], lr, dt, ALU.mult))
            step(tt(s5t[:, 1, :], li, dt, ALU.mult))
            step(ts(s5t[:, 2, :], s5t[:, 1, :], 1.0 / (2.0 * np.pi), MAGIC, ALU.mult, ALU.add))
            step(ts(s5t[:, 2, :], s5t[:, 2, :], MAGIC, None, ALU.subtract))
            step(stt(s5t[:, 1, :], s5t[:, 2, :], -TWO_PI_HI, s5t[:, 1, :], ALU.mult, ALU.add))
            step(stt(s5t[:, 1, :], s5t[:, 2, :], -TWO_PI_LO, s5t[:, 1, :], ALU.mult, ALU.add))
            step(ts(s5t[:, 1, :], s5t[:, 1, :], PI_LIM, -PI_LIM, ALU.min, ALU.max))
            step(ts(s5t[:, 2, :], s5t[:, 1, :], -1.0, None, ALU.mult))
            tt(s5t[:, 2, :], s5t[:, 2, :], s5t[:, 1, :], ALU.max).then_inc(s5_angle_ready, up(s5_angle_ready, "ang"))
            dve.wait_ge(s5_angle_ready, now(s5_angle_ready))
            dve.wait_ge(trig_ready, at("trig"))
            step(dve.memset(pw[:, 0, 0, :], 1.0))
            step(dve.memset(pw[:, 1, 0, :], 0.0))
            ar, ai = pw[:, 0, 1, :], pw[:, 1, 1, :]
            step(tt(ar, s5t[:, 0, :], s5t[:, 4, :], ALU.mult))
            step(tt(ai, s5t[:, 0, :], s5t[:, 3, :], ALU.mult))
            t0, t1, t2 = s5t[:, 5, :], s5t[:, 6, :], s5t[:, 7, :]
            for m in range(1, 8):
                step(tt(t0, pw[:, 0, m, :], ar, ALU.mult))
                step(tt(t1, pw[:, 1, m, :], ai, ALU.mult))
                step(tt(pw[:, 0, m + 1, :], t0, t1, ALU.subtract))
                step(tt(t0, pw[:, 0, m, :], ai, ALU.mult))
                step(tt(t1, pw[:, 1, m, :], ar, ALU.mult))
                step(tt(pw[:, 1, m + 1, :], t0, t1, ALU.add))
            step(tt(t0, lr, lr, ALU.mult))
            step(tt(t1, li, li, ALU.mult))
            step(tt(t2, t0, t1, ALU.add))
            step(dve.reciprocal(t2, t2))
            step(ts(s5t[:, 0, :], ar, 1.0, None, ALU.subtract))
            step(tt(t0, s5t[:, 0, :], lr, ALU.mult))
            step(tt(t1, ai, li, ALU.mult))
            step(tt(t0, t0, t1, ALU.add))
            step(tt(fz[:, 0, :], t0, t2, ALU.mult))
            step(tt(t0, ai, lr, ALU.mult))
            step(tt(t1, s5t[:, 0, :], li, ALU.mult))
            step(tt(t0, t0, t1, ALU.subtract))
            step(tt(fz[:, 1, :], t0, t2, ALU.mult))

            dve.wait_ge(x_in, 16)
            dve.wait_ge(act_drained, at("read:ssq0"))
            step(dve.reciprocal(rb[:, :], rb[:, :]))
            tt(yT[:, :, :], xT[:, :, :], bc(rb[:, :], 1, KD), ALU.mult).then_inc(x_scaled, up(x_scaled, "npre0"))
            dve.wait_ge(x_scaled, now(x_scaled))
            for m in range(4):
                dve.wait_ge(acc_full, filled(f"adaT{m}"))
                tt(modT[:, m], flatbuf(f"adaT{m}", 24, 9), bc(bmod[:, m, :], 2, 9), ALU.add).then_inc(
                    dve_drained, up(dve_drained, f"read:adaT{m}"))
                dve.wait_ge(dve_drained, now(dve_drained))
                step(ts(modA[:, m], modT[:, m, KD:2 * KD, :], 1.0, None, ALU.add))
                tt(modA[:, m], modA[:, m], bc(nrm[:, m, :], 2, 9), ALU.mult).then_inc(
                    mod_ready, up(mod_ready, f"mod{m}"))
                dve.wait_ge(mod_ready, now(mod_ready))
                if m == 0:
                    step(tt(seqs(hT[:, :, SEQ:T]), seqs(yT[:, :, SEQ:T]), bc(modA[:, 0, :, 1:9], 3, LS), ALU.mult))
                    tt(seqs(hT[:, :, SEQ:T]), seqs(hT[:, :, SEQ:T]), bc(modT[:, 0, 0:KD, 1:9], 3, LS),
                              ALU.add).then_inc(sample_input_ready, up(sample_input_ready, "hs0"))
                    dve.wait_ge(sample_input_ready, now(sample_input_ready))
            step(dve.memset(gt[:, :, :, :], 0.0))
            dve.wait_ge(acc_full, filled("ba"))
            for rows, t0_, nt in ((P, 0, 4), (TS, 4, 1)):
                src = buf("ba")[0:rows, 0, 16 * t0_:16 * (t0_ + nt)].rearrange("p (t c) -> p t c", c=16)
                step(dve.tensor_copy(gt[0:rows, BB, t0_:t0_ + nt, :], src[:, :, 0:8]))
                ins = tt(gt[0:rows, BA, t0_:t0_ + nt, :], src[:, :, 8:16], bc(hp[0:rows, 1, :], 1, nt), ALU.add)
                if t0_:
                    ins.then_inc(dve_drained, up(dve_drained, "read:ba"))
                    dve.wait_ge(dve_drained, now(dve_drained))
                else:
                    step(ins)
            step(ts(gt[:, G2], gt[:, BA], -1.0, None, ALU.mult))
            tt(gt[:, G2], gt[:, G2], gt[:, BA], ALU.max).then_inc(gate_args_ready, up(gate_args_ready, "ba"))
            dve.wait_ge(gate_args_ready, now(gate_args_ready))
            dve.wait_ge(softplus_ready, at("splus"))
            step(stt(gt[:, G1], gt[:, BA], 0.0, gt[:, G2], ALU.max, ALU.add))
            step(tt(gt[:, G1], gt[:, G1], bc(hp[:, 0, :], 1, 5), ALU.mult))
            ts(gt[:, GG], gt[:, G1], -1.0, None, ALU.mult).then_inc(g_ready, up(g_ready, "gg"))
            dve.wait_ge(g_ready, now(g_ready))
            dve.wait_ge(conv_in, 32)
            dve.wait_ge(prompt_input_ready, at("h0"))
            for i in range(2):
                step(dve.memset(raw[i][:, 0:3], 0.0))
            for m in range(QKV + 3):
                if m < QKV:
                    dve.wait_ge(act_drained, at(f"read:p{m}"))
                    dst = qkv[:, m, 0:SEQ]
                    sdst = qkv[:, m, SEQ:T].rearrange("p (b s) -> p b s", s=LS)
                    if m == 0:
                        dve.wait_ge(acc_full, filled("adaT3"))
                    step(ts(dst, raw[m % 2][:, 0:SEQ], cw[:, m, 0:1], None, ALU.mult))
                    for j in range(1, CW):
                        step(stt(dst, raw[m % 2][:, j:j + SEQ], cw[:, m, j:j + 1], dst, ALU.mult, ALU.add))
                    dve.wait_ge(history_ready, at(f"cs{m}"))
                    step(ts(sdst, sraw[m % 2][:, :, 0:LS], cw[:, m, 0:1], None, ALU.mult))
                    for j in range(1, CW):
                        ins = stt(sdst, sraw[m % 2][:, :, j:j + LS], cw[:, m, j:j + 1], sdst, ALU.mult, ALU.add)
                        if j < CW - 1:
                            step(ins)
                        else:
                            ins.then_inc(conv_done, up(conv_done, f"conv{m}"))
                            dve.wait_ge(conv_done, now(conv_done))
                if 3 <= m < 19:
                    dve.wait_ge(act_drained, at(f"read:l{m - 3}"))
                    step(dve.reciprocal(ln[(m - 3) % 2], ln[(m - 3) % 2]))
                    tt(qkv[:, m - 3, :], qkv[:, m - 3, :], ln[(m - 3) % 2], ALU.mult).then_inc(
                        l2_done, up(l2_done, f"l2{m - 3}"))
                    dve.wait_ge(l2_done, now(l2_done))
            dve.wait_ge(acc_full, filled("G"))
            for b, dst in ((0, GCOL), (1, GLAST)):
                step(dve.tensor_copy(gt[:, dst, 0:4, :],
                                     buf("G")[:, b, 0:32].rearrange("p (t h) -> p t h", t=4)))
                ins = dve.tensor_copy(gt[0:TS, dst, 4, :], buf("G")[0:TS, b, 32:40])
                if b:
                    ins.then_inc(dve_drained, up(dve_drained, "read:G"))
                    dve.wait_ge(dve_drained, now(dve_drained))
                else:
                    step(ins)
            tt(gt[:, G2], gt[:, GLAST], gt[:, GCOL], ALU.subtract).then_inc(
                log_decay_ready, up(log_decay_ready, "gcol"))
            dve.wait_ge(log_decay_ready, now(log_decay_ready))
            dve.wait_ge(decay_cols_ready, at("ecol"))
            step(stt(gt[:, CKBG], gt[:, G1], -1.0, gt[:, BETA], ALU.mult, ALU.mult))
            dve.wait_ge(conv_stored, 32)
            for t, c0, n in tiles:
                dve.wait_ge(acc_full, filled(f"su{t - 1}" if t else "p31"))
                tt(um(M, n), bc(cst[0:n, tri(t), 0:n], 1, H), bc(gt[0:n, GG, t, :], 2, n), ALU.mult).then_inc(
                    row_masks_ready, up(row_masks_ready, f"ru{t}"))
                dve.wait_ge(row_masks_ready, now(row_masks_ready))
                tt(um(MT, n), bc(cst[0:n, IDENT, 0:n], 1, H), bc(gt[0:n, BETA, t, :], 2, n), ALU.mult).then_inc(
                    row_masks_ready, up(row_masks_ready, f"rub{t}"))
                dve.wait_ge(row_masks_ready, now(row_masks_ready))
                dve.wait_ge(decay_rows_ready, at(f"eG{t}"))
                tt(um(EX, n), flatbuf(f"gr{t}", H, n)[0:n], bc(gt[0:n, GCOL, t, :], 2, n), ALU.subtract).then_inc(
                    dve_drained, up(dve_drained, f"read:gr{t}"))
                dve.wait_ge(dve_drained, now(dve_drained))
                ts(um(EX, n), um(EX, n), 0.0, None, ALU.min).then_inc(
                    decay_diff_ready, up(decay_diff_ready, f"diff{t}"))
                dve.wait_ge(decay_diff_ready, now(decay_diff_ready))
                dve.wait_ge(decay_exp_ready, at(f"ex{t}"))
                step(tt(um(EX, n), um(EX, n), bc(cst[0:n, tri(t), 0:n], 1, H), ALU.mult))
                dve.wait_ge(acc_full, filled(f"kk{t}"))
                tt(um(AT, n), flatbuf(f"kk{t}", H, n)[0:n], um(EX, n), ALU.mult).then_inc(
                    dve_drained, up(dve_drained, f"read:kk{t}"))
                dve.wait_ge(dve_drained, now(dve_drained))
                ins = tt(um(AT, n), um(AT, n), flatbuf(f"br{t}", H, n)[0:n], ALU.mult)
                ins.then_inc(dve_drained, up(dve_drained, f"read:br{t}", f"AT{t}"))
                dve.wait_ge(dve_drained, now(dve_drained))
                dve.wait_ge(acc_full, filled(f"qk{t}"))
                tt(um(QKE, n), flatbuf(f"qk{t}", H, n)[0:n], um(EX, n), ALU.mult).then_inc(
                    dve_drained, up(dve_drained, f"read:qk{t}"))
                dve.wait_ge(dve_drained, now(dve_drained))
                tt(qkv[:, 0:H, c0:c0 + n], qkv[:, 0:H, c0:c0 + n], um(EG, n, P), ALU.mult).then_inc(
                    q_decayed, up(q_decayed, f"qdT{t}"))
                dve.wait_ge(q_decayed, now(q_decayed))
                dve.wait_ge(acc_full, filled(f"kt{t}"))
                step(tt(ur(KBGT, n), flatbuf(f"kt{t}", H, P)[0:n], bc(gt[0:n, CKBG, t, :], 2, P), ALU.mult))
                tt(ur(KDECT, n), flatbuf(f"kt{t}", H, P)[0:n], bc(gt[0:n, CKDEC, t, :], 2, P), ALU.mult).then_inc(
                    dve_drained, up(dve_drained, f"read:kt{t}"))
                dve.wait_ge(dve_drained, now(dve_drained))
                dve.wait_ge(acc_full, filled(f"vt{t}"))
                tt(ur(VB, n), flatbuf(f"vt{t}", H, P)[0:n], bc(gt[0:n, BETA, t, :], 2, P), ALU.mult).then_inc(
                    dve_drained, up(dve_drained, f"read:vt{t}"))
                dve.wait_ge(dve_drained, now(dve_drained))
                dve.wait_ge(a_block_ready, at(f"ab{t}_0"))
                dve.wait_ge(acc_full, filled(f"A0{t}"))
                eye = bc(cst[0:n, IDENT, 0:n], 1, H)
                step(tt(um(MT, n), eye, um(AB, n), ALU.subtract))
                tt(um(M, n), eye, flatbuf(f"A0{t}", H, n)[0:n], ALU.subtract).then_inc(
                    dve_drained, up(dve_drained, f"read:A0{t}", f"MT{t}_0"))
                dve.wait_ge(dve_drained, now(dve_drained))
                for l in range(1, levels(t)):
                    if l < levels(t) - 1:
                        dve.wait_ge(acc_full, filled(f"MX{t}_{l}"))
                        tt(um(M, n), um(M, n), flatbuf(f"MX{t}_{l}", H, n)[0:n], ALU.subtract).then_inc(
                            dve_drained, up(dve_drained, f"read:MX{t}_{l}"))
                        dve.wait_ge(dve_drained, now(dve_drained))
                    dve.wait_ge(acc_full, filled(f"MTX{t}_{l}"))
                    ins = tt(um(MT, n), um(MT, n), flatbuf(f"MTX{t}_{l}", H, n)[0:n], ALU.subtract)
                    ins.then_inc(dve_drained, up(dve_drained, f"read:MTX{t}_{l}", f"MT{t}_{l}"))
                    dve.wait_ge(dve_drained, now(dve_drained))
                if t < 4:
                    dve.wait_ge(acc_full, filled(f"su{t}"))
                    if t == 0:
                        dve.wait_ge(zeros_stored, 48)
                        for s in over_stored:
                            dve.wait_ge(s, 16)
                    step(tt(S[:, :, :], S[:, :, :], bc(um(EG, n, P)[:, :, n - 1], 2, P), ALU.mult))
                    ins = tt(S[:, :, :], S[:, :, :], flatbuf(f"su{t}", H, P), ALU.add)
                    ins.then_inc(dve_drained, up(dve_drained, f"read:su{t}", f"S{t}"))
                    dve.wait_ge(dve_drained, now(dve_drained))
            for h in range(H):
                n = TS
                dve.wait_ge(acc_full, filled(f"suS{h}"))
                if h >= 2:
                    dve.wait_ge(snew_out[h % 2], 16 * (h // 2))
                step(tt(snew[h % 2], s0v[h], bc(um(EG, n, P)[:, h, LS - 1:TS:LS], 2, P), ALU.mult))
                ins = tt(snew[h % 2], snew[h % 2], flatbuf(f"suS{h}", NSEQ, P), ALU.add)
                ins.then_inc(dve_drained, up(dve_drained, f"read:suS{h}", f"snew{h}"))
                dve.wait_ge(dve_drained, now(dve_drained))

            for h in range(H):
                dve.wait_ge(act_drained, at(f"read:on{h}"))
                step(dve.reciprocal(hT[:, h, :], hT[:, h, :]))
                step(tt(yT[:, h, :], yT[:, h, :], hT[:, h, :], ALU.mult))
                stt(yT[:, h, :], yT[:, h, :], onrm[:, 0:1], zT[:, h, :], ALU.mult, ALU.mult).then_inc(
                    o_normed, up(o_normed, "onorm" if h == H - 1 else None))
                dve.wait_ge(o_normed, now(o_normed))
            for m in range(KD):
                dve.wait_ge(acc_full, filled(f"w{m}"))
                ps = buf(f"w{m}")
                residual(m, 0, [(ps[:, 0, 0:HT], 0, HT), (ps[:, 1, 0:SEQ - HT], HT, SEQ - HT)],
                         ps[:, 1, SEQ - HT:HT], rb[:, 0:TS], "x1" if m == KD - 1 else None, f"w{m}")

            def choose(values, width, out):
                step(dve.tensor_reduce(rtv["tm"], values, AX.X, ALU.max))
                step(tt(out, values, bc(rtv["tm"], 2, 4), ALU.is_ge))
                step(tt(out, out, bc(cst[:, MISC, 4:8], 1, 5), ALU.mult))
                step(dve.tensor_reduce(width, out, AX.X, ALU.max))
                step(tt(out, out, bc(width, 2, 4), ALU.is_equal))

            def moe(layer, i, m):
                r = rtv
                step(dve.memset(rt[:, 0:340], 0.0))
                step(dve.memset(rx[:, 0:707], 0.0))
                step(dve.memset(r["one"], 1.0))
                dve.wait_ge(acc_full, filled(f"rt{layer}"))
                for rows, t0, nt in ((P, 0, 4), (TS, 4, 1)):
                    src = buf(f"rt{layer}")[0:rows, 0, 20 * t0:20 * (t0 + nt)].rearrange("p (t c) -> p t c", c=20)
                    ins = tt(r["L"][0:rows, t0:t0 + nt, :], src, bc(br[0:rows, layer, :], 1, nt), ALU.add)
                    if t0:
                        ins.then_inc(dve_drained, up(dve_drained, f"read:rt{layer}"))
                        dve.wait_ge(dve_drained, now(dve_drained))
                    else:
                        step(ins)
                lg, le = r["L"][:, :, 0:4], r["L"][:, :, 4:20].rearrange("p t (g e) -> p t g e", g=4)
                choose(lg, r["gm"], r["ohg"])
                tt(r["ge"], lg, bc(r["tm"], 2, 4), ALU.subtract).then_inc(
                    group_diff_ready, up(group_diff_ready, f"rga{layer}"))
                dve.wait_ge(group_diff_ready, now(group_diff_ready))
                dve.wait_ge(group_exp_ready, at(f"rgb{layer}"))
                step(dve.tensor_reduce(r["pg"], r["ge"], AX.X, ALU.add))
                step(dve.reciprocal(r["pg"], r["pg"]))
                step(tt(r["t16"], le, bc(r["ohg"], 3, 4), ALU.mult))
                step(dve.tensor_reduce(r["sel"], r["t16"].rearrange("p t g e -> p t e g"), AX.X, ALU.add))
                choose(r["sel"], r["gm"], r["oh1"])
                step(dve.tensor_copy(r["m1"], r["tm"]))
                step(stt(r["t4"], r["oh1"], -BIG, r["sel"], ALU.mult, ALU.add))
                choose(r["t4"], r["gm"], r["oh2"])
                tt(r["e2"], r["tm"], r["m1"], ALU.subtract).then_inc(
                    expert_diff_ready, up(expert_diff_ready, f"rea{layer}"))
                step(tt(choice[0], bc(r["ohg"], 3, 4), bc(r["oh1"], 2, 4), ALU.mult))
                step(tt(choice[1], bc(r["ohg"], 3, 4), bc(r["oh2"], 2, 4), ALU.mult))
                tt(chosen[2], chosen[0], chosen[1], ALU.add).then_inc(one_hots_ready, 1)
                dve.wait_ge(expert_diff_ready, now(expert_diff_ready))
                dve.wait_ge(expert_exp_ready, at(f"reb{layer}"))
                step(ts(r["w1"], r["e2"], 1.0, None, ALU.add))
                step(dve.reciprocal(r["w1"], r["w1"]))
                step(tt(r["w1"], r["w1"], r["pg"], ALU.mult))
                step(tt(r["w2"], r["w1"], r["e2"], ALU.mult))
                dve.wait_ge(acc_full, filled(f"rk{layer}"))
                ps = buf(f"rk{layer}")
                step(dve.tensor_copy(r["rank"][:, 0:4, :], ps[:, 0, 0:4 * E].rearrange("p (t e) -> p t e", e=E)))
                step(dve.tensor_copy(r["rank"][0:TS, 4, :], ps[0:TS, 0, 4 * E:5 * E]))
                dve.tensor_copy(r["tot"], ps[:, 1, 0:E]).then_inc(dve_drained, up(dve_drained, f"read:rk{layer}"))
                dve.wait_ge(dve_drained, now(dve_drained))
                for c in range(1, -(-T // P)):
                    step(stt(r["chunks"], r["tot"], P * c + 0.5, r["chunks"], ALU.is_ge, ALU.add))
                step(dve.tensor_tensor_scan(r["cum"], r["one"], r["chunks"], 0.0, ALU.mult, ALU.add))
                step(tt(r["le"], bc(r["cum"], 1, NOVER), bc(cst[:, MISC, 40:40 + NOVER], 2, E), ALU.is_le))
                step(dve.tensor_reduce(r["over"][:, 0:NOVER], r["le"], AX.X, ALU.add))
                step(ts(r["over"][:, 0:NOVER], r["over"][:, 0:NOVER], float(E - 1), None, ALU.min))
                step(dve.tensor_copy(r["over"][:, 8:9], r["cum"][:, E - 1:E]))
                step(dve.tensor_copy(over[:, :], r["over"]))
                step(tt(r["far"], r["cum"], r["chunks"], ALU.subtract))
                step(stt(r["far"], r["far"], float(P), cst[:, MISC, 24:24 + E], ALU.mult, ALU.add))
                step(ts(r["pos"], r["rank"], P + 0.5, None, ALU.is_ge))
                step(tt(r["pos"], r["pos"], bc(r["far"], 1, 5), ALU.mult))
                step(tt(r["rank"], r["rank"], bc(cst[:, MISC, 8:8 + E], 1, 5), ALU.add))
                step(tt(r["pos"], r["pos"], r["rank"], ALU.add))
                for k in range(TOP):
                    step(tt(r["po"], r["pos"], chosen[k], ALU.mult))
                    step(dve.tensor_reduce(r["row"][:, k, :], r["po"], AX.X, ALU.add))
                dve.tensor_copy(row_of[:, :, :], r["row"]).then_inc(routed, 1)
                dve.wait_ge(routed, layer + 1)
                done = E * layer

                def turn(i, first=False):
                    for j in range(2):
                        dve.wait_ge(s1_ready, i * 2 + (done + j + 1))
                        tt(hid[j], s1[j], acc[:, H_ACC, 1, 0:2 * P], ALU.mult).then_inc(hid_ready, 1)
                        dve.wait_ge(y_full, i * 2 + (done + j + 1))
                        if not first:
                            dve.wait_ge(ys_stored[j], i * 16 + 16 * (E // 2) * layer)
                        dve.tensor_copy(yc[j], acc[:, Y_ACC + j].rearrange("p b c -> p (b c)")).then_inc(yc_ready, 1)
                        dve.wait_ge(yc_ready, i * 2 + (done + j + 1))

                turn(0, first=True)
                with dve.Fori(1, E // 2) as it:
                    turn(it)
                for s in ys_stored:
                    dve.wait_ge(s, 16 * (E // 2) * (layer + 1))
                n_over = dve.value_load(over[0:1, 8:9], min_val=0, max_val=NOVER)
                with dve.Fori(0, NOVER) as j:
                    with dve.If(n_over > j):
                        dve.wait_ge(over_s1_ready[layer], j + 1)
                        tt(hid[0], s1[0], acc[:, H_ACC, 1, 0:2 * P], ALU.mult).then_inc(over_hid_ready[layer], 1)
                        dve.wait_ge(over_y_full[layer], j + 1)
                        dve.tensor_copy(yc[0], acc[:, Y_ACC].rearrange("p b c -> p (b c)")).then_inc(
                            over_yc_ready[layer], 1)
                for t_ in range(len(tiles) + 1):
                    if t_ < len(tiles):
                        t, c0, n = tiles[t_]
                        ot, (g1, g2) = otok[t % 2][0:n, :], (g[0:n, :] for g in got[t % 2])
                        dve.wait_ge(gathered[t % 2], at(f"g{layer}_{t}"))
                        step(ts(ot, g1, r["w1"][0:n, t:t + 1], None, ALU.mult))
                        stt(ot, g2, r["w2"][0:n, t:t + 1], ot, ALU.mult, ALU.add).then_inc(
                            combined, up(combined, f"o{layer}_{t}"))
                        dve.wait_ge(combined, now(combined))
                    if t_:
                        t, c0, n = tiles[t_ - 1]
                        dve.wait_ge(acc_full, filled(f"ot{layer}_{t}"))
                        src = flatbuf(f"ot{layer}_{t}", KD, n)
                        tmp = xtmp[:, 0:KD * n].rearrange("p (k n) -> p k n", n=n)
                        if t < 4:
                            ins = tt(tmp, src, bc(modT[:, m, 16:24, 0], 2, n), ALU.mult)
                        else:
                            ins = tt(seqs(tmp), seqs(src), bc(modT[:, m, 16:24, 1:9], 3, LS), ALU.mult)
                        ins.then_inc(dve_drained, up(dve_drained, f"read:ot{layer}_{t}"))
                        dve.wait_ge(dve_drained, now(dve_drained))
                        tt(xT[:, :, c0:c0 + n], xT[:, :, c0:c0 + n], tmp, ALU.add).then_inc(
                            x_ready, up(x_ready, f"x{i + 1}" if t == 4 else None))
                        dve.wait_ge(x_ready, now(x_ready))

            norm(1, 1)
            moe(0, 1, 1)
            norm(2, 2)

            dve.wait_ge(bc_in, 32)
            e0, e1 = (extra[:, i, :].rearrange("p (q c) -> p q c", q=NPAIR) for i in range(2))
            fr, fi = bc(fz[:, 0, :], 2, 32), bc(fz[:, 1, :], 2, 32)
            step(tt(e0, BC[:, 0], fr, ALU.mult))
            step(tt(e1, BC[:, 1], fi, ALU.mult))
            step(tt(e0, e0, e1, ALU.subtract))
            step(tt(e1, BC[:, 1], fr, ALU.mult))
            step(tt(BC[:, 1], BC[:, 0], fi, ALU.mult))
            step(tt(BC[:, 1], BC[:, 1], e1, ALU.add))
            dve.tensor_copy(BC[:, 0], e0).then_inc(s5_b_ready, up(s5_b_ready, "bb"))
            dve.wait_ge(s5_b_ready, now(s5_b_ready))
            for c in range(KD + 1):
                if c < KD:
                    if c:
                        dve.wait_ge(acc_full, filled(f"zr{c - 1}"))
                    zv, ev = zview(Z[0]), zview(extra[:, 0, :])
                    step(tt(zv, powers(0, 0, 8, c), over_m(BC[:, 0, 4 * c:4 * c + 4, :], 8), ALU.mult))
                    step(tt(ev, powers(1, 0, 8, c), over_m(BC[:, 1, 4 * c:4 * c + 4, :], 8), ALU.mult))
                    tt(zv, zv, ev, ALU.subtract).then_inc(zr_ready, up(zr_ready, f"zr{c}"))
                    dve.wait_ge(zr_ready, now(zr_ready))
                if c:
                    dve.wait_ge(acc_full, filled(f"inc{c - 1}"))
                    dve.tensor_copy(INC[:, :, 4 * c - 4:4 * c, :],
                                          buf(f"inc{c - 1}")[:, :, 0:4 * NCK].rearrange("p r (j c) -> p r j c", j=4)).then_inc(
                                              dve_drained, up(dve_drained, f"read:inc{c - 1}"))
                    dve.wait_ge(dve_drained, now(dve_drained))
            a8r, a8i = pw[:, 0, 8, :], pw[:, 1, 8, :]
            dve.wait_ge(zi_ready, at("zi7"))
            step(ts(BC[:, 1], BC[:, 1], -1.0, None, ALU.mult))
            step(ts(aim[:, 0, :], a8i, -1.0, None, ALU.mult))
            step(dve.tensor_copy(aim[:, 1, :], a8i))
            step(dve.memset(SIN[:, :, :, 0], 0.0))
            with dve.Fori(0, NCP // 8) as it:
                counts.enter(dve_order, it, 40)
                for k in range(8):
                    cur = SIN[:, :, :, it * 8 + k]
                    step(tt(st1, cur, bc(a8r, 1, 2), ALU.mult))
                    step(tt(st2[:, 0, :], SIN[:, 1, :, it * 8 + k], aim[:, 0, :], ALU.mult))
                    step(tt(st2[:, 1, :], SIN[:, 0, :, it * 8 + k], aim[:, 1, :], ALU.mult))
                    step(tt(st1, st1, INC[:, :, :, it * 8 + k], ALU.add))
                    step(tt(SIN[:, :, :, it * 8 + (k + 1)], st1, st2, ALU.add))
            counts.leave(dve_order, NCP // 8)
            step(dve.tensor_copy(fin_p, SIN[:, :, :, NCP]))
            step(dve.tensor_copy(SIN[:, :, :, NCP:NCK], s0ri))
            e0, e1 = (extra[:, i, 0:512].rearrange("p (r q b) -> p r q b", r=2, q=NPAIR) for i in range(2))
            step(tt(e0, s0ri, bc(bc(a8r, 1, 2), 3, NSEQ), ALU.mult))
            for r in range(2):
                step(tt(e1[:, r], s0ri[:, 1 - r], bc(aim[:, r], 2, NSEQ), ALU.mult))
            step(tt(e0, e0, e1, ALU.add))
            tt(fin_s, e0, INC[:, :, :, NCP:NCK], ALU.add).then_inc(s5_fin_ready, up(s5_fin_ready, "s5fin"))
            dve.wait_ge(s5_fin_ready, now(s5_fin_ready))
            ts(SIN[:, 1], SIN[:, 1], -1.0, None, ALU.mult).then_inc(entry_states_ready, up(entry_states_ready, "sin"))
            dve.wait_ge(entry_states_ready, now(entry_states_ready))
            for c in range(KD):
                if c:
                    dve.wait_ge(acc_full, filled(f"yc{c - 1}"))
                step(tt(CA[0], powers(0, 0, 9, c), over_m(BC[:, 2, 4 * c:4 * c + 4, :], 9), ALU.mult))
                step(tt(catmp[0], powers(1, 0, 9, c), over_m(BC[:, 3, 4 * c:4 * c + 4, :], 9), ALU.mult))
                tt(CA[0], CA[0], catmp[0], ALU.subtract).then_inc(ca_re_ready, up(ca_re_ready, f"car{c}"))
                dve.wait_ge(ca_re_ready, now(ca_re_ready))
                dve.wait_ge(acc_full, filled(f"K{c}"))
                if c:
                    dve.wait_ge(acc_full, filled(f"ys{c - 1}"))
                quad = bc(bc(cst[:, MISC, 0:4], 1, 8), 3, 32)
                tt(KB.rearrange("p m (j c) -> p m j c", j=4), bc(flatbuf(f"K{c}", 8, 32), 2, 4), quad,
                         ALU.mult).then_inc(dve_drained, up(dve_drained, f"read:K{c}", f"kb{c}"))
                dve.wait_ge(dve_drained, now(dve_drained))
                dve.wait_ge(acc_full, filled(f"ys{c}"))
                for b in range(2):
                    tc = lambda ap: ap.rearrange("p (c t) -> p t c", t=8)[:, 4 * b:4 * b + 4]
                    ins = stt(tc(yT[:, c, :]), tc(zT[:, c, :]), s5d[:, c:c + 1],
                              buf(f"ys{c}")[:, b, 0:4 * NCK].rearrange("p (t c) -> p t c", t=4), ALU.mult, ALU.add)
                    if b:
                        ins.then_inc(dve_drained, up(dve_drained, f"read:ys{c}", "ysum" if c == KD - 1 else None))
                        dve.wait_ge(dve_drained, now(dve_drained))
                    else:
                        step(ins)
            for m in range(KD):
                dve.wait_ge(acc_full, filled(f"ga{m}"))
                dve.wait_ge(act_drained, at(f"read:gg{m}"))
                t_ = hflat[:, T * (m % 2):T * (m % 2) + T]
                tt(halves(t_), tok(f"ga{m}"), halves(extra[:, m % 2, 0:T]), ALU.mult).then_inc(
                    dve_drained, up(dve_drained, f"read:ga{m}", f"glu{m}"))
                dve.wait_ge(dve_drained, now(dve_drained))
                residual(m, 2, [(t_[:, 0:SEQ], 0, SEQ)], t_[:, SEQ:T], rb[:, 0:TS], "x3" if m == KD - 1 else None)
            norm(3, 3)
            moe(1, 3, 3)
            norm(4, None)

        @block.gpsimd
        def _(pool):
            def step(ins):
                ins.then_inc(pool_order, up(pool_order))
                pool.wait_ge(pool_order, now(pool_order))

            tt = pool.tensor_tensor
            step(pool.memset(small[:, 0:1], EPS))
            step(pool.memset(small[:, 1:2], P * EPS))
            step(pool.memset(small[:, 2:3], float(np.pi / 2)))
            pool.memset(ones[:, :], 1.0).then_inc(ones_ready, up(ones_ready, "ones"))
            pool.wait_ge(ones_ready, now(ones_ready))
            pool.wait_ge(conv_in, 32)
            for m in range(QKV):
                pool.wait_ge(act_drained, at(f"read:p{m}"))
                if m >= 2:
                    pool.wait_ge(conv_done, at(f"conv{m - 2}"))
                r = raw[m % 2][:, 3:3 + T]
                rs = r[:, SEQ:T].rearrange("p (b s) -> p b s", s=LS)
                step(pool.tensor_copy(sraw[m % 2][:, :, 0:3], cs_in[:, m]))
                step(pool.tensor_copy(cs_out[:, m], rs[:, :, LS - 3:LS]))
                step(pool.tensor_copy(cp_out[:, m, :], r[:, SEQ - 3:SEQ]))
                pool.tensor_copy(sraw[m % 2][:, :, 3:11], rs).then_inc(history_ready, up(history_ready, f"cs{m}"))
                pool.wait_ge(history_ready, now(history_ready))
            for t, c0, n in tiles:
                for l in range(levels(t)):
                    if l == 0:
                        pool.wait_ge(dve_drained, at(f"AT{t}"))
                        if t:
                            pool.wait_ge(acc_full, filled(f"su{t - 1}"))
                    elif l == 1:
                        pool.wait_ge(dve_drained, at(f"MT{t}_0"))
                    else:
                        pool.wait_ge(acc_full, filled(f"X{t}_{l - 1}"))
                    tt(um(AB, n), um(AT, n), bc(cst[0:n, LEV + l, 0:n], 1, H), ALU.mult).then_inc(
                        a_block_ready, up(a_block_ready, f"ab{t}_{l}"))
                    pool.wait_ge(a_block_ready, now(a_block_ready))
            pool.wait_ge(act_drained, at("read:vtr"))
            for h in range(H):
                if h >= 2:
                    pool.wait_ge(acc_full, filled(f"suS{h - 2}"))
                tt(vmask[h % 2], bc(ur(AB, TS)[:, h, :], 1, NSEQ), bc(cst[0:TS, ONES8, 0:TS:LS], 2, P),
                          ALU.mult).then_inc(v_masked, up(v_masked, f"vm{h}"))
                pool.wait_ge(v_masked, now(v_masked))

            def scatter(layer):
                pool.wait_ge(routed, layer + 1)
                if layer == 0:
                    pool.wait_ge(zeros_stored, 48)
                    for s in over_stored:
                        pool.wait_ge(s, 16)
                for t, c0, n in tiles:
                    pool.wait_ge(act_drained, at(f"read:tm{layer}_{t}"))
                    for k in range(TOP):
                        pool.indirect_dma_start(
                            xs[:, :], bass.IndirectOffsetOnAxis(ap=row_of[0:n, k, t:t + 1], axis=0),
                            htok[t][0:n, :], None).then_inc(scattered, 16)

            def gather(layer):
                for s in ys_stored:
                    pool.wait_ge(s, 16 * (E // 2) * (layer + 1))
                n_over = pool.value_load(over[0:1, 8:9], min_val=0, max_val=NOVER)
                with pool.Fori(0, NOVER) as j:
                    with pool.If(n_over > j):
                        pool.wait_ge(over_stored[layer], j * 16 + 32)
                for t, c0, n in tiles:
                    if t >= 2:
                        pool.wait_ge(combined, at(f"o{layer}_{t - 2}"))
                    for k in range(TOP):
                        pool.indirect_dma_start(
                            got[t % 2][k][0:n, :], None, ys[:, :],
                            bass.IndirectOffsetOnAxis(ap=row_of[0:n, k, t:t + 1], axis=0)).then_inc(
                            gathered[t % 2], up(gathered[t % 2], f"g{layer}_{t}", by=16))

            scatter(0)
            gather(0)
            pool.wait_ge(s5_b_ready, at("bb"))
            for c in range(KD):
                if c:
                    pool.wait_ge(acc_full, filled(f"zi{c - 1}"))
                zv, ev = zview(Z[1]), zview(extra[:, 1, :])
                step(tt(zv, powers(0, 0, 8, c), over_m(BC[:, 1, 4 * c:4 * c + 4, :], 8), ALU.mult))
                step(tt(ev, powers(1, 0, 8, c), over_m(BC[:, 0, 4 * c:4 * c + 4, :], 8), ALU.mult))
                tt(zv, zv, ev, ALU.add).then_inc(zi_ready, up(zi_ready, f"zi{c}"))
                pool.wait_ge(zi_ready, now(zi_ready))
                if c >= 2:
                    pool.wait_ge(acc_full, filled(f"inc{c - 2}"))
                pool.wait_ge(act_drained, at(f"read:u{c}"))
                for j in range(4):
                    ins = pool.tensor_scalar(uM[c % 2][:, j, :], zT[:, c, :], cst[:, MISC, j:j + 1], None, ALU.mult)
                    ins.then_inc(u_masked, up(u_masked, f"um{c}"))
                    pool.wait_ge(u_masked, now(u_masked))
            pool.wait_ge(entry_states_ready, at("sin"))
            for c in range(KD):
                if c:
                    pool.wait_ge(acc_full, filled(f"yc{c - 1}"))
                step(tt(CA[1], powers(0, 0, 9, c), over_m(BC[:, 3, 4 * c:4 * c + 4, :], 9), ALU.mult))
                step(tt(catmp[1], powers(1, 0, 9, c), over_m(BC[:, 2, 4 * c:4 * c + 4, :], 9), ALU.mult))
                tt(CA[1], CA[1], catmp[1], ALU.add).then_inc(ca_im_ready, up(ca_im_ready, f"cai{c}"))
                pool.wait_ge(ca_im_ready, now(ca_im_ready))
            scatter(1)
            gather(1)


def _layouts(x):
    f = lambda n: np.asarray(x[n])
    a = {}
    tokens = np.concatenate([f("x_prompt").reshape(SEQ, D), f("x_sample").reshape(TS, D)], 0)
    a["xT"] = tokens.T.reshape(KD, P, T).transpose(1, 0, 2)
    cc = np.concatenate([f("c_prompt"), f("c_sample")], 0)
    a["cT"] = cc.T.reshape(KD, P, 9).transpose(1, 0, 2)
    a["masks"] = constant_masks()
    col = lambda v: v.reshape(-1, P).T
    a["bmod"] = np.stack([col(f("b_mod_mix")[0]), col(f("b_mod_ffn")[0]), col(f("b_mod_mix")[1]),
                          col(f("b_mod_ffn")[1])], 1)
    a["nrm"] = np.stack([col(f("norm_mix")[0]), col(f("norm_ffn")[0]), col(f("norm_mix")[1]),
                         col(f("norm_ffn")[1]), col(f("norm_final"))], 1)
    for n in ("w_mod_mix", "w_mod_ffn"):
        a[n] = f(n).reshape(2, 2, 4, P, 6, 512).transpose(0, 4, 1, 3, 2, 5).reshape(2, 12, P, UNIT)

    def pairs(w):
        k, m = w.shape
        return w.reshape(k // P, P, m // 256, 2, P).transpose(2, 1, 3, 0, 4).reshape(m // 256, P, UNIT)

    w_in = f("gdn_w_in")[0]
    a["w_in"] = pairs(w_in[:, 0:4 * D])
    a["w_ba"] = w_in[:, 4 * D:].reshape(KD, P, 16).transpose(1, 0, 2)
    a["w_out"] = pairs(f("gdn_w_out")[0])
    a["s5in"] = pairs(f("s5_w_in")[0])
    a["glu"] = f("s5_w_glu")[0].reshape(KD, P, 2, KD, P).transpose(3, 1, 2, 0, 4).reshape(KD, P, UNIT)
    for n, s in (("w1", "moe_w1"), ("w3", "moe_w3")):
        a[n] = f(s).reshape(2, E, KD, P, 2, P).transpose(0, 1, 3, 4, 2, 5).reshape(2, E, P, UNIT)
    a["w2"] = f("moe_w2").reshape(2, E, 2, P, D).transpose(0, 1, 3, 2, 4).reshape(2, E, P, UNIT)
    a["wr"] = np.concatenate([f("moe_w_rg"), f("moe_w_re")], 2).reshape(2, KD, P, 20).transpose(2, 0, 1, 3)
    a["br"] = np.concatenate([f("moe_b_rg"), f("moe_b_re")], 1)
    a["conv"] = f("state_conv")[0].reshape(NSEQ, 3, QKV, P).transpose(3, 2, 0, 1)
    a["cw"] = f("gdn_conv_w")[0].reshape(CW, QKV, P).transpose(2, 1, 0)
    a["a_log"], a["dt_bias"] = f("gdn_a_log")[0], f("gdn_dt_bias")[0]
    a["onrm"] = f("gdn_o_norm")[0].reshape(P, 1)
    a["s0"] = f("state_delta")[0].transpose(1, 2, 0, 3)
    states = lambda v: v.reshape(NPAIR, 2, 64).transpose(1, 2, 0).reshape(P, NPAIR)
    a["lam"] = np.stack([states(f("s5_lam_re")[0]), states(f("s5_lam_im")[0])], 1)
    a["log_dt"] = f("s5_log_dt")[0].reshape(NPAIR, 2).T
    a["s5d"] = f("s5_d")[0].reshape(KD, P).T
    bcs = np.zeros((2, 64, 4, NPAIR, 2, 16), np.float32)
    for k, n in enumerate(("s5_b_re", "s5_b_im", "s5_c_re", "s5_c_im")):
        v = f(n)[0].reshape(NPAIR, 2, *f(n).shape[2:])
        v = v.transpose(1, 2, 0, 3) if k < 2 else v.transpose(1, 3, 0, 2)
        for g in range(2):
            bcs[g, :, k, :, g, :] = v[g]
    a["bc"] = bcs.reshape(P, 4, NPAIR, 32)
    s0 = np.stack([f("state_ssm_re")[0], f("state_ssm_im")[0]], 0).reshape(2, NSEQ, NPAIR, 2, 64)
    a["s0ri"] = s0.transpose(3, 4, 0, 2, 1).reshape(P, 2, NPAIR, NSEQ)
    return {n: np.ascontiguousarray(v) for n, v in a.items()}


_OUTS = {"y": (P, KD, T), "p_delta": (P, H, P), "p_conv": (P, QKV, 3), "s_conv": (P, QKV, NSEQ, 3),
         "s_delta": (H, P, NSEQ, P), "p_ssm": (P, 2, NPAIR), "s_ssm": (P, 2, NPAIR, NSEQ)}


def _build(arrays, bacc, book):
    nc = bacc.Bacc("TRN2", target_bir_lowering=False, num_devices=1)
    d = {n: nc.dram_tensor(f"in_{n}", v.shape, F32, kind="ExternalInput").ap() for n, v in arrays.items()}
    o = {n: nc.dram_tensor(f"out_{n}", s, F32, kind="ExternalOutput").ap() for n, s in _OUTS.items()}
    for n in ("xs", "ys"):
        d[n] = nc.dram_tensor(n, (CHUNKS * P, D), F32).ap()
    trunk(nc, d, o, book)
    return nc


def kernel(**inputs):
    import concourse.bacc as bacc
    from concourse.bass_utils import run_bass_kernel_spmd as run

    arrays = _layouts(inputs)
    book = {}
    _build(arrays, bacc, book)
    nc = _build(arrays, bacc, book)
    r = run(nc, [{f"in_{n}": v for n, v in arrays.items()}], core_ids=[0]).results[0]
    g = {n: r[f"out_{n}"] for n in _OUTS}
    y = g["y"].transpose(2, 1, 0).reshape(T, D)
    states = lambda v: v.reshape(2, 64, NPAIR).transpose(2, 0, 1).reshape(1, 1, 64, 64)
    sstates = lambda v: v.reshape(2, 64, NPAIR, NSEQ).transpose(3, 2, 0, 1).reshape(1, NSEQ, 64, 64)
    c = np.ascontiguousarray
    return (c(y[0:SEQ].reshape(1, SEQ, D)), c(y[SEQ:].reshape(NSEQ, LS, D)),
            c(g["p_delta"].transpose(1, 0, 2).reshape(1, 1, H, P, P)),
            c(g["p_conv"].transpose(2, 1, 0).reshape(1, 1, 3, QKV * P)),
            c(states(g["p_ssm"][:, 0])), c(states(g["p_ssm"][:, 1])),
            c(g["s_delta"].transpose(2, 0, 1, 3).reshape(1, NSEQ, H, P, P)),
            c(g["s_conv"].transpose(2, 3, 1, 0).reshape(1, NSEQ, 3, QKV * P)),
            c(sstates(g["s_ssm"][:, 0])), c(sstates(g["s_ssm"][:, 1])))
```

```python
from contextlib import ExitStack

import numpy as np
import concourse.bass as bass
from concourse import mybir

F32 = mybir.dt.float32
I32 = mybir.dt.int32
ALU = mybir.AluOpType
ACT = mybir.ActivationFunctionType
AX = mybir.AxisListType

P = 128
D = 1024
KD = D // P
SEQ, NSEQ, LS = 512, 8, 8
TS = NSEQ * LS
T = SEQ + TS
HT = T // 2
H = 8
NCK = T // 8
NCP = SEQ // 8
NPAIR = 32
E, NG, EG = 16, 4, 4
TOP = 2
NOVER = (TOP * T) // P - 1
CHUNKS = E + NOVER
EPS = 1e-6
NSLOT = 6
UNIT = 2048
NACC = 4
XT_ACC, H_ACC, Y_ACC = 0, 1, 2
CW = 4
QKV = 24
Q_DVE = 22
NLEV = 7
LATE = [(0, 4), (0, 5)] + [(m, nb) for m in range(1, 4) for nb in range(6)]
N_LATE = len(LATE)
IDENT, TRIU, TRIU8, ONES8, MISC, LEV = 0, 1, 2, 3, 4, 5
N_CONST = LEV + NLEV
MAGIC = 12582912.0
TWO_PI_HI = 6.28125
TWO_PI_LO = 0.0019353071795864769
BIG = 1e30
PI_LIM = 3.1415925
READ_BY_SCALAR = {"ssq", "ada", "l", "p", "X", "wT", "vn", "o", "vtr", "oS", "osum", "u", "zr", "zi", "yc", "gg",
                  "tm", "baq", "rtq"}


def constant_masks():
    j, i = np.meshgrid(np.arange(P), np.arange(P), indexing="ij")
    same = (i // LS) == (j // LS)
    misc = np.where(i < 4, j // 32 == i, np.where(i < 8, 8 - i, 0))
    misc = np.where((i >= 8) & (i < 24), P * (i - 8) - 1, misc)
    misc = np.where((i >= 24) & (i < 40), P * (E - 1) - P * (i - 24), misc)
    misc = np.where((i >= 40) & (i < 48), i - 40, misc)
    misc = np.where((i >= 48) & (i < 57), j % 32 == i - 48, misc)
    misc = np.where(i == 64, 1, misc)
    misc = np.where((i >= 72) & (i < 92), j % 32 == i - 72, misc)
    m = [i == j, i >= j, (i >= j) & same, same, misc]
    for l in range(NLEV):
        b = 1 << l
        m.append((i // (2 * b) == j // (2 * b)) & ((i // b) % 2 == 1) & ((j // b) % 2 == 0))
    return np.ascontiguousarray(np.stack(m, 1).astype(np.float32))


class Counts:

    def __init__(self, book):
        self.book, self.n, self.loop = book, {}, {}

    def up(self, sem, *labels, by=1):
        self.n[id(sem)] = self.n.get(id(sem), 0) + by
        for label in labels:
            if label is not None:
                self.book["at", label] = self.n[id(sem)]
        return by

    def now(self, sem):
        n = self.n.get(id(sem), 0)
        if id(sem) in self.loop:
            i, per, _ = self.loop[id(sem)]
            return i * per + n
        return n

    def enter(self, sem, i, per):
        self.loop[id(sem)] = i, per, self.n.get(id(sem), 0)

    def leave(self, sem, times):
        _, per, base = self.loop.pop(id(sem))
        assert self.n[id(sem)] - base == per
        self.n[id(sem)] = base + times * per


def levels(t):
    return NLEV if t < 4 else 3


def ring_units():
    out = [("mod", 0, u) for u in range(8)]
    for m in range(32):
        if m % 2 == 0:
            out.append(("w_in", 0, m // 2))
        if m < N_LATE:
            out += [("mod", LATE[m][0], 2 * LATE[m][1] + kh) for kh in range(2)]
    out += [("w_out", 0, u) for u in range(4)]
    out += [("moe", 0, u) for u in range(3 * E)]
    out += [("s5in", 0, u) for u in range(4)] + [("glu", 0, u) for u in range(8)]
    out += [("moe", 1, u) for u in range(3 * E)]
    return out



def trunk(nc, d, o, book):
    units = ring_units()
    unit_no = {u: n for n, u in enumerate(units)}
    with ExitStack() as ctx:
        def sb(name, shape):
            return ctx.enter_context(nc.sbuf_tensor(name, shape, F32))

        def sem(name):
            return ctx.enter_context(nc.semaphore(name))

        counts = Counts(book)
        up, now = counts.up, counts.now

        xT = sb("xT", [P, KD, T])
        hT = sb("hT", [P, KD, T])
        yT = sb("yT", [P, KD, T])
        zT = sb("zT", [P, KD, T])
        big = sb("big", [P, QKV * T])
        ring = sb("ring", [P, NSLOT, UNIT])
        modT = sb("modT", [P, 4, 24, 9])
        modA = sb("modA", [P, 4, KD, 9])
        rb = sb("rb", [P, T])
        extra = sb("extra", [P, 2, 1024])
        cst = sb("cst", [P, N_CONST, P])
        small = sb("small", [P, 4])
        ones = sb("ones", [P, P])
        cT = sb("cT", [P, KD, 9])
        bmod = sb("bmod", [P, 4, 24])
        nrm = sb("nrm", [P, 5, KD])
        w_ba = sb("w_ba", [P, KD, 16])
        hp = sb("hp", [P, 2, H])
        onrm = sb("onrm", [P, 1])
        lam = sb("lam", [P, 3, NPAIR])
        pw = sb("pw", [P, 2, 9, NPAIR])
        fz = sb("fz", [P, 2, NPAIR])
        s5t = sb("s5t", [P, 8, NPAIR])
        s5d = sb("s5d", [P, KD])
        wr = sb("wr", [P, 2, KD, 20])
        br = sb("br", [P, 2, 20])
        gt = sb("gt", [P, 10, 5, H])
        row_of = ctx.enter_context(nc.sbuf_tensor("row_of", [P, TOP, 5], I32))
        over = ctx.enter_context(nc.sbuf_tensor("over", [P, 9], I32))
        S = sb("S", [P, H, P])
        acc = ctx.enter_context(nc.psum_tensor("acc", [P, NACC, 2, 512], F32))

        hflat = hT[:, :, :].rearrange("p k t -> p (k t)")
        yflat = yT[:, :, :].rearrange("p k t -> p (k t)")
        m_sb = [big[:, 512 * nb:512 * nb + 512] for nb in range(4)] + [rb[:, 0:512]]
        c32 = zT[:, :, :].rearrange("p k t -> p (k t)")[:, 0:KD * 32].rearrange("p (k c) -> p k c", c=32)
        qkv = big[:, :].rearrange("p (m t) -> p m t", t=T)
        unit = [hflat[:, 1024 * i:1024 * (i + 1)] for i in range(4)]
        unit += [ring[:, s, 1024 * j:1024 * (j + 1)] for s in (2, 3) for j in range(2)]
        unit += [extra[:, j, :] for j in range(2)]
        EG, EX, AT, AB, M, MT, KBGT, KDECT, VB, QKE, VN = range(11)
        spare = [ring[:, s, 1024 * j:1024 * (j + 1)] for s in (0, 1, 4, 5) for j in range(2)]
        odd = {k: spare[i] for i, k in enumerate((EG, EX, AT, KBGT, KDECT, VB, QKE))}
        raw = [yflat[:, 640 * i:640 * i + T + 3] for i in range(2)]
        sraw = [yflat[:, 1280 + 88 * i:1280 + 88 * (i + 1)].rearrange("p (b s) -> p b s", s=11) for i in range(2)]
        sq = [yflat[:, 1536 + T * i:1536 + T * (i + 1)] for i in range(2)]
        ln = [yflat[:, 2688 + T * i:2688 + T * (i + 1)] for i in range(2)]
        cs_in = extra[:, 0, 0:QKV * 24].rearrange("p (m b s) -> p m b s", b=NSEQ, s=3)
        cs_out = extra[:, 1, 0:QKV * 24].rearrange("p (m b s) -> p m b s", b=NSEQ, s=3)
        cp_out = extra[:, 1, 600:600 + QKV * 3].rearrange("p (m s) -> p m s", s=3)
        cw = extra[:, 1, 700:700 + QKV * CW].rearrange("p (m s) -> p m s", s=CW)
        BA, BB, BETA, GG, G1, G2, GCOL, GLAST, CKBG, CKDEC = range(10)
        s0v = [qkv[:, 8 * (h // 4):8 * (h // 4) + 8, P * (h % 4):P * (h % 4) + P] for h in range(H)]
        snew = [qkv[:, 16:24, P * i:P * i + P] for i in range(2)]
        vmask = [qkv[0:TS, 16:24, 256 + P * i:256 + P * i + P] for i in range(2)]
        head_rows = extra[0:H, 0, :].rearrange("p (h n) -> p h n", n=P)
        half = 2 * NPAIR * NCK
        INC = big[:, 0:half].rearrange("p (r q c) -> p r q c", r=2, q=NPAIR)
        SIN = big[:, half:2 * half].rearrange("p (r q c) -> p r q c", r=2, q=NPAIR)
        Z = [big[:, half + 1024 * i:half + 1024 * (i + 1)] for i in range(2)]
        ZT = big[:, half + 2048:half + 4096].rearrange("p (r m n) -> p r m n", r=2, m=8)
        uM = [big[:, 2 * half + 4 * T * i:2 * half + 4 * T * (i + 1)].rearrange("p (j t) -> p j t", j=4)
              for i in range(2)]
        CA = [[big[:, a0 + 1152 * i:a0 + 1152 * (i + 1)].rearrange("p (m q c) -> p m q c", m=9, q=4)
               for i in range(2)] for a0 in (2 * half, 2304)]
        eflat = extra[:, :, :].rearrange("p i n -> p (i n)")
        KB = [v.rearrange("p (m n) -> p m n", m=8) for v in (big[:, 2 * half + 2304:2 * half + 3328], eflat[:, 0:1024])]
        YS = [v[0:NCK].rearrange("p (t n) -> p t n", t=8)
              for v in (big[:, 2 * half + 3328:2 * half + 4352], eflat[:, 1024:2048])]
        catmp = [v.rearrange("p (m q c) -> p m q c", m=9, q=4)
                 for v in (big[:, 0:1152], big[:, 1152:2304], eflat[:, 0:1152])]
        BC = yflat[:, 0:4096].rearrange("p (k q c) -> p k q c", k=4, q=NPAIR)
        s0ri = yflat[:, 4096:4608].rearrange("p (r q b) -> p r q b", r=2, q=NPAIR)
        sflat = S[:, :, :].rearrange("p h n -> p (h n)")
        fin_p = sflat[:, 0:64].rearrange("p (r q) -> p r q", r=2)
        fin_s = sflat[:, 64:576].rearrange("p (r q b) -> p r q b", r=2, q=NPAIR)
        POW8 = sflat[:, 64:576].rearrange("p (r q j) -> p r q j", r=2, j=8)
        BLK = hflat[:, 0:640].rearrange("p (b r q) -> p b r q", r=2, q=NPAIR)
        sc1, sc2 = (hflat[:, 1024 + 512 * i:1536 + 512 * i].rearrange("p (r q b) -> p r q b", r=2, b=8) for i in range(2))
        st1, st2 = (hflat[:, 640 + 64 * i:704 + 64 * i].rearrange("p (r q) -> p r q", r=2) for i in range(2))
        sc4 = hflat[:, 2048:4096].rearrange("p (q b j) -> p q b j", q=NPAIR, j=8)
        sc5 = extra[:, :, :].rearrange("p i n -> p (i n)")[:, 1152:1152 + 64 * (NPAIR - Q_DVE)].rearrange(
            "p (q b j) -> p q b j", q=NPAIR - Q_DVE, j=8)
        a64 = sflat[:, 768:896].rearrange("p (k q) -> p k q", k=4)
        aim = sflat[:, 704:768].rearrange("p (r q) -> p r q", r=2)
        htok = [big[:, D * t:D * (t + 1)] for t in range(5)]
        got = [[big[:, D * i:D * (i + 1)] for i in pair] for pair in ((0, 1), (2, 3), (4, 5), (6, 7), (8, 12))]
        otok = [big[:, D * (9 + i):D * (10 + i)] for i in range(2)]
        xtmp = big[:, D * 11:D * 12]
        xc = [yflat[:, D * i:D * (i + 1)] for i in range(2)]
        yc = [yflat[:, D * (2 + i):D * (3 + i)] for i in range(2)]
        zflat = zT[:, :, :].rearrange("p k t -> p (k t)")
        xcT = [zflat[:, D * i:D * (i + 1)].rearrange("p (k n) -> p k n", n=P) for i in range(2)]
        hid = [zflat[:, 2 * D + 2 * P * i:2 * D + 2 * P * (i + 1)] for i in range(2)]
        s1 = [zflat[:, 2 * D + 2 * P * (2 + i):2 * D + 2 * P * (3 + i)] for i in range(2)]
        rt = extra[:, 0, :]
        rt_rows, ba_rows = extra[:, 0, 424:424 + T], sq[0]
        rx = extra[:, 1, :]

        xs, ys = d["xs"], d["ys"]
        xs_chunks, ys_chunks = (v.rearrange("(c p) n -> c p n", p=P) for v in (xs, ys))

        acc_full = sem("acc_full")
        dve_drained = sem("dve_drained")
        act_drained = sem("act_drained")
        slot_loaded = [sem(f"slot{i}_loaded") for i in range(NSLOT)]
        consts_in, x_in, conv_in, s0_in, bc_in = (sem(n) for n in ("consts_in", "x_in", "conv_in", "s0_in", "bc_in"))
        snew_out = [sem("snew_out0"), sem("snew_out1")]
        stored, conv_stored = sem("stored"), sem("conv_stored")
        first_inverse_ready = sem("first_inverse_ready")
        pe_half, act_half, dve_half = sem("pe_half"), sem("act_half"), sem("dve_half")
        dve_order, act_order, pool_order = sem("dve_order"), sem("act_order"), sem("pool_order")
        zero_ready, zeros_stored = sem("zero_ready"), sem("zeros_stored")
        one_hots_ready = sem("one_hots_ready")
        routed = sem("routed")
        scattered = sem("scattered")
        xc_loaded = [sem("xc_loaded0"), sem("xc_loaded1")]
        xt_full, xt_out = sem("xt_full"), sem("xt_out")
        h_full, s1_ready, hid_ready = sem("h_full"), sem("s1_ready"), sem("hid_ready")
        y_full, yc_ready = sem("y_full"), sem("yc_ready")
        ys_stored = [sem("ys_stored0"), sem("ys_stored1")]
        gathered = [sem(f"gathered{t}") for t in range(5)]
        weighted, combined = sem("weighted"), sem("combined")
        over_loaded = [[sem(f"over_loaded{p}{l}") for l in range(2)] for p in range(2)]
        (over_xt_full, over_xt_out, over_h_full, over_s1_ready, over_hid_ready, over_y_full,
         over_yc_ready, over_stored) = (
            [sem(f"over_{n}{l}") for l in range(2)] for n in (
                "xt_full", "xt_out", "h_full", "s1_ready", "hid_ready", "y_full", "yc_ready", "stored"))
        s5_angle_ready = sem("s5_angle_ready")
        gate_args_ready = sem("gate_args_ready")
        s5_b_ready = sem("s5_b_ready")
        ca_re_ready = sem("ca_re_ready")
        conv_done = sem("conv_done")
        decay_diff_ready = sem("decay_diff_ready")
        log_decay_ready = sem("log_decay_ready")
        g_ready = sem("g_ready")
        sample_input_ready = sem("sample_input_ready")
        l2_done = sem("l2_done")
        mod_ready = sem("mod_ready")
        x_scaled = sem("x_scaled")
        o_normed = sem("o_normed")
        o_root_ready = sem("o_root_ready")
        out_ready = sem("out_ready")
        q_decayed = sem("q_decayed")
        expert_diff_ready = sem("expert_diff_ready")
        group_diff_ready = sem("group_diff_ready")
        row_masks_ready = sem("row_masks_ready")
        s5_fin_ready = sem("s5_fin_ready")
        entry_states_ready = sem("entry_states_ready")
        blocks_ready, chunks_completed = sem("blocks_ready"), sem("chunks_completed")
        b_im_negated = sem("b_im_negated")
        x_ready = sem("x_ready")
        zr_ready = sem("zr_ready")
        qkv_silu_done = sem("qkv_silu_done")
        dt_ready = sem("dt_ready")
        decay_rows_ready = sem("decay_rows_ready")
        decay_cols_ready = sem("decay_cols_ready")
        decay_exp_ready = sem("decay_exp_ready")
        gelu_done = sem("gelu_done")
        prompt_input_ready = sem("prompt_input_ready")
        l2_squares_ready = sem("l2_squares_ready")
        squares_ready = sem("squares_ready")
        o_squares_ready = sem("o_squares_ready")
        expert_exp_ready = sem("expert_exp_ready")
        group_exp_ready = sem("group_exp_ready")
        silu_c_ready = sem("silu_c_ready")
        softplus_ready = sem("softplus_ready")
        trig_ready = sem("trig_ready")
        a_block_ready = sem("a_block_ready")
        ca_im_ready = sem("ca_im_ready")
        head_rows_ready = sem("head_rows_ready")
        first_ca_ready = sem("first_ca_ready")
        history_ready = sem("history_ready")
        ones_ready = sem("ones_ready")
        u_masked = sem("u_masked")
        v_masked = sem("v_masked")
        zi_ready = sem("zi_ready")

        def at(label):
            return book.get(("at", label), 1)

        def reader(name):
            stem = name[:min(name.find(c) for c in name if c.isdigit())] if any(c.isdigit() for c in name) else name
            return act_drained if stem in READ_BY_SCALAR else dve_drained

        def filled(name):
            return use(name) + 1

        def use(name):
            return book.get(("use", name), 0)

        def buf(name):
            return acc[:, use(name) % NACC, :, :]

        def flatbuf(name, n, w):
            return buf(name).rearrange("p b c -> p (b c)")[:, 0:n * w].rearrange("p (n w) -> p n w", w=w)

        def tok(name):
            return buf(name)[:, :, 0:HT]

        def halves(ap):
            return ap.rearrange("p (b t) -> p b t", b=2)

        def bc(ap, axis, n):
            x = ap.unsqueeze(axis)
            return x.broadcast_to([n if i == axis else s for i, s in enumerate(x.shape)])

        def of_tile(k, t):
            if k == VN:
                return unit[AB] if t == 4 else spare[7]
            return odd[k] if t % 2 and k in odd else unit[k]

        def um(k, t, n, rows=None):
            rows = n if rows is None else rows
            return of_tile(k, t)[0:rows, 0:H * n].rearrange("p (h n) -> p h n", n=n)

        def ur(k, t, n):
            return of_tile(k, t)[0:n, 0:H * P].rearrange("p (h n) -> p h n", n=P)

        def both(ap):
            return ap.rearrange("p (h x n) -> p h x n", x=2, n=TS)

        def both_halves():
            return of_tile(EX, 4).rearrange("p (x h n) -> p h x n", x=2, n=TS)

        def four(b):
            return slice(4 * b, 4 * b + 4)

        def bank(name, b, n):
            return buf(name)[0:n, b, 0:4 * n].rearrange("p (h n) -> p h n", n=n)

        tiles = [(t, P * t, P if t < 4 else TS) for t in range(5)]
        tri = lambda t: TRIU if t < 4 else TRIU8
        block = ctx.enter_context(nc.Block())

        rtv = {"L": rt[:, 0:100].rearrange("p (t c) -> p t c", t=5),
               "ge": rt[:, 100:120].rearrange("p (t c) -> p t c", t=5),
               "ohg": rt[:, 120:140].rearrange("p (t c) -> p t c", t=5),
               "t4": rt[:, 140:160].rearrange("p (t c) -> p t c", t=5),
               "t16": rt[:, 160:240].rearrange("p (t g e) -> p t g e", t=5, g=4),
               "sel": rt[:, 240:260].rearrange("p (t c) -> p t c", t=5),
               "oh1": rt[:, 260:280].rearrange("p (t c) -> p t c", t=5),
               "oh2": rt[:, 280:300].rearrange("p (t c) -> p t c", t=5),
               "gm": rt[:, 300:305], "pg": rt[:, 305:310], "m1": rt[:, 310:315], "m2": rt[:, 315:320],
               "e2": rt[:, 320:325], "w1": rt[:, 325:330], "w2": rt[:, 330:335], "tm": rt[:, 335:340],
               "rank": rx[:, 240:320].rearrange("p (t e) -> p t e", t=5),
               "pos": rx[:, 320:400].rearrange("p (t e) -> p t e", t=5),
               "po": rx[:, 400:480].rearrange("p (t e) -> p t e", t=5),
               "tot": rx[:, 480:496], "chunks": rx[:, 496:512], "cum": rx[:, 512:528], "far": rx[:, 528:544],
               "le": rx[:, 544:672].rearrange("p (j e) -> p j e", e=E), "over": rx[:, 672:681],
               "row": rx[:, 681:691].rearrange("p (k t) -> p k t", k=TOP), "one": rx[:, 691:707]}
        choice = [rx[:, 80 * i:80 * (i + 1)].rearrange("p (t g e) -> p t g e", t=5, g=4) for i in range(3)]
        chosen = [rx[:, 80 * i:80 * (i + 1)].rearrange("p (t e) -> p t e", t=5) for i in range(3)]

        def zview(ap):
            return ap.rearrange("p (m q c) -> p m q c", m=8, q=4)

        def powers(r, m0, m1, c):
            return bc(pw[:, r, m0:m1, 4 * c:4 * c + 4], 3, 32)

        def over_m(ap, n):
            return bc(ap, 1, n)

        def unit_source(kind, a, u):
            if kind == "mod":
                return d["w_mod_mix" if a % 2 == 0 else "w_mod_ffn"][a // 2, u]
            if kind == "moe":
                return d[("w1", "w3", "w2")[u % 3]][a, u // 3]
            return d[kind][u]

        @block.sync
        def _(sp):
            def consts(dst, src):
                sp.dma_start(dst, src).then_inc(consts_in, up(consts_in, by=16))

            sp.dma_start(xT[:, :, :], d["xT"]).then_inc(x_in, 16)
            consts(cT[:, :, :], d["cT"])
            for dst, src in ((cst[:, :, :], "masks"), (bmod[:, :, :], "bmod"), (nrm[:, :, :], "nrm"),
                             (w_ba[:, :, :], "w_ba"), (onrm[:, :], "onrm"), (s5d[:, :], "s5d"),
                             (wr[:, :, :, :], "wr")):
                consts(dst, d[src])
            for i, src in enumerate(("a_log", "dt_bias")):
                consts(hp[:, i, :], d[src].partition_broadcast(P))
            for l in range(2):
                consts(br[:, l, :], d["br"][l].partition_broadcast(P))
            consts(lam[:, 0:2, :], d["lam"])
            for g in range(2):
                consts(lam[64 * g:64 * g + 64, 2, :], d["log_dt"][g].partition_broadcast(64))
            book["consts"] = now(consts_in)

            def load(n):
                if n >= NSLOT:
                    sp.wait_ge(acc_full, book.get(("unit_read", n - NSLOT), 1))
                loaded = slot_loaded[n % NSLOT]
                sp.dma_start(ring[:, n % NSLOT, :], unit_source(*units[n])).then_inc(
                    loaded, up(loaded, ("unit", n), by=16))

            def moe_loads(layer):
                first = unit_no["moe", layer, 0]
                done = E * layer
                for j in range(6):
                    load(first + j)
                sp.wait_ge(scattered, 16 * TOP * 5 * (layer + 1))
                for j in range(2):
                    sp.dma_start(xc[j], xs_chunks[j]).then_inc(xc_loaded[j], 16)
                for s in slot_loaded:
                    counts.enter(s, None, 16)

                def turn(i, last=False):
                    for j in range(2):
                        slots = [(first + 3 * j + x) % NSLOT for x in range(3)]
                        if not last:
                            sp.wait_ge(xt_full, i * 2 + (done + j + 1))
                            sp.dma_start(xc[j], xs_chunks[i * 2 + (2 + j)]).then_inc(xc_loaded[j], 16)
                            sp.wait_ge(h_full, i * 2 + (done + j + 1))
                            sp.dma_start(ring[:, slots[0], :], d["w1"][layer][i * 2 + (2 + j)]).then_inc(
                                slot_loaded[slots[0]], up(slot_loaded[slots[0]], by=16))
                            sp.dma_start(ring[:, slots[1], :], d["w3"][layer][i * 2 + (2 + j)]).then_inc(
                                slot_loaded[slots[1]], up(slot_loaded[slots[1]], by=16))
                            sp.wait_ge(y_full, i * 2 + (done + j + 1))
                            sp.dma_start(ring[:, slots[2], :], d["w2"][layer][i * 2 + (2 + j)]).then_inc(
                                slot_loaded[slots[2]], up(slot_loaded[slots[2]], by=16))
                        sp.wait_ge(yc_ready, i * 2 + (done + j + 1))
                        sp.dma_start(ys_chunks[i * 2 + j], yc[j]).then_inc(ys_stored[j], 16)
                        if last:
                            overflow_load(j, j)

                def overflow_load(j, p, again=False):
                    with sp.If(n_over > j):
                        if again:
                            sp.wait_ge(over_y_full[layer], j - 1)
                        e = sp.value_load(over[0:1, bass.ds(j, 1)], min_val=0, max_val=E - 1)
                        for x, w in enumerate(("w1", "w3", "w2")):
                            sp.dma_start(ring[:, (first + 3 * p + x) % NSLOT, :].unsqueeze(1),
                                         d[w][layer][bass.ds(e, 1)].rearrange("e p n -> p e n")).then_inc(
                                over_loaded[p][layer], 16)
                        sp.dma_start(xc[p], xs_chunks[j + E]).then_inc(over_loaded[p][layer], 16)

                sp.wait_ge(routed, layer + 1)
                n_over = sp.value_load(over[0:1, 8:9], min_val=0, max_val=NOVER)
                with sp.Fori(0, E // 2 - 1) as i:
                    turn(i)
                for s in slot_loaded:
                    counts.leave(s, E // 2 - 1)
                turn(E // 2 - 1, last=True)
                with sp.Fori(1, NOVER // 2) as i:
                    for p in range(2):
                        overflow_load(i * 2 + p, p, again=True)
                sp.wait_ge(combined, at(f"o{layer}_3"))

            for n in range(unit_no["w_in", 0, 0]):
                load(n)
            sp.dma_start(cs_in, d["conv"]).then_inc(conv_in, up(conv_in, by=16))
            sp.dma_start(cw, d["cw"]).then_inc(conv_in, up(conv_in, by=16))
            for n in range(unit_no["w_in", 0, 0], unit_no["w_out", 0, 0]):
                load(n)
            sp.wait_ge(zero_ready, 1)
            zero = S[:, :, :].rearrange("p h n -> p (h n)").unsqueeze(1).broadcast_to([P, CHUNKS // 3, D])
            for c in range(3):
                rows = xs.rearrange("(c p) n -> p c n", p=P)[:, CHUNKS // 3 * c:CHUNKS // 3 * (c + 1), :]
                sp.dma_start(rows, zero).then_inc(zeros_stored, up(zeros_stored, by=16))
            for l in range(2):
                rows = ys.rearrange("(c p) n -> p c n", p=P)[:, E + NOVER // 2 * l:E + NOVER // 2 * (l + 1), :]
                sp.dma_start(rows, zero[:, 0:NOVER // 2, :]).then_inc(zeros_stored, up(zeros_stored, by=16))
            sp.wait_ge(history_ready, at(f"cs{QKV - 1}"))
            sp.dma_start(o["s_conv"], cs_out).then_inc(conv_stored, up(conv_stored, by=16))
            sp.dma_start(o["p_conv"], cp_out).then_inc(conv_stored, up(conv_stored, by=16))
            sp.wait_ge(acc_full, filled("o3"))
            for h in range(H):
                sp.dma_start(s0v[h], d["s0"][h]).then_inc(s0_in, up(s0_in, by=16))
            sp.wait_ge(dve_drained, at("S3"))
            sp.dma_start(o["p_delta"], S[:, :, :]).then_inc(stored, up(stored, by=16))
            for n in range(unit_no["w_out", 0, 0], unit_no["moe", 0, 0]):
                load(n)
            for h in range(H):
                sp.wait_ge(dve_drained, at(f"snew{h}"))
                sp.dma_start(o["s_delta"][h], snew[h % 2]).then_inc(snew_out[h % 2], up(snew_out[h % 2], by=16))
            sp.wait_ge(acc_full, filled("suS7"))
            moe_loads(0)
            for n in range(unit_no["s5in", 0, 0], unit_no["glu", 0, 0]):
                load(n)
            sp.wait_ge(prompt_input_ready, at("h2"))
            sp.wait_ge(sample_input_ready, at("hs2"))
            sp.dma_start(BC, d["bc"]).then_inc(bc_in, up(bc_in, by=16))
            sp.dma_start(s0ri, d["s0ri"]).then_inc(bc_in, up(bc_in, by=16))
            for n in range(unit_no["glu", 0, 0], unit_no["moe", 1, 0]):
                load(n)
            sp.wait_ge(s5_fin_ready, at("s5fin"))
            sp.dma_start(o["p_ssm"], fin_p).then_inc(stored, up(stored, by=16))
            sp.dma_start(o["s_ssm"], fin_s).then_inc(stored, up(stored, by=16))
            moe_loads(1)
            for k in range(0, KD, 2):
                sp.wait_ge(out_ready, at(f"out{k + 1}"))
                sp.dma_start(o["y"][:, k:k + 2, :], yT[:, k:k + 2, :]).then_inc(stored, up(stored, by=16))
            sp.wait_ge(stored, now(stored))
            sp.wait_ge(conv_stored, now(conv_stored))
            for s in snew_out:
                sp.wait_ge(s, now(s))

        @block.tensor
        def _(pe):
            state = {"n": 0}

            def begin(name):
                n = state["n"]
                book["use", name] = n
                book["name", n] = name
                if n >= NACC:
                    last = book["name", n - NACC]
                    pe.wait_ge(reader(last), at("read:" + last))
                state["n"] += 1
                return acc[:, n % NACC, :, :]

            def weights(n):
                pe.wait_ge(slot_loaded[n % NSLOT], at(("unit", n)))
                return ring[:, n % NSLOT, :]

            def project(name, w, rhs):
                ps = begin(name)
                for b in range(2):
                    for k in range(KD):
                        mm = pe.matmul(ps[:, b, 0:HT], w[:, k, :], rhs[:, k, HT * b:HT * b + HT],
                                       start=(k == 0), stop=(k == KD - 1))
                mm.then_inc(acc_full, 1)

            def norm_sums(i):
                ps = begin(f"ssq{i}")
                if i % 2 or i == 0:
                    src = yT if i == 0 else zT
                    for k in range(KD):
                        pe.wait_ge(squares_ready, at(f"nsq{i}_{k if i else 0}"))
                        for b in range(2):
                            mm = pe.matmul(ps[:, b, 0:HT], ones[:, :], src[:, k, HT * b:HT * b + HT],
                                           start=(k == 0), stop=(k == KD - 1))
                else:
                    for t, c0, n in tiles:
                        pe.wait_ge(squares_ready, at(f"nsq{i}_{t}"))
                        for b in range(2):
                            lo, hi = max(c0, HT * b), min(c0 + n, HT * b + HT)
                            for k in range(KD if lo < hi else 0):
                                mm = pe.matmul(ps[:, b, lo - HT * b:hi - HT * b], ones[:, :], zT[:, k, lo:hi],
                                               start=(k == 0), stop=(k == KD - 1), skip_group_check=True)
                mm.then_inc(acc_full, 1)

            def await_input(i):
                pe.wait_ge(prompt_input_ready, at(f"h{i}"))
                pe.wait_ge(sample_input_ready, at(f"hs{i}"))

            def heads(name, lhsT, rhs, out=None):
                begin(name)
                for h in range(H):
                    mm = pe.matmul(out[:, h, :], lhsT(h), rhs(h), start=True, stop=True, skip_group_check=True)
                mm.then_inc(acc_full, 1)

            def adaln(m, nb):
                ps = begin(f"ada{m}_{nb}")
                for kh in range(2):
                    n = unit_no["mod", m, 2 * nb + kh]
                    w = weights(n).rearrange("p (k c) -> p k c", k=4)
                    for k in range(4):
                        mm = pe.matmul(ps[32 * k:32 * k + 32, 0, :], c32[:, 4 * kh + k, :], w[:, k, :],
                                       start=(kh == 0), stop=(kh == 1), skip_group_check=True)
                    book["unit_read", n] = state["n"]
                mm.then_inc(acc_full, 1)

            def adaln_turn(m, nb):
                pe.wait_ge(act_drained, at(f"read:ada{m}_{nb}"))
                out = flatbuf(f"adaT{m}_{nb}", 4, 9)
                begin(f"adaT{m}_{nb}")
                src = m_sb[4 if (m, nb) in LATE else nb]
                for j in range(4):
                    mm = pe.matmul(out[:, j, :], src[:, P * j:P * j + P], cst[:, MISC, 48:57],
                                   start=True, stop=True, skip_group_check=True)
                mm.then_inc(acc_full, 1)

            def prepare(t, step_):
                _, c0, n = tiles[t]
                k_ = lambda h: qkv[:, 8 + h, c0:c0 + n]
                q_ = lambda h: qkv[:, h, c0:c0 + n]
                v_ = lambda h: qkv[:, 16 + h, c0:c0 + n]
                if step_ < 2:
                    name, u, ready = ((f"gr{t}", AT, f"ru{t}"), (f"br{t}", QKE, f"rub{t}"))[step_]
                    pe.wait_ge(row_masks_ready, at(ready))
                    ps = begin(name)
                    w = min(512, H * n)
                    for b in range(H * n // w):
                        mm = pe.matmul(ps[:, b, 0:w], ones[0:n, :], of_tile(u, t)[0:n, w * b:w * b + w],
                                       start=True, stop=True)
                    mm.then_inc(acc_full, 1)
                elif step_ == 2:
                    heads(f"kk{t}", k_, k_, flatbuf(f"kk{t}", H, n)[0:n])
                elif step_ == 3:
                    heads(f"qk{t}", k_, q_, flatbuf(f"qk{t}", H, n)[0:n])
                else:
                    name, src = ((f"kt{t}", k_), (f"vt{t}", v_))[step_ - 4]
                    begin(name)
                    out = flatbuf(name, H, P)[0:n]
                    for h in range(H):
                        mm = pe.transpose(out[:, h, :], src(h), cst[:, IDENT, :])
                    mm.then_inc(acc_full, 1)

            def half_heads(name, b, n, lhsT, rhs):
                out = bank(name, b, n)
                for h in range(4):
                    mm = pe.matmul(out[:, h, :], lhsT[:, 4 * b + h, :], rhs[:, 4 * b + h, :], start=True, stop=True,
                                   skip_group_check=True)
                if b == 0:
                    mm.then_inc(pe_half, up(pe_half, f"half:{name}"))
                else:
                    mm.then_inc(acc_full, 1)

            def first_block(t):
                n = tiles[t][2]
                pe.wait_ge(a_block_ready, at(f"ab{t}_0"))
                begin(f"A0{t}")
                out = flatbuf(f"A0{t}", H, n)[0:n]
                for h in range(H):
                    mm = pe.transpose(out[:, h, :], um(AB, t, n)[:, h, :], cst[0:n, IDENT, 0:n])
                mm.then_inc(acc_full, 1)

            def delta_tile(t, c0, n):
                q_ = lambda h: qkv[:, h, c0:c0 + n]
                m_, mt, ab, x = um(M, t, n), um(MT, t, n), um(AB, t, n), um(EX, t, n)
                for l in range(1, levels(t)):
                    x_name, m_name, mt_name = f"X{t}_{l}", f"MX{t}_{l}", f"MTX{t}_{l}"
                    pe.wait_ge(a_block_ready, at(f"ab{t}_{l}"))
                    begin(x_name)
                    for b in range(2):
                        if l == 1:
                            pe.wait_ge(first_inverse_ready, at(f"MT{t}_0"))
                        elif b == 0:
                            pe.wait_ge(dve_half, at(f"read half:MX{t}_{l - 1}"))
                        else:
                            pe.wait_ge(dve_drained, at(f"read:MX{t}_{l - 1}"))
                        half_heads(x_name, b, n, ab, m_)
                    if t < 4:
                        prepare(t + 1, l - 1)
                    if l < levels(t) - 1:
                        begin(m_name)
                    begin(mt_name)
                    for b in range(2):
                        if b == 0:
                            pe.wait_ge(act_half, at(f"read half:{x_name}"))
                        else:
                            pe.wait_ge(act_drained, at(f"read:{x_name}"))
                        if l > 1 and b == 0:
                            pe.wait_ge(dve_half, at(f"read half:MTX{t}_{l - 1}"))
                        elif l > 1:
                            pe.wait_ge(dve_drained, at(f"read:MTX{t}_{l - 1}"))
                        if l < levels(t) - 1:
                            half_heads(m_name, b, n, mt, x)
                        half_heads(mt_name, b, n, x, mt)
                pe.wait_ge(dve_half, at(f"read half:MTX{t}_{levels(t) - 1}"))
                pe.wait_ge(dve_drained, at(f"MT{t}_{levels(t) - 1}"))
                pe.wait_ge(dve_drained, at(f"read:kt{t}"))
                pe.wait_ge(dve_drained, at(f"read:vt{t}"))
                heads(f"wT{t}", lambda h: ur(KBGT, t, n)[:, h, :], lambda h: um(MT, t, n)[:, h, :],
                      flatbuf(f"wT{t}", H, n))
                if t < 4:
                    first_block(t + 1)
                pe.wait_ge(act_drained, at(f"read:wT{t}"))
                if t < 4:
                    if t:
                        pe.wait_ge(dve_drained, at(f"S{t - 1}"))
                    begin(f"vn{t}")
                    out = flatbuf(f"vn{t}", H, P)
                    for h in range(H):
                        pe.matmul(out[:, h, :], um(MT, t, n)[:, h, :], ur(VB, t, n)[:, h, :], start=True, stop=False,
                                  skip_group_check=True)
                        mm = pe.matmul(out[:, h, :], um(EX, t, n, P)[:, h, :], S[:, h, :], start=False, stop=True,
                                       skip_group_check=True)
                    mm.then_inc(acc_full, 1)
                    pe.wait_ge(act_drained, at(f"read:vn{t}"))
                    pe.wait_ge(q_decayed, at(f"qdT{t}"))
                    begin(f"o{t}")
                    out = flatbuf(f"o{t}", H, n)
                    for h in range(H):
                        pe.matmul(out[:, h, :], S[:, h, :], q_(h), start=True, stop=False, skip_group_check=True)
                        mm = pe.matmul(out[:, h, :], ur(VN, t, n)[:, h, :], um(QKE, t, n)[:, h, :], start=False,
                                       stop=True, skip_group_check=True)
                    mm.then_inc(acc_full, 1)
                    heads(f"su{t}", lambda h: ur(KDECT, t, n)[:, h, :], lambda h: ur(VN, t, n)[:, h, :],
                          flatbuf(f"su{t}", H, P))
                    return
                pe.wait_ge(s0_in, 16 * H)
                pe.wait_ge(q_decayed, at("q4"))
                begin("vtr")
                begin("oS")
                out = both(buf("oS").rearrange("p b c -> p (b c)"))
                wq = both_halves()
                for h in range(H):
                    for b in range(NSEQ):
                        pe.matmul(out[:, h, :, LS * b:LS * b + LS], s0v[h][:, b, :], wq[:, h, :, LS * b:LS * b + LS],
                                  start=(h % 4 == 0 and b == 0), stop=False, skip_group_check=True)
                for h in range(H):
                    mm = pe.matmul(out[:, h, 0, :], ur(VB, t, n)[:, h, :], um(MT, t, n)[:, h, :], start=False,
                                   stop=True, skip_group_check=True)
                mm.then_inc(pe_half, up(pe_half, "half:oS"))
                pe.wait_ge(act_half, at("read half:oS"))
                vtr = flatbuf("vtr", H, P)[0:n]
                for h in range(H):
                    mm = pe.transpose(vtr[:, h, :], um(M, t, n, P)[:, h, :], cst[:, IDENT, :])
                mm.then_inc(acc_full, 1)
                pe.wait_ge(act_drained, at("read:vtr"))
                for h in range(H):
                    mm = pe.matmul(out[:, h, 1, :], ur(VN, t, n)[:, h, :], um(QKE, t, n)[:, h, :], start=False,
                                   stop=True, skip_group_check=True)
                mm.then_inc(acc_full, 1)
                for h in range(H):
                    pe.wait_ge(v_masked, at(f"vm{h}"))
                    ps = begin(f"suS{h}")
                    for b in range(2):
                        mm = pe.matmul(ps[:, b, :], ur(KDECT, t, n)[:, h, :], vmask[h % 2][:, 4 * b:4 * b + 4, :],
                                       start=True, stop=True)
                    mm.then_inc(acc_full, 1)

            def narrow(name, w, width):
                ps = begin(name)
                for b in range(2):
                    for k in range(KD):
                        cols = 32 if k < KD - 1 else width
                        mm = pe.matmul(ps[32 * (k % 4):32 * (k % 4) + cols, b, 0:HT], w[:, width * k:width * k + cols],
                                       hT[:, k, HT * b:HT * b + HT], start=(k < 4), stop=(k >= 4),
                                       skip_group_check=True)
                mm.then_inc(acc_full, 1)

            def narrow_turn(name, src, width):
                pe.wait_ge(act_drained, at(f"read:{name[:2]}q{name[2:]}"))
                ps = begin(name)
                for t, c0, n in tiles:
                    mm = pe.matmul(ps[0:n, 0, width * t:width * t + width], src[:, c0:c0 + n],
                                   cst[:, MISC, 72:72 + width], start=True, stop=True, skip_group_check=True)
                mm.then_inc(acc_full, 1)

            def route(layer, i):
                await_input(i)
                narrow(f"rtq{layer}", wr[:, layer, :, :].rearrange("p k c -> p (k c)"), 20)
                for t, c0, n in tiles:
                    if t == 1:
                        narrow_turn(f"rt{layer}", rt_rows, 20)
                    out = flatbuf(f"tm{layer}_{t}", KD, P)
                    begin(f"tm{layer}_{t}")
                    for k in range(KD):
                        mm = pe.transpose(out[0:n, k, :], hT[:, k, c0:c0 + n], cst[:, IDENT, :])
                    mm.then_inc(acc_full, 1)
                pe.wait_ge(one_hots_ready, layer + 1)
                ps = begin(f"rk{layer}")
                for t, c0, n in tiles:
                    for b in range(t + 1):
                        before = ones[:, 0:n] if b < t else cst[0:n, TRIU, 0:n]
                        pe.matmul(ps[0:n, 0, E * t:E * (t + 1)], before, chosen[2][0:P if b < t else n, b, :],
                                  start=(b == 0), stop=(b == t), skip_group_check=True)
                for t, c0, n in tiles:
                    mm = pe.matmul(ps[:, 1, 0:E], ones[0:n, :], chosen[2][0:n, t, :], start=(t == 0), stop=(t == 4))
                mm.then_inc(acc_full, 1)

            def turn_rows(x, xt):
                for k in range(KD):
                    mm = pe.transpose(xt[:, k, :], x[:, P * k:P * (k + 1)], cst[:, IDENT, :])
                return mm

            def hidden(w1, w3, xt):
                for x, w in ((0, w1), (1, w3)):
                    wv = w.rearrange("p (m k c) -> p m k c", m=2, k=KD)
                    for f in range(2):
                        for k in range(KD):
                            mm = pe.matmul(acc[:, H_ACC, x, P * f:P * (f + 1)], wv[:, f, k, :], xt[:, k, :],
                                           start=(k == 0), stop=(k == KD - 1), skip_group_check=True)
                return mm

            def outputs(y, hd, w2):
                for b in range(2):
                    for f in range(2):
                        mm = pe.matmul(y[:, b, :], hd[:, P * f:P * (f + 1)], w2[:, D * f + 512 * b:D * f + 512 * (b + 1)],
                                       start=(f == 0), stop=(f == 1))
                return mm

            def moe(layer):
                for n in range(state["n"] - NACC, state["n"]):
                    last = book["name", n]
                    pe.wait_ge(reader(last), at("read:" + last))
                first = unit_no["moe", layer, 0]
                done = E * layer
                xt_acc = acc[:, XT_ACC].rearrange("p b c -> p (b c)").rearrange("p (k n) -> p k n", n=P)
                pe.wait_ge(xc_loaded[0], 16 * (E // 2) * layer + 16)
                turn_rows(xc[0], xt_acc).then_inc(xt_full, 1)

                def turn(i, last=False):
                    for j in range(2):
                        slots = [(first + 3 * j + x) % NSLOT for x in range(3)]
                        w1, w3, w2 = (ring[:, s, :] for s in slots)
                        loaded = [at(("unit", first + 3 * j + x)) for x in range(3)]
                        pe.wait_ge(slot_loaded[slots[0]], i * 16 + loaded[0])
                        pe.wait_ge(slot_loaded[slots[1]], i * 16 + loaded[1])
                        pe.wait_ge(xt_out, i * 2 + (done + j + 1))
                        hidden(w1, w3, xcT[j]).then_inc(h_full, 1)
                        if not (last and j == 1):
                            pe.wait_ge(xc_loaded[1 - j], i * 16 + (16 * (E // 2) * layer + 16 + 16 * j))
                            turn_rows(xc[1 - j], xt_acc).then_inc(xt_full, 1)
                        pe.wait_ge(slot_loaded[slots[2]], i * 16 + loaded[2])
                        pe.wait_ge(hid_ready, i * 2 + (done + j + 1))
                        outputs(acc[:, Y_ACC + j], hid[j], w2).then_inc(y_full, 1)

                with pe.Fori(0, E // 2 - 1) as i:
                    turn(i)
                turn(E // 2 - 1, last=True)
                for j in range(6):
                    book["unit_read", first + 3 * E - 6 + j] = state["n"]
                n_over = pe.value_load(over[0:1, 8:9], min_val=0, max_val=NOVER)
                with pe.Fori(0, NOVER // 2) as i:
                    for p in range(2):
                        with pe.If(n_over > i * 2 + p):
                            w1, w3, w2 = (ring[:, (first + 3 * p + x) % NSLOT, :] for x in range(3))
                            pe.wait_ge(over_loaded[p][layer], i * 64 + 64)
                            turn_rows(xc[p], xt_acc).then_inc(over_xt_full[layer], 1)
                            pe.wait_ge(over_xt_out[layer], i * 2 + (p + 1))
                            hidden(w1, w3, xcT[p]).then_inc(over_h_full[layer], 1)
                            pe.wait_ge(over_hid_ready[layer], i * 2 + (p + 1))
                            outputs(acc[:, Y_ACC + p], hid[p], w2).then_inc(over_y_full[layer], 1)
                for t, c0, n in tiles:
                    pe.wait_ge(combined, at(f"o{layer}_{t}"))
                    out = flatbuf(f"ot{layer}_{t}", KD, n)
                    begin(f"ot{layer}_{t}")
                    for k in range(KD):
                        mm = pe.transpose(out[:, k, :], otok[t % 2][0:n, P * k:P * (k + 1)], cst[0:n, IDENT, 0:n])
                    mm.then_inc(acc_full, 1)

            def s5():
                await_input(2)
                for m in range(KD):
                    n = unit_no["s5in", 0, m // 2]
                    w = weights(n).rearrange("p (m k c) -> p m k c", m=2, k=KD)
                    project(f"u{m}", w[:, m % 2], hT)
                    book["unit_read", n] = state["n"]
                for c in range(KD):
                    for r, name in enumerate(("zr", "zi")):
                        if r == 0:
                            pe.wait_ge(zr_ready, at(f"zr{c}"))
                        else:
                            pe.wait_ge(zi_ready, at(f"zi{c}"))
                        begin(f"{name}{c}")
                        out = flatbuf(f"{name}{c}", 8, P)
                        for m in range(8):
                            mm = pe.transpose(out[:, m, :], Z[r][:, P * m:P * m + P], cst[:, IDENT, :])
                        mm.then_inc(acc_full, 1)
                    pe.wait_ge(act_drained, at(f"read:zi{c}"))
                    pe.wait_ge(u_masked, at(f"um{c}"))
                    ps = begin(f"inc{c}")
                    uv = uM[c % 2].rearrange("p j (c t) -> p t j c", t=8)
                    for r in range(2):
                        for tau in range(8):
                            mm = pe.matmul(ps[:, r, 0:4 * NCK].rearrange("p (j c) -> p j c", j=4),
                                           ZT[:, r, 7 - tau, :], uv[:, tau], start=(tau == 0), stop=(tau == 7))
                    mm.then_inc(acc_full, 1)
                def responses(c):
                    CAc = CA[c % 2]
                    if c == 0:
                        pe.wait_ge(first_ca_ready, 2)
                    else:
                        pe.wait_ge(ca_re_ready, at(f"car{c}"))
                        pe.wait_ge(ca_im_ready, at(f"cai{c}"))
                    ps = begin(f"K{c}")
                    for j in range(4):
                        q = 4 * c + j
                        for r in range(2):
                            mm = pe.matmul(ps[32 * j:32 * j + 32, 0, 0:256].rearrange("p (m c) -> p m c", m=8),
                                           BC[:, r, q, :], CAc[r][:, 0:8, j, :], start=(r == 0), stop=(r == 1),
                                           skip_group_check=True)
                    mm.then_inc(acc_full, 1)
                    if c == 0:
                        pe.wait_ge(entry_states_ready, at("sin"))
                    ps = begin(f"yc{c}")
                    for j in range(4):
                        q = 4 * c + j
                        for r in range(2):
                            mm = pe.matmul(ps[0:NCK, j // 2, 256 * (j % 2):256 * (j % 2) + 256].rearrange(
                                               "p (m c) -> p m c", m=8),
                                           SIN[:, r, q, :], CAc[r][:, 1:9, j, :], start=(r == 0), stop=(r == 1),
                                           skip_group_check=True)
                    mm.then_inc(acc_full, 1)

                pe.wait_ge(b_im_negated, 1)
                responses(0)
                for c in range(KD):
                    if c < KD - 1:
                        responses(c + 1)
                    pe.wait_ge(dve_drained, at(f"kb{c}"))
                    pe.wait_ge(act_drained, at(f"read:yc{c}"))
                    ps = begin(f"ys{c}")
                    uv = zT[:, c, :].rearrange("p (c t) -> p t c", t=8)
                    for b in range(2):
                        ov = ps[:, b, 0:4 * NCK].rearrange("p (t c) -> p t c", t=4)
                        for lag in range(8):
                            lo, hi = max(4 * b, lag), 4 * b + 4
                            if lo >= hi:
                                continue
                            pe.matmul(ov[:, lo - 4 * b:4], KB[c % 2][:, lag, :], uv[:, lo - lag:hi - lag],
                                      start=(lag == 0), stop=False, skip_group_check=True)
                        for tau in range(4):
                            mm = pe.matmul(ov[:, tau, :], YS[c % 2][:, 4 * b + tau, :], cst[0:NCK, IDENT, 0:NCK],
                                           start=False, stop=(tau == 3), skip_group_check=True)
                    mm.then_inc(acc_full, 1)
                pe.wait_ge(gelu_done, at("gelu"))
                for m in range(KD):
                    n = unit_no["glu", 0, m]
                    w = weights(n).rearrange("p (m k c) -> p m k c", m=2, k=KD)
                    project(f"ga{m}", w[:, 0], hT)
                    project(f"gg{m}", w[:, 1], hT)
                    book["unit_read", n] = state["n"]

            pe.wait_ge(consts_in, book.get("consts", 16))
            pe.wait_ge(ones_ready, at("ones"))
            norm_sums(0)
            pe.wait_ge(silu_c_ready, at("silu_c"))
            for nb in range(4):
                adaln(0, nb)
                if nb:
                    adaln_turn(0, nb - 1)
            adaln_turn(0, 3)
            await_input(0)
            narrow("baq", w_ba[:, :, :].rearrange("p k c -> p (k c)"), 16)
            for m in range(32):
                n = unit_no["w_in", 0, m // 2]
                w = weights(n).rearrange("p (m k c) -> p m k c", m=2, k=KD)
                project(f"p{m}", w[:, m % 2], hT)
                if m == 0:
                    narrow_turn("ba", ba_rows, 16)
                book["unit_read", n] = state["n"]
                if 2 <= m < 18:
                    pe.wait_ge(l2_squares_ready, at(f"l2sq{m - 2}"))
                    ps = begin(f"l{m - 2}")
                    for b in range(2):
                        mm = pe.matmul(ps[:, b, 0:HT], ones[:, :], sq[m % 2][:, HT * b:HT * b + HT],
                                       start=True, stop=True)
                    mm.then_inc(acc_full, 1)
                if 1 <= m <= N_LATE:
                    adaln_turn(*LATE[m - 1])
                if m < N_LATE:
                    adaln(*LATE[m])
            pe.wait_ge(g_ready, at("gg"))
            ps = begin("G")
            for t, c0, n in tiles:
                for b, mask in ((0, cst[0:n, tri(t), 0:n]), (1, ones[0:n, 0:n] if t < 4 else cst[0:n, ONES8, 0:n])):
                    mm = pe.matmul(ps[0:n, b, 8 * t:8 * t + 8], mask, gt[0:n, GG, t, :], start=True, stop=True,
                                   skip_group_check=True)
            mm.then_inc(acc_full, 1)
            pe.wait_ge(l2_done, at("l215"))
            pe.wait_ge(qkv_silu_done, at("act23"))
            for step_ in range(6):
                prepare(0, step_)
            first_block(0)
            for t, c0, n in tiles:
                delta_tile(t, c0, n)
            pe.wait_ge(o_squares_ready, at("osq"))
            ps = begin("osum")
            for h in range(H):
                for b in range(2):
                    mm = pe.matmul(ps[0:H, b, 0:HT], cst[:, MISC, 64 - h:64 - h + H], hT[:, h, HT * b:HT * b + HT],
                                   start=(h == 0), stop=(h == H - 1))
            mm.then_inc(acc_full, 1)
            pe.wait_ge(head_rows_ready, 1)
            pe.wait_ge(o_root_ready, 1)
            for h in range(H):
                ps = begin(f"og{h}")
                for b in range(2):
                    mm = pe.matmul(ps[:, b, 0:HT], head_rows[:, h, :], rb[0:H, HT * b:HT * b + HT],
                                   start=True, stop=True)
                mm.then_inc(acc_full, 1)
            pe.wait_ge(o_normed, at("onorm"))
            for m in range(KD):
                n = unit_no["w_out", 0, m // 2]
                w = weights(n).rearrange("p (m k c) -> p m k c", m=2, k=KD)
                project(f"w{m}", w[:, m % 2], yT)
                book["unit_read", n] = state["n"]
            norm_sums(1)
            route(0, 1)
            moe(0)
            norm_sums(2)
            s5()
            norm_sums(3)
            route(1, 3)
            moe(1)
            norm_sums(4)

        @block.scalar
        def _(act):
            def step(ins):
                ins.then_inc(act_order, up(act_order))
                act.wait_ge(act_order, now(act_order))

            def load_table(func):
                step(act.activation(small[:, 3:4], small[:, 0:1], func))

            def norm(i, m):
                for j in range(KD if i % 2 else 5):
                    act.wait_ge(x_ready, at(f"x{i}_{j}"))
                    _, c0, n = tiles[j % 5]
                    part = (slice(None), j, slice(None)) if i % 2 else (slice(None), slice(None), slice(c0, c0 + n))
                    act.activation(zT[part], xT[part], ACT.Square).then_inc(
                        squares_ready, up(squares_ready, f"nsq{i}_{j}"))
                act.wait_ge(squares_ready, now(squares_ready))
                load_table(ACT.Sqrt)
                act.wait_ge(acc_full, filled(f"ssq{i}"))
                act.activation(halves(rb[:, :]), tok(f"ssq{i}"), ACT.Sqrt, bias=small[:, 0:1], scale=1.0 / D).then_inc(
                    act_drained, up(act_drained, f"read:ssq{i}"))
                act.wait_ge(act_drained, now(act_drained))
                if m is None:
                    return
                act.wait_ge(mod_ready, at(f"mod{m}"))
                for k in range(KD):
                    act.wait_ge(x_scaled, at(f"npre{i}_{k}"))
                    ins = act.activation(hT[:, k, 0:SEQ], yT[:, k, 0:SEQ], ACT.Identity,
                                         bias=modT[:, m, k, 0:1], scale=modA[:, m, k, 0:1])
                    if k < KD - 1:
                        ins.then_inc(act_order, up(act_order))
                act.wait_ge(act_order, now(act_order))
                ins.then_inc(prompt_input_ready, up(prompt_input_ready, f"h{i}"))
                act.wait_ge(prompt_input_ready, now(prompt_input_ready))

            def rows_out(layer):
                act.wait_ge(acc_full, filled(f"rtq{layer}"))
                if layer == 0:
                    act.wait_ge(conv_stored, 32)
                act.activation(halves(rt_rows), tok(f"rtq{layer}"), ACT.Copy).then_inc(
                    act_drained, up(act_drained, f"read:rtq{layer}"))
                act.wait_ge(act_drained, now(act_drained))
                if layer == 0:
                    for s in snew_out:
                        act.wait_ge(s, 16 * (H // 2))
                for t, c0, n in tiles:
                    act.wait_ge(acc_full, filled(f"tm{layer}_{t}"))
                    act.activation(htok[t][0:n, :], flatbuf(f"tm{layer}_{t}", 1, D)[0:n, 0, :], ACT.Copy).then_inc(
                        act_drained, up(act_drained, f"read:tm{layer}_{t}"))
                    act.wait_ge(act_drained, now(act_drained))

            def moe(layer):
                done = E * layer
                xt_acc = acc[:, XT_ACC].rearrange("p b c -> p (b c)").rearrange("p (k n) -> p k n", n=P)
                load_table(ACT.Silu)
                act.wait_ge(xt_full, done + 1)
                act.activation(xcT[0], xt_acc, ACT.Copy).then_inc(xt_out, 1)

                def turn(i, last=False):
                    for j in range(2):
                        act.wait_ge(h_full, i * 2 + (done + j + 1))
                        act.activation(s1[j], acc[:, H_ACC, 0, 0:2 * P], ACT.Silu).then_inc(s1_ready, 1)
                        if not (last and j == 1):
                            act.wait_ge(xt_full, i * 2 + (done + j + 2))
                            act.activation(xcT[1 - j], xt_acc, ACT.Copy).then_inc(xt_out, 1)

                with act.Fori(0, E // 2 - 1) as i:
                    turn(i)
                turn(E // 2 - 1, last=True)
                act.wait_ge(routed, layer + 1)
                n_over = act.value_load(over[0:1, 8:9], min_val=0, max_val=NOVER)
                with act.Fori(0, NOVER // 2) as i:
                    for p in range(2):
                        with act.If(n_over > i * 2 + p):
                            act.wait_ge(over_xt_full[layer], i * 2 + (p + 1))
                            act.activation(xcT[p], xt_acc, ACT.Copy).then_inc(over_xt_out[layer], 1)
                            act.wait_ge(over_h_full[layer], i * 2 + (p + 1))
                            act.activation(s1[p], acc[:, H_ACC, 0, 0:2 * P], ACT.Silu).then_inc(
                                over_s1_ready[layer], 1)
                for t, c0, n in tiles:
                    g1 = got[t][0][0:n, :]
                    act.wait_ge(gathered[t], at(f"g{layer}_{t}"))
                    act.activation(g1, g1, ACT.Copy, scale=rtv["w1"][0:n, t:t + 1]).then_inc(
                        weighted, up(weighted, f"w{layer}_{t}"))

            act.wait_ge(consts_in, book.get("consts", 16))
            act.wait_ge(ones_ready, at("ones"))
            act.activation(c32[:, :, 0:9], cT[:, :, :], ACT.Silu).then_inc(silu_c_ready, up(silu_c_ready, "silu_c"))
            act.wait_ge(silu_c_ready, now(silu_c_ready))
            step(act.activation(lam[:, 2, :], lam[:, 2, :], ACT.Exp))
            act.activation(hp[:, 0, :], hp[:, 0, :], ACT.Exp).then_inc(dt_ready, up(dt_ready, "dt"))
            act.wait_ge(dt_ready, now(dt_ready))
            act.wait_ge(s5_angle_ready, at("ang"))
            step(act.activation(s5t[:, 0, :], s5t[:, 0, :], ACT.Exp))
            step(act.activation(s5t[:, 3, :], s5t[:, 1, :], ACT.Sin))
            act.activation(s5t[:, 4, :], s5t[:, 2, :], ACT.Sin, bias=small[:, 2:3], scale=-1.0).then_inc(
                trig_ready, up(trig_ready, "trig"))
            act.wait_ge(trig_ready, now(trig_ready))
            act.wait_ge(x_in, 16)
            act.activation(yT[:, :, :], xT[:, :, :], ACT.Square).then_inc(squares_ready, up(squares_ready, "nsq0_0"))
            act.wait_ge(squares_ready, now(squares_ready))
            act.wait_ge(acc_full, filled("ssq0"))
            act.activation(halves(rb[:, :]), tok("ssq0"), ACT.Sqrt, bias=small[:, 0:1], scale=1.0 / D).then_inc(
                act_drained, up(act_drained, "read:ssq0"))
            act.wait_ge(act_drained, now(act_drained))

            def modulation(m, nb):
                act.wait_ge(acc_full, filled(f"ada{m}_{nb}"))
                late = (m, nb) in LATE
                if late and (m, nb) != LATE[0]:
                    act.wait_ge(acc_full, filled("adaT%d_%d" % LATE[LATE.index((m, nb)) - 1]))
                act.activation(m_sb[4 if late else nb], buf(f"ada{m}_{nb}")[:, 0, :], ACT.Copy).then_inc(
                    act_drained, up(act_drained, f"read:ada{m}_{nb}"))
                act.wait_ge(act_drained, now(act_drained))

            for nb in range(4):
                modulation(0, nb)
            act.wait_ge(x_scaled, at("npre0"))
            act.wait_ge(mod_ready, at("mod0"))
            for k in range(KD):
                ins = act.activation(hT[:, k, 0:SEQ], yT[:, k, 0:SEQ], ACT.Identity,
                                     bias=modT[:, 0, k, 0:1], scale=modA[:, 0, k, 0:1])
                if k < KD - 1:
                    ins.then_inc(act_order, up(act_order))
            act.wait_ge(act_order, now(act_order))
            ins.then_inc(prompt_input_ready, up(prompt_input_ready, "h0"))
            act.wait_ge(prompt_input_ready, now(prompt_input_ready))
            act.wait_ge(acc_full, filled("baq"))
            act.activation(halves(ba_rows), tok("baq"), ACT.Copy).then_inc(act_drained, up(act_drained, "read:baq"))
            act.wait_ge(act_drained, now(act_drained))
            act.wait_ge(gate_args_ready, at("ba"))
            step(act.activation(gt[:, BETA], gt[:, BB], ACT.Sigmoid))
            step(act.activation(gt[:, G1], gt[:, G2], ACT.Exp, scale=-1.0))
            act.activation(gt[:, G2], gt[:, G1], ACT.Ln, bias=1.0).then_inc(
                softplus_ready, up(softplus_ready, "splus"))
            act.wait_ge(softplus_ready, now(softplus_ready))
            for m in range(32 + 3):
                if m < QKV:
                    act.wait_ge(acc_full, filled(f"p{m}"))
                    if m >= 2:
                        act.wait_ge(conv_done, at(f"conv{m - 2}"))
                        act.wait_ge(history_ready, at(f"cs{m - 2}"))
                    act.activation(halves(raw[m % 2][:, 3:3 + T]), tok(f"p{m}"), ACT.Copy).then_inc(
                        act_drained, up(act_drained, f"read:p{m}"))
                    act.wait_ge(act_drained, now(act_drained))
                elif m < 32:
                    act.wait_ge(acc_full, filled(f"p{m}"))
                    act.activation(halves(zT[:, m - QKV, :]), tok(f"p{m}"), ACT.Silu).then_inc(
                        act_drained, up(act_drained, f"read:p{m}"))
                    act.wait_ge(act_drained, now(act_drained))
                if 1 <= m <= QKV:
                    act.wait_ge(conv_done, at(f"conv{m - 1}"))
                    act.activation(qkv[:, m - 1, :], qkv[:, m - 1, :], ACT.Silu).then_inc(
                        qkv_silu_done, up(qkv_silu_done, f"act{m - 1}"))
                    act.wait_ge(qkv_silu_done, now(qkv_silu_done))
                if 1 <= m <= 16:
                    if m >= 3:
                        act.wait_ge(acc_full, filled(f"l{m - 3}"))
                    act.activation(sq[(m - 1) % 2], qkv[:, m - 1, :], ACT.Square).then_inc(
                        l2_squares_ready, up(l2_squares_ready, f"l2sq{m - 1}"))
                    act.wait_ge(l2_squares_ready, now(l2_squares_ready))
                if 2 <= m < 18:
                    act.wait_ge(acc_full, filled(f"l{m - 2}"))
                    if m >= 4:
                        act.wait_ge(l2_done, at(f"l2{m - 4}"))
                    is_q = m - 2 < 8
                    act.activation(halves(ln[m % 2]), tok(f"l{m - 2}"), ACT.Sqrt,
                                         bias=small[:, 1:2] if is_q else small[:, 0:1],
                                         scale=float(P) if is_q else 1.0).then_inc(
                                             act_drained, up(act_drained, f"read:l{m - 2}"))
                    act.wait_ge(act_drained, now(act_drained))
                if m < N_LATE:
                    modulation(*LATE[m])
            act.wait_ge(log_decay_ready, at("gcol"))
            step(act.activation(gt[:, G1], gt[:, GCOL], ACT.Exp))
            act.activation(gt[:, CKDEC], gt[:, G2], ACT.Exp).then_inc(decay_cols_ready, up(decay_cols_ready, "ecol"))
            act.wait_ge(decay_cols_ready, now(decay_cols_ready))

            def decay_rows(t):
                n = tiles[t][2]
                act.wait_ge(acc_full, filled(f"gr{t}"))
                if t >= 2:
                    act.wait_ge(dve_drained, at(f"S{t - 2}"))
                act.activation(um(EG, t, n, P), flatbuf(f"gr{t}", H, n), ACT.Exp).then_inc(
                    decay_rows_ready, up(decay_rows_ready, f"eG{t}"))
                act.wait_ge(decay_rows_ready, now(decay_rows_ready))

            def decay_between(t):
                n = tiles[t][2]
                act.wait_ge(decay_diff_ready, at(f"diff{t}"))
                act.activation(um(EX, t, n), um(EX, t, n), ACT.Exp).then_inc(
                    decay_exp_ready, up(decay_exp_ready, f"ex{t}"))
                act.wait_ge(decay_exp_ready, now(decay_exp_ready))

            decay_rows(0)
            decay_between(0)
            for t, c0, n in tiles:
                for l in range(1, levels(t)):
                    name = f"X{t}_{l}"
                    for b in range(2):
                        if b == 0:
                            act.wait_ge(pe_half, at(f"half:{name}"))
                        else:
                            act.wait_ge(acc_full, filled(name))
                        if l == 1:
                            act.wait_ge(dve_drained, at(f"read:qk{t}"))
                        elif b == 0:
                            act.wait_ge(pe_half, at(f"half:MTX{t}_{l - 1}"))
                        else:
                            act.wait_ge(acc_full, filled(f"MTX{t}_{l - 1}"))
                        ins = act.activation(um(EX, t, n)[:, four(b), :], bank(name, b, n), ACT.Copy)
                        if b == 0:
                            ins.then_inc(act_half, up(act_half, f"read half:{name}"))
                        else:
                            ins.then_inc(act_drained, up(act_drained, f"read:{name}"))
                    act.wait_ge(act_half, now(act_half))
                    act.wait_ge(act_drained, now(act_drained))
                    if t < 4 and l == 1:
                        decay_rows(t + 1)
                    if t < 4 and l == 2:
                        decay_between(t + 1)
                act.wait_ge(acc_full, filled(f"wT{t}"))
                act.activation(um(EX, t, n, P), flatbuf(f"wT{t}", H, n), ACT.Copy).then_inc(
                    act_drained, up(act_drained, f"read:wT{t}"))
                act.wait_ge(act_drained, now(act_drained))
                if t < 4:
                    act.wait_ge(acc_full, filled(f"vn{t}"))
                    act.activation(ur(VN, t, n), flatbuf(f"vn{t}", H, P), ACT.Copy).then_inc(
                        act_drained, up(act_drained, f"read:vn{t}"))
                    act.wait_ge(act_drained, now(act_drained))
                    act.wait_ge(acc_full, filled(f"o{t}"))
                    act.activation(yT[:, :, c0:c0 + n], flatbuf(f"o{t}", H, n), ACT.Copy).then_inc(
                        act_drained, up(act_drained, f"read:o{t}"))
                    act.wait_ge(act_drained, now(act_drained))
                else:
                    out = both(buf("oS").rearrange("p b c -> p (b c)"))
                    act.wait_ge(pe_half, at("half:oS"))
                    act.activation(um(M, t, n, P), out[:, :, 0, :], ACT.Copy).then_inc(
                        act_half, up(act_half, "read half:oS"))
                    act.wait_ge(act_half, now(act_half))
                    act.wait_ge(acc_full, filled("vtr"))
                    act.activation(ur(VN, t, n), flatbuf("vtr", H, P)[0:n], ACT.Copy).then_inc(
                        act_drained, up(act_drained, "read:vtr"))
                    act.wait_ge(act_drained, now(act_drained))
                    act.wait_ge(acc_full, filled("oS"))
                    act.activation(yT[:, :, c0:c0 + n], out[:, :, 1, :], ACT.Copy).then_inc(
                        act_drained, up(act_drained, "read:oS"))
                    act.wait_ge(act_drained, now(act_drained))
            act.wait_ge(dve_drained, at("snew7"))
            act.activation(hT[:, :, :], yT[:, :, :], ACT.Square).then_inc(o_squares_ready, up(o_squares_ready, "osq"))
            act.wait_ge(o_squares_ready, now(o_squares_ready))
            load_table(ACT.Sqrt)
            act.wait_ge(acc_full, filled("osum"))
            act.activation(halves(rb[0:H, :]), tok("osum")[0:H], ACT.Sqrt, bias=small[0:H, 0:1],
                           scale=1.0 / P).then_inc(act_drained, up(act_drained, "read:osum"))
            act.wait_ge(act_drained, now(act_drained))
            norm(1, 1)

            def route(layer):
                load_table(ACT.Exp)
                act.wait_ge(group_diff_ready, at(f"rga{layer}"))
                act.activation(rtv["ge"], rtv["ge"], ACT.Exp).then_inc(
                    group_exp_ready, up(group_exp_ready, f"rgb{layer}"))
                act.wait_ge(group_exp_ready, now(group_exp_ready))
                act.wait_ge(expert_diff_ready, at(f"rea{layer}"))
                act.activation(rtv["e2"], rtv["e2"], ACT.Exp).then_inc(
                    expert_exp_ready, up(expert_exp_ready, f"reb{layer}"))
                act.wait_ge(expert_exp_ready, now(expert_exp_ready))

            rows_out(0)
            route(0)
            moe(0)
            norm(2, 2)
            for m in range(KD):
                act.wait_ge(acc_full, filled(f"u{m}"))
                act.activation(halves(zT[:, m, :]), tok(f"u{m}"), ACT.Copy).then_inc(
                    act_drained, up(act_drained, f"read:u{m}"))
                act.wait_ge(act_drained, now(act_drained))

            def mask_u(c):
                if c >= 2:
                    act.wait_ge(acc_full, filled(f"inc{c - 2}"))
                for j in range(4):
                    act.activation(uM[c % 2][:, j, :], zT[:, c, :], ACT.Copy, scale=cst[:, MISC, j:j + 1]).then_inc(
                        u_masked, up(u_masked, f"um{c}"))
                act.wait_ge(u_masked, now(u_masked))

            mask_u(0)
            for c in range(KD):
                for r, name in enumerate(("zr", "zi")):
                    act.wait_ge(acc_full, filled(f"{name}{c}"))
                    if c and r == 0:
                        act.wait_ge(acc_full, filled(f"inc{c - 1}"))
                    act.activation(ZT[:, r], flatbuf(f"{name}{c}", 8, P), ACT.Copy).then_inc(
                        act_drained, up(act_drained, f"read:{name}{c}"))
                    act.wait_ge(act_drained, now(act_drained))
                if c < KD - 1:
                    mask_u(c + 1)
            for c in range(KD):
                act.wait_ge(acc_full, filled(f"yc{c}"))
                if c >= 2:
                    act.wait_ge(acc_full, filled(f"ys{c - 2}"))
                act.activation(YS[c % 2].rearrange("p t (j c) -> p j t c", j=4),
                                     flatbuf(f"yc{c}", 4, 256)[0:NCK].rearrange("p j (t c) -> p j t c", t=8),
                                     ACT.Copy).then_inc(act_drained, up(act_drained, f"read:yc{c}"))
                act.wait_ge(act_drained, now(act_drained))
            load_table(ACT.Gelu_apprx_tanh)
            act.wait_ge(dve_drained, at("ysum"))
            act.activation(hT[:, :, :], hT[:, :, :], ACT.Gelu_apprx_tanh).then_inc(gelu_done, up(gelu_done, "gelu"))
            act.wait_ge(gelu_done, now(gelu_done))
            load_table(ACT.Sigmoid)
            for m in range(KD):
                act.wait_ge(acc_full, filled(f"gg{m}"))
                if m >= 2:
                    act.wait_ge(dve_drained, at(f"glu{m - 2}"))
                act.activation(halves(extra[:, m % 2, 0:T]), tok(f"gg{m}"), ACT.Sigmoid).then_inc(
                    act_drained, up(act_drained, f"read:gg{m}"))
                act.wait_ge(act_drained, now(act_drained))
            norm(3, 3)
            rows_out(1)
            route(1)
            moe(1)
            norm(4, None)

        @block.vector
        def _(dve):
            def step(ins):
                ins.then_inc(dve_order, up(dve_order))
                dve.wait_ge(dve_order, now(dve_order))

            def start(ins):
                ins.then_inc(dve_order, up(dve_order))

            tt, ts, stt = dve.tensor_tensor, dve.tensor_scalar, dve.scalar_tensor_tensor

            def seqs(ap):
                return ap.rearrange("p k (b s) -> p k b s", s=LS)

            def norm(i, m):
                dve.wait_ge(act_drained, at(f"read:ssq{i}"))
                step(dve.reciprocal(rb[:, :], rb[:, :]))
                if m is None:
                    for k in range(KD):
                        stt(yT[:, k, :], xT[:, k, :], nrm[:, 4, k:k + 1], rb[:, :], ALU.mult, ALU.mult).then_inc(
                            out_ready, up(out_ready, f"out{k}"))
                    dve.wait_ge(out_ready, now(out_ready))
                    return
                for k in range(KD):
                    tt(yT[:, k, :], xT[:, k, :], rb[:, :], ALU.mult).then_inc(x_scaled, up(x_scaled, f"npre{i}_{k}"))
                dve.wait_ge(x_scaled, now(x_scaled))
                step(tt(seqs(hT[:, :, SEQ:T]), seqs(yT[:, :, SEQ:T]), bc(modA[:, m, :, 1:9], 3, LS), ALU.mult))
                tt(seqs(hT[:, :, SEQ:T]), seqs(hT[:, :, SEQ:T]), bc(modT[:, m, 0:KD, 1:9], 3, LS), ALU.add).then_inc(
                    sample_input_ready, up(sample_input_ready, f"hs{i}"))
                dve.wait_ge(sample_input_ready, now(sample_input_ready))

            def residual(k, m, prompt, sample, tmp, label=None, name=None):
                gate = modT[:, m, 16 + k, :]
                for src, c0, n in prompt:
                    step(stt(xT[:, k, c0:c0 + n], src, gate[:, 0:1], xT[:, k, c0:c0 + n], ALU.mult, ALU.add))
                ins = tt(tmp.rearrange("p (b s) -> p b s", s=LS), sample.rearrange("p (b s) -> p b s", s=LS),
                         bc(gate[:, 1:9], 2, LS), ALU.mult)
                if name:
                    ins.then_inc(dve_drained, up(dve_drained, "read:" + name))
                    dve.wait_ge(dve_drained, now(dve_drained))
                else:
                    step(ins)
                tt(xT[:, k, SEQ:T], xT[:, k, SEQ:T], tmp, ALU.add).then_inc(x_ready, up(x_ready, label))
                dve.wait_ge(x_ready, now(x_ready))

            dve.memset(S[:, :, :], 0.0).then_inc(zero_ready, 1)
            dve.wait_ge(zero_ready, 1)
            dve.wait_ge(consts_in, book.get("consts", 16))
            dve.wait_ge(dt_ready, at("dt"))
            lr, li, dt = lam[:, 0, :], lam[:, 1, :], lam[:, 2, :]
            step(tt(s5t[:, 0, :], lr, dt, ALU.mult))
            step(tt(s5t[:, 1, :], li, dt, ALU.mult))
            step(ts(s5t[:, 2, :], s5t[:, 1, :], 1.0 / (2.0 * np.pi), MAGIC, ALU.mult, ALU.add))
            step(ts(s5t[:, 2, :], s5t[:, 2, :], MAGIC, None, ALU.subtract))
            step(stt(s5t[:, 1, :], s5t[:, 2, :], -TWO_PI_HI, s5t[:, 1, :], ALU.mult, ALU.add))
            step(stt(s5t[:, 1, :], s5t[:, 2, :], -TWO_PI_LO, s5t[:, 1, :], ALU.mult, ALU.add))
            step(ts(s5t[:, 1, :], s5t[:, 1, :], PI_LIM, -PI_LIM, ALU.min, ALU.max))
            step(ts(s5t[:, 2, :], s5t[:, 1, :], -1.0, None, ALU.mult))
            tt(s5t[:, 2, :], s5t[:, 2, :], s5t[:, 1, :], ALU.max).then_inc(s5_angle_ready, up(s5_angle_ready, "ang"))
            dve.wait_ge(s5_angle_ready, now(s5_angle_ready))
            dve.wait_ge(x_in, 16)
            dve.wait_ge(act_drained, at("read:ssq0"))
            step(dve.reciprocal(rb[:, :], rb[:, :]))
            tt(yT[:, :, :], xT[:, :, :], bc(rb[:, :], 1, KD), ALU.mult).then_inc(x_scaled, up(x_scaled, "npre0"))
            dve.wait_ge(x_scaled, now(x_scaled))

            def modulation(m, nb):
                dve.wait_ge(acc_full, filled(f"adaT{m}_{nb}"))
                tt(modT[:, m, 4 * nb:4 * nb + 4], flatbuf(f"adaT{m}_{nb}", 4, 9),
                   bc(bmod[:, m, 4 * nb:4 * nb + 4], 2, 9), ALU.add).then_inc(
                    dve_drained, up(dve_drained, f"read:adaT{m}_{nb}"))
                dve.wait_ge(dve_drained, now(dve_drained))
                if nb == 3:
                    step(ts(modA[:, m], modT[:, m, KD:2 * KD, :], 1.0, None, ALU.add))
                    tt(modA[:, m], modA[:, m], bc(nrm[:, m, :], 2, 9), ALU.mult).then_inc(
                        mod_ready, up(mod_ready, f"mod{m}"))
                    dve.wait_ge(mod_ready, now(mod_ready))

            for nb in range(4):
                modulation(0, nb)
            step(tt(seqs(hT[:, :, SEQ:T]), seqs(yT[:, :, SEQ:T]), bc(modA[:, 0, :, 1:9], 3, LS), ALU.mult))
            tt(seqs(hT[:, :, SEQ:T]), seqs(hT[:, :, SEQ:T]), bc(modT[:, 0, 0:KD, 1:9], 3, LS), ALU.add).then_inc(
                sample_input_ready, up(sample_input_ready, "hs0"))
            dve.wait_ge(sample_input_ready, now(sample_input_ready))
            dve.wait_ge(trig_ready, at("trig"))
            step(dve.memset(pw[:, 0, 0, :], 1.0))
            step(dve.memset(pw[:, 1, 0, :], 0.0))
            ar, ai = pw[:, 0, 1, :], pw[:, 1, 1, :]
            step(tt(ar, s5t[:, 0, :], s5t[:, 4, :], ALU.mult))
            step(tt(ai, s5t[:, 0, :], s5t[:, 3, :], ALU.mult))
            t0, t1, t2 = s5t[:, 5, :], s5t[:, 6, :], s5t[:, 7, :]
            for m in range(1, 8):
                step(tt(t0, pw[:, 0, m, :], ar, ALU.mult))
                step(tt(t1, pw[:, 1, m, :], ai, ALU.mult))
                step(tt(pw[:, 0, m + 1, :], t0, t1, ALU.subtract))
                step(tt(t0, pw[:, 0, m, :], ai, ALU.mult))
                step(tt(t1, pw[:, 1, m, :], ar, ALU.mult))
                step(tt(pw[:, 1, m + 1, :], t0, t1, ALU.add))
            step(tt(t0, lr, lr, ALU.mult))
            step(tt(t1, li, li, ALU.mult))
            step(tt(t2, t0, t1, ALU.add))
            step(dve.reciprocal(t2, t2))
            step(ts(s5t[:, 0, :], ar, 1.0, None, ALU.subtract))
            step(tt(t0, s5t[:, 0, :], lr, ALU.mult))
            step(tt(t1, ai, li, ALU.mult))
            step(tt(t0, t0, t1, ALU.add))
            step(tt(fz[:, 0, :], t0, t2, ALU.mult))
            step(tt(t0, ai, lr, ALU.mult))
            step(tt(t1, s5t[:, 0, :], li, ALU.mult))
            step(tt(t0, t0, t1, ALU.subtract))
            step(tt(fz[:, 1, :], t0, t2, ALU.mult))
            step(dve.memset(gt[:, :, :, :], 0.0))
            dve.wait_ge(acc_full, filled("ba"))
            for rows, t0_, nt in ((P, 0, 4), (TS, 4, 1)):
                src = buf("ba")[0:rows, 0, 16 * t0_:16 * (t0_ + nt)].rearrange("p (t c) -> p t c", c=16)
                step(dve.tensor_copy(gt[0:rows, BB, t0_:t0_ + nt, :], src[:, :, 0:8]))
                ins = tt(gt[0:rows, BA, t0_:t0_ + nt, :], src[:, :, 8:16], bc(hp[0:rows, 1, :], 1, nt), ALU.add)
                if t0_:
                    ins.then_inc(dve_drained, up(dve_drained, "read:ba"))
                    dve.wait_ge(dve_drained, now(dve_drained))
                else:
                    step(ins)
            step(ts(gt[:, G2], gt[:, BA], -1.0, None, ALU.mult))
            tt(gt[:, G2], gt[:, G2], gt[:, BA], ALU.max).then_inc(gate_args_ready, up(gate_args_ready, "ba"))
            dve.wait_ge(gate_args_ready, now(gate_args_ready))
            dve.wait_ge(softplus_ready, at("splus"))
            step(stt(gt[:, G1], gt[:, BA], 0.0, gt[:, G2], ALU.max, ALU.add))
            step(tt(gt[:, G1], gt[:, G1], bc(hp[:, 0, :], 1, 5), ALU.mult))
            ts(gt[:, GG], gt[:, G1], -1.0, None, ALU.mult).then_inc(g_ready, up(g_ready, "gg"))
            dve.wait_ge(g_ready, now(g_ready))
            dve.wait_ge(conv_in, 32)
            dve.wait_ge(prompt_input_ready, at("h0"))
            for i in range(2):
                step(dve.memset(raw[i][:, 0:3], 0.0))
            for m in range(QKV + 3):
                if 2 <= m < N_LATE + 2:
                    modulation(*LATE[m - 2])
                if m < QKV:
                    dve.wait_ge(act_drained, at(f"read:p{m}"))
                    dst = qkv[:, m, 0:SEQ]
                    sdst = qkv[:, m, SEQ:T].rearrange("p (b s) -> p b s", s=LS)
                    if m == 0:
                        dve.wait_ge(acc_full, filled("adaT0_3"))
                    step(ts(dst, raw[m % 2][:, 0:SEQ], cw[:, m, 0:1], None, ALU.mult))
                    for j in range(1, CW):
                        step(stt(dst, raw[m % 2][:, j:j + SEQ], cw[:, m, j:j + 1], dst, ALU.mult, ALU.add))
                    dve.wait_ge(history_ready, at(f"cs{m}"))
                    step(ts(sdst, sraw[m % 2][:, :, 0:LS], cw[:, m, 0:1], None, ALU.mult))
                    for j in range(1, CW):
                        ins = stt(sdst, sraw[m % 2][:, :, j:j + LS], cw[:, m, j:j + 1], sdst, ALU.mult, ALU.add)
                        if j < CW - 1:
                            step(ins)
                        else:
                            ins.then_inc(conv_done, up(conv_done, f"conv{m}"))
                            dve.wait_ge(conv_done, now(conv_done))
                if 3 <= m < 19:
                    dve.wait_ge(act_drained, at(f"read:l{m - 3}"))
                    step(dve.reciprocal(ln[(m - 3) % 2], ln[(m - 3) % 2]))
                    tt(qkv[:, m - 3, :], qkv[:, m - 3, :], ln[(m - 3) % 2], ALU.mult).then_inc(
                        l2_done, up(l2_done, f"l2{m - 3}"))
                    dve.wait_ge(l2_done, now(l2_done))
            dve.wait_ge(acc_full, filled("G"))
            for b, dst in ((0, GCOL), (1, GLAST)):
                step(dve.tensor_copy(gt[:, dst, 0:4, :],
                                     buf("G")[:, b, 0:32].rearrange("p (t h) -> p t h", t=4)))
                ins = dve.tensor_copy(gt[0:TS, dst, 4, :], buf("G")[0:TS, b, 32:40])
                if b:
                    ins.then_inc(dve_drained, up(dve_drained, "read:G"))
                    dve.wait_ge(dve_drained, now(dve_drained))
                else:
                    step(ins)
            tt(gt[:, G2], gt[:, GLAST], gt[:, GCOL], ALU.subtract).then_inc(
                log_decay_ready, up(log_decay_ready, "gcol"))
            dve.wait_ge(log_decay_ready, now(log_decay_ready))
            dve.wait_ge(decay_cols_ready, at("ecol"))
            step(stt(gt[:, CKBG], gt[:, G1], -1.0, gt[:, BETA], ALU.mult, ALU.mult))
            dve.wait_ge(conv_stored, 32)

            def row_masks(t):
                n = tiles[t][2]
                for k, mask, factor, label in ((AT, tri(t), GG, f"ru{t}"), (QKE, IDENT, BETA, f"rub{t}")):
                    tt(um(k, t, n), bc(cst[0:n, mask, 0:n], 1, H), bc(gt[0:n, factor, t, :], 2, n), ALU.mult).then_inc(
                        row_masks_ready, up(row_masks_ready, label))
                    dve.wait_ge(row_masks_ready, now(row_masks_ready))

            def prepare(t, step_):
                _, c0, n = tiles[t]
                x = um(EX, t, n)
                if step_ == 0:
                    dve.wait_ge(decay_rows_ready, at(f"eG{t}"))
                    tt(x, flatbuf(f"gr{t}", H, n)[0:n], bc(gt[0:n, GCOL, t, :], 2, n), ALU.subtract).then_inc(
                        dve_drained, up(dve_drained, f"read:gr{t}"))
                    dve.wait_ge(dve_drained, now(dve_drained))
                    ts(x, x, 0.0, None, ALU.min).then_inc(decay_diff_ready, up(decay_diff_ready, f"diff{t}"))
                    dve.wait_ge(decay_diff_ready, now(decay_diff_ready))
                elif step_ == 1:
                    dve.wait_ge(decay_exp_ready, at(f"ex{t}"))
                    step(tt(x, x, bc(cst[0:n, tri(t), 0:n], 1, H), ALU.mult))
                    dve.wait_ge(acc_full, filled(f"br{t}"))
                    tt(um(AT, t, n), flatbuf(f"br{t}", H, n)[0:n], x, ALU.mult).then_inc(
                        dve_drained, up(dve_drained, f"read:br{t}"))
                    dve.wait_ge(dve_drained, now(dve_drained))
                elif step_ == 2:
                    dve.wait_ge(acc_full, filled(f"kk{t}"))
                    tt(um(AT, t, n), um(AT, t, n), flatbuf(f"kk{t}", H, n)[0:n], ALU.mult).then_inc(
                        dve_drained, up(dve_drained, f"read:kk{t}", f"AT{t}"))
                    dve.wait_ge(dve_drained, now(dve_drained))
                elif step_ == 3:
                    dve.wait_ge(acc_full, filled(f"qk{t}"))
                    tt(um(QKE, t, n), flatbuf(f"qk{t}", H, n)[0:n], x, ALU.mult).then_inc(
                        dve_drained, up(dve_drained, f"read:qk{t}"))
                    dve.wait_ge(dve_drained, now(dve_drained))
                    tt(qkv[:, 0:H, c0:c0 + n], qkv[:, 0:H, c0:c0 + n], um(EG, t, n, P), ALU.mult).then_inc(
                        q_decayed, up(q_decayed, f"qdT{t}"))
                    dve.wait_ge(q_decayed, now(q_decayed))
                    if t == 4:
                        dve.tensor_copy(both_halves()[:, :, 1, :], qkv[:, 0:H, c0:c0 + n]).then_inc(
                            q_decayed, up(q_decayed, "q4"))
                        dve.wait_ge(q_decayed, now(q_decayed))
                elif step_ == 4:
                    dve.wait_ge(acc_full, filled(f"kt{t}"))
                    start(tt(ur(KBGT, t, n), flatbuf(f"kt{t}", H, P)[0:n], bc(gt[0:n, CKBG, t, :], 2, P), ALU.mult))
                    tt(ur(KDECT, t, n), flatbuf(f"kt{t}", H, P)[0:n], bc(gt[0:n, CKDEC, t, :], 2, P),
                       ALU.mult).then_inc(dve_drained, up(dve_drained, f"read:kt{t}"))
                    dve.wait_ge(dve_order, now(dve_order))
                    dve.wait_ge(dve_drained, now(dve_drained))
                else:
                    dve.wait_ge(acc_full, filled(f"vt{t}"))
                    tt(ur(VB, t, n), flatbuf(f"vt{t}", H, P)[0:n], bc(gt[0:n, BETA, t, :], 2, P), ALU.mult).then_inc(
                        dve_drained, up(dve_drained, f"read:vt{t}"))
                    dve.wait_ge(dve_drained, now(dve_drained))

            dve.wait_ge(acc_full, filled("p31"))
            row_masks(0)
            for step_ in range(6):
                prepare(0, step_)

            def first_inverse(t):
                n = tiles[t][2]
                eye = bc(cst[0:n, IDENT, 0:n], 1, H)
                dve.wait_ge(acc_full, filled(f"A0{t}"))
                tt(um(M, t, n), eye, flatbuf(f"A0{t}", H, n)[0:n], ALU.subtract).then_inc(
                    dve_drained, up(dve_drained, f"read:A0{t}"))
                dve.wait_ge(dve_drained, now(dve_drained))
                if t:
                    dve.wait_ge(acc_full, filled(f"vn{t - 1}"))
                tt(um(MT, t, n), eye, um(AB, t, n), ALU.subtract).then_inc(
                    first_inverse_ready, up(first_inverse_ready, f"MT{t}_0"))
                dve.wait_ge(first_inverse_ready, now(first_inverse_ready))

            first_inverse(0)
            row_masks(1)
            for t, c0, n in tiles:
                for l in range(1, levels(t)):
                    for b in range(2):
                        for u, name in ((M, f"MX{t}_{l}"), (MT, f"MTX{t}_{l}")):
                            if u == M and l == levels(t) - 1:
                                continue
                            if b == 0:
                                dve.wait_ge(pe_half, at(f"half:{name}"))
                            else:
                                dve.wait_ge(acc_full, filled(name))
                            old = um(u, t, n)[:, four(b), :]
                            ins = tt(old, old, bank(name, b, n), ALU.subtract)
                            if b == 0:
                                ins.then_inc(dve_half, up(dve_half, f"read half:{name}"))
                            else:
                                ins.then_inc(dve_drained, up(dve_drained, f"read:{name}",
                                                             f"MT{t}_{l}" if u == MT else None))
                    dve.wait_ge(dve_half, now(dve_half))
                    dve.wait_ge(dve_drained, now(dve_drained))
                    if t < 4:
                        prepare(t + 1, l - 1)
                if t < 4:
                    first_inverse(t + 1)
                if t < 3:
                    dve.wait_ge(acc_full, filled(f"o{t}"))
                    row_masks(t + 2)
                if t < 4:
                    dve.wait_ge(acc_full, filled(f"su{t}"))
                    if t == 0:
                        dve.wait_ge(zeros_stored, 80)
                    step(tt(S[:, :, :], S[:, :, :], bc(um(EG, t, n, P)[:, :, n - 1], 2, P), ALU.mult))
                    ins = tt(S[:, :, :], S[:, :, :], flatbuf(f"su{t}", H, P), ALU.add)
                    ins.then_inc(dve_drained, up(dve_drained, f"read:su{t}", f"S{t}"))
                    dve.wait_ge(dve_drained, now(dve_drained))
            t, _, n = tiles[4]
            for h in range(H):
                dve.wait_ge(acc_full, filled(f"suS{h}"))
                if h >= 2:
                    dve.wait_ge(snew_out[h % 2], 16 * (h // 2))
                step(tt(snew[h % 2], s0v[h], bc(um(EG, t, n, P)[:, h, LS - 1:TS:LS], 2, P), ALU.mult))
                ins = tt(snew[h % 2], snew[h % 2], flatbuf(f"suS{h}", NSEQ, P), ALU.add)
                ins.then_inc(dve_drained, up(dve_drained, f"read:suS{h}", f"snew{h}"))
                dve.wait_ge(dve_drained, now(dve_drained))

            dve.wait_ge(act_drained, at("read:osum"))
            dve.reciprocal(rb[0:H, :], rb[0:H, :]).then_inc(o_root_ready, 1)
            dve.wait_ge(o_root_ready, 1)
            for h in range(H):
                dve.wait_ge(acc_full, filled(f"og{h}"))
                tt(halves(yT[:, h, :]), halves(yT[:, h, :]), tok(f"og{h}"), ALU.mult).then_inc(
                    dve_drained, up(dve_drained, f"read:og{h}"))
                dve.wait_ge(dve_drained, now(dve_drained))
                stt(yT[:, h, :], yT[:, h, :], onrm[:, 0:1], zT[:, h, :], ALU.mult, ALU.mult).then_inc(
                    o_normed, up(o_normed, "onorm" if h == H - 1 else None))
                dve.wait_ge(o_normed, now(o_normed))
            for m in range(KD):
                dve.wait_ge(acc_full, filled(f"w{m}"))
                ps = buf(f"w{m}")
                residual(m, 0, [(ps[:, 0, 0:HT], 0, HT), (ps[:, 1, 0:SEQ - HT], HT, SEQ - HT)],
                         ps[:, 1, SEQ - HT:HT], rb[:, 0:TS], f"x1_{m}", f"w{m}")

            def choose(values, width, out):
                step(dve.tensor_reduce(rtv["tm"], values, AX.X, ALU.max))
                step(tt(out, values, bc(rtv["tm"], 2, 4), ALU.is_ge))
                step(tt(out, out, bc(cst[:, MISC, 4:8], 1, 5), ALU.mult))
                step(dve.tensor_reduce(width, out, AX.X, ALU.max))
                step(tt(out, out, bc(width, 2, 4), ALU.is_equal))

            def moe(layer, i, m):
                r = rtv
                step(dve.memset(rt[:, 0:340], 0.0))
                step(dve.memset(rx[:, 0:707], 0.0))
                step(dve.memset(r["one"], 1.0))
                dve.wait_ge(acc_full, filled(f"rt{layer}"))
                for rows, t0, nt in ((P, 0, 4), (TS, 4, 1)):
                    src = buf(f"rt{layer}")[0:rows, 0, 20 * t0:20 * (t0 + nt)].rearrange("p (t c) -> p t c", c=20)
                    ins = tt(r["L"][0:rows, t0:t0 + nt, :], src, bc(br[0:rows, layer, :], 1, nt), ALU.add)
                    if t0:
                        ins.then_inc(dve_drained, up(dve_drained, f"read:rt{layer}"))
                        dve.wait_ge(dve_drained, now(dve_drained))
                    else:
                        step(ins)
                lg, le = r["L"][:, :, 0:4], r["L"][:, :, 4:20].rearrange("p t (g e) -> p t g e", g=4)
                choose(lg, r["gm"], r["ohg"])
                tt(r["ge"], lg, bc(r["tm"], 2, 4), ALU.subtract).then_inc(
                    group_diff_ready, up(group_diff_ready, f"rga{layer}"))
                dve.wait_ge(group_diff_ready, now(group_diff_ready))
                dve.wait_ge(group_exp_ready, at(f"rgb{layer}"))
                step(dve.tensor_reduce(r["pg"], r["ge"], AX.X, ALU.add))
                step(dve.reciprocal(r["pg"], r["pg"]))
                step(tt(r["t16"], le, bc(r["ohg"], 3, 4), ALU.mult))
                step(dve.tensor_reduce(r["sel"], r["t16"].rearrange("p t g e -> p t e g"), AX.X, ALU.add))
                choose(r["sel"], r["gm"], r["oh1"])
                step(dve.tensor_copy(r["m1"], r["tm"]))
                step(stt(r["t4"], r["oh1"], -BIG, r["sel"], ALU.mult, ALU.add))
                choose(r["t4"], r["gm"], r["oh2"])
                tt(r["e2"], r["tm"], r["m1"], ALU.subtract).then_inc(
                    expert_diff_ready, up(expert_diff_ready, f"rea{layer}"))
                step(tt(choice[0], bc(r["ohg"], 3, 4), bc(r["oh1"], 2, 4), ALU.mult))
                step(tt(choice[1], bc(r["ohg"], 3, 4), bc(r["oh2"], 2, 4), ALU.mult))
                tt(chosen[2], chosen[0], chosen[1], ALU.add).then_inc(one_hots_ready, 1)
                dve.wait_ge(expert_diff_ready, now(expert_diff_ready))
                dve.wait_ge(expert_exp_ready, at(f"reb{layer}"))
                step(ts(r["w1"], r["e2"], 1.0, None, ALU.add))
                step(dve.reciprocal(r["w1"], r["w1"]))
                step(tt(r["w1"], r["w1"], r["pg"], ALU.mult))
                step(tt(r["w2"], r["w1"], r["e2"], ALU.mult))
                dve.wait_ge(acc_full, filled(f"rk{layer}"))
                ps = buf(f"rk{layer}")
                step(dve.tensor_copy(r["rank"][:, 0:4, :], ps[:, 0, 0:4 * E].rearrange("p (t e) -> p t e", e=E)))
                step(dve.tensor_copy(r["rank"][0:TS, 4, :], ps[0:TS, 0, 4 * E:5 * E]))
                dve.tensor_copy(r["tot"], ps[:, 1, 0:E]).then_inc(dve_drained, up(dve_drained, f"read:rk{layer}"))
                dve.wait_ge(dve_drained, now(dve_drained))
                for c in range(1, -(-T // P)):
                    step(stt(r["chunks"], r["tot"], P * c + 0.5, r["chunks"], ALU.is_ge, ALU.add))
                step(dve.tensor_tensor_scan(r["cum"], r["one"], r["chunks"], 0.0, ALU.mult, ALU.add))
                step(tt(r["le"], bc(r["cum"], 1, NOVER), bc(cst[:, MISC, 40:40 + NOVER], 2, E), ALU.is_le))
                step(dve.tensor_reduce(r["over"][:, 0:NOVER], r["le"], AX.X, ALU.add))
                step(ts(r["over"][:, 0:NOVER], r["over"][:, 0:NOVER], float(E - 1), None, ALU.min))
                step(dve.tensor_copy(r["over"][:, 8:9], r["cum"][:, E - 1:E]))
                step(dve.tensor_copy(over[:, :], r["over"]))
                step(tt(r["far"], r["cum"], r["chunks"], ALU.subtract))
                step(stt(r["far"], r["far"], float(P), cst[:, MISC, 24:24 + E], ALU.mult, ALU.add))
                step(ts(r["pos"], r["rank"], P + 0.5, None, ALU.is_ge))
                step(tt(r["pos"], r["pos"], bc(r["far"], 1, 5), ALU.mult))
                step(tt(r["rank"], r["rank"], bc(cst[:, MISC, 8:8 + E], 1, 5), ALU.add))
                step(tt(r["pos"], r["pos"], r["rank"], ALU.add))
                for k in range(TOP):
                    step(tt(r["po"], r["pos"], chosen[k], ALU.mult))
                    step(dve.tensor_reduce(r["row"][:, k, :], r["po"], AX.X, ALU.add))
                dve.tensor_copy(row_of[:, :, :], r["row"]).then_inc(routed, 1)
                dve.wait_ge(routed, layer + 1)
                done = E * layer

                def turn(i, first=False):
                    for j in range(2):
                        dve.wait_ge(s1_ready, i * 2 + (done + j + 1))
                        tt(hid[j], s1[j], acc[:, H_ACC, 1, 0:2 * P], ALU.mult).then_inc(hid_ready, 1)
                        dve.wait_ge(y_full, i * 2 + (done + j + 1))
                        if not first:
                            dve.wait_ge(ys_stored[j], i * 16 + 16 * (E // 2) * layer)
                        dve.tensor_copy(yc[j], acc[:, Y_ACC + j].rearrange("p b c -> p (b c)")).then_inc(yc_ready, 1)
                        dve.wait_ge(yc_ready, i * 2 + (done + j + 1))

                turn(0, first=True)
                with dve.Fori(1, E // 2) as it:
                    turn(it)
                for s in ys_stored:
                    dve.wait_ge(s, 16 * (E // 2) * (layer + 1))
                n_over = dve.value_load(over[0:1, 8:9], min_val=0, max_val=NOVER)

                def overflow_turn(i, first=False):
                    for p in range(2):
                        with dve.If(n_over > i * 2 + p):
                            dve.wait_ge(over_s1_ready[layer], i * 2 + (p + 1))
                            tt(hid[p], s1[p], acc[:, H_ACC, 1, 0:2 * P], ALU.mult).then_inc(over_hid_ready[layer], 1)
                            dve.wait_ge(over_y_full[layer], i * 2 + (p + 1))
                            if not first:
                                dve.wait_ge(over_stored[layer], i * 32 + (16 * p - 16))
                            dve.tensor_copy(yc[p], acc[:, Y_ACC + p].rearrange("p b c -> p (b c)")).then_inc(
                                over_yc_ready[layer], 1)

                overflow_turn(0, first=True)
                with dve.Fori(1, NOVER // 2) as it:
                    overflow_turn(it)
                for t_ in range(len(tiles) + 1):
                    if t_ < len(tiles):
                        t, c0, n = tiles[t_]
                        ot, (g1, g2) = otok[t % 2][0:n, :], (g[0:n, :] for g in got[t])
                        dve.wait_ge(gathered[t], at(f"g{layer}_{t}"))
                        dve.wait_ge(weighted, at(f"w{layer}_{t}"))
                        stt(ot, g2, r["w2"][0:n, t:t + 1], g1, ALU.mult, ALU.add).then_inc(
                            combined, up(combined, f"o{layer}_{t}"))
                        dve.wait_ge(combined, now(combined))
                    if t_:
                        t, c0, n = tiles[t_ - 1]
                        dve.wait_ge(acc_full, filled(f"ot{layer}_{t}"))
                        src = flatbuf(f"ot{layer}_{t}", KD, n)
                        tmp = xtmp[:, 0:KD * n].rearrange("p (k n) -> p k n", n=n)
                        if t < 4:
                            ins = tt(tmp, src, bc(modT[:, m, 16:24, 0], 2, n), ALU.mult)
                        else:
                            ins = tt(seqs(tmp), seqs(src), bc(modT[:, m, 16:24, 1:9], 3, LS), ALU.mult)
                        ins.then_inc(dve_drained, up(dve_drained, f"read:ot{layer}_{t}"))
                        dve.wait_ge(dve_drained, now(dve_drained))
                        tt(xT[:, :, c0:c0 + n], xT[:, :, c0:c0 + n], tmp, ALU.add).then_inc(
                            x_ready, up(x_ready, f"x{i + 1}_{t}"))
                        dve.wait_ge(x_ready, now(x_ready))

            norm(1, 1)
            moe(0, 1, 1)
            norm(2, 2)

            dve.wait_ge(bc_in, 32)
            e0, e1 = (extra[:, i, :].rearrange("p (q c) -> p q c", q=NPAIR) for i in range(2))
            fr, fi = bc(fz[:, 0, :], 2, 32), bc(fz[:, 1, :], 2, 32)
            step(tt(e0, BC[:, 0], fr, ALU.mult))
            step(tt(e1, BC[:, 1], fi, ALU.mult))
            step(tt(e0, e0, e1, ALU.subtract))
            step(tt(e1, BC[:, 1], fr, ALU.mult))
            step(tt(BC[:, 1], BC[:, 0], fi, ALU.mult))
            step(tt(BC[:, 1], BC[:, 1], e1, ALU.add))
            dve.tensor_copy(BC[:, 0], e0).then_inc(s5_b_ready, up(s5_b_ready, "bb"))
            dve.wait_ge(s5_b_ready, now(s5_b_ready))
            a8r, a8i = pw[:, 0, 8, :], pw[:, 1, 8, :]

            def power_step(out_r, out_i, xr, xi, yr, yi):
                start(tt(st1[:, 0], xr, yr, ALU.mult))
                start(tt(st1[:, 1], xi, yi, ALU.mult))
                start(tt(st2[:, 0], xr, yi, ALU.mult))
                step(tt(st2[:, 1], xi, yr, ALU.mult))
                start(tt(out_r, st1[:, 0], st1[:, 1], ALU.subtract))
                step(tt(out_i, st2[:, 0], st2[:, 1], ALU.add))

            for c in range(KD + 1):
                if 1 <= c <= 8:
                    if c == 1:
                        dve.wait_ge(acc_full, filled("u7"))
                        start(ts(aim[:, 0, :], a8i, -1.0, None, ALU.mult))
                        start(dve.tensor_copy(aim[:, 1, :], a8i))
                        start(dve.memset(POW8[:, 0, :, 0], 1.0))
                        start(dve.memset(POW8[:, 1, :, 0], 0.0))
                        start(dve.tensor_copy(POW8[:, 0, :, 1], a8r))
                        step(dve.tensor_copy(POW8[:, 1, :, 1], a8i))
                    else:
                        out_r, out_i = (POW8[:, 0, :, c], POW8[:, 1, :, c]) if c < 8 else (a64[:, 0], a64[:, 1])
                        power_step(out_r, out_i, POW8[:, 0, :, c - 1], POW8[:, 1, :, c - 1], a8r, a8i)
                    if c == 8:
                        step(ts(a64[:, 2], a64[:, 1], -1.0, None, ALU.mult))
                if c < KD:
                    if c:
                        dve.wait_ge(acc_full, filled(f"zr{c - 1}"))
                    zv, ev = zview(Z[0]), zview(extra[:, 0, :])
                    step(tt(zv, powers(0, 0, 8, c), over_m(BC[:, 0, 4 * c:4 * c + 4, :], 8), ALU.mult))
                    step(tt(ev, powers(1, 0, 8, c), over_m(BC[:, 1, 4 * c:4 * c + 4, :], 8), ALU.mult))
                    tt(zv, zv, ev, ALU.subtract).then_inc(zr_ready, up(zr_ready, f"zr{c}"))
                    dve.wait_ge(zr_ready, now(zr_ready))
                if c:
                    dve.wait_ge(acc_full, filled(f"inc{c - 1}"))
                    dve.tensor_copy(INC[:, :, 4 * c - 4:4 * c, :],
                                          buf(f"inc{c - 1}")[:, :, 0:4 * NCK].rearrange("p r (j c) -> p r j c", j=4)).then_inc(
                                              dve_drained, up(dve_drained, f"read:inc{c - 1}"))
                    dve.wait_ge(dve_drained, now(dve_drained))
            dve.wait_ge(zi_ready, at("zi7"))
            ts(BC[:, 1], BC[:, 1], -1.0, None, ALU.mult).then_inc(b_im_negated, 1)
            dve.wait_ge(b_im_negated, 1)
            sinb, incb = (v[:, :, :, 0:NCP].rearrange("p r q (b j) -> p r q b j", j=8) for v in (SIN, INC))
            start(dve.memset(BLK[:, 0], 0.0))
            step(dve.memset(sinb[:, :, :, :, 0], 0.0))
            rows8 = lambda v: bc(v, 2, 8)
            for k in range(8):
                out = sinb[:, :, :, :, k + 1] if k < 7 else BLK[:, 1:9].rearrange("p b r q -> p r q b")
                if k == 0:
                    step(dve.tensor_copy(out, incb[:, :, :, :, 0]))
                    continue
                cur = sinb[:, :, :, :, k]
                start(tt(sc1, cur, bc(bc(a8r, 1, 2), 3, 8), ALU.mult))
                start(tt(sc2[:, 0], cur[:, 1], rows8(aim[:, 0, :]), ALU.mult))
                step(tt(sc2[:, 1], cur[:, 0], rows8(aim[:, 1, :]), ALU.mult))
                step(tt(sc1, sc1, incb[:, :, :, :, k], ALU.add))
                step(tt(out, sc1, sc2, ALU.add))
            for b in range(1, 8):
                start(tt(st1, BLK[:, b], bc(a64[:, 0], 1, 2), ALU.mult))
                start(tt(st2[:, 0, :], BLK[:, b, 1], a64[:, 2], ALU.mult))
                step(tt(st2[:, 1, :], BLK[:, b, 0], a64[:, 1], ALU.mult))
                step(tt(st1, st1, st2, ALU.add))
                step(tt(BLK[:, b + 1], BLK[:, b + 1], st1, ALU.add))
            start(dve.tensor_copy(fin_p, BLK[:, 8]))
            dve.tensor_copy(SIN[:, :, :, NCP:NCK], s0ri).then_inc(blocks_ready, 1)
            dve.wait_ge(blocks_ready, 1)
            for r, i_, j_, op in ((0, 0, 0, ALU.add), (1, 0, 1, ALU.add), (0, 1, 1, ALU.subtract), (1, 1, 0, ALU.add)):
                step(tt(sc4[:, 0:Q_DVE], bc(POW8[:, i_, 0:Q_DVE], 2, 8),
                        bc(BLK[:, 0:8, j_, 0:Q_DVE].rearrange("p b q -> p q b"), 3, 8), ALU.mult))
                own = sinb[:, r, 0:Q_DVE]
                step(tt(own, own, sc4[:, 0:Q_DVE], op))
            dve.wait_ge(chunks_completed, 1)
            e0, e1 = sc1, sc2
            step(tt(e0, s0ri, bc(bc(a8r, 1, 2), 3, NSEQ), ALU.mult))
            for r in range(2):
                step(tt(e1[:, r], s0ri[:, 1 - r], bc(aim[:, r], 2, NSEQ), ALU.mult))
            step(tt(e0, e0, e1, ALU.add))
            tt(fin_s, e0, INC[:, :, :, NCP:NCK], ALU.add).then_inc(s5_fin_ready, up(s5_fin_ready, "s5fin"))
            dve.wait_ge(s5_fin_ready, now(s5_fin_ready))
            ts(SIN[:, 1], SIN[:, 1], -1.0, None, ALU.mult).then_inc(entry_states_ready, up(entry_states_ready, "sin"))
            dve.wait_ge(entry_states_ready, now(entry_states_ready))
            for c_ in range(KD + 1):
                if c_ < KD - 1:
                    c = c_ + 1
                    if c >= 2:
                        dve.wait_ge(acc_full, filled(f"yc{c - 2}"))
                    re = CA[c % 2][0]
                    start(tt(re, powers(0, 0, 9, c), over_m(BC[:, 2, 4 * c:4 * c + 4, :], 9), ALU.mult))
                    step(tt(catmp[0], powers(1, 0, 9, c), over_m(BC[:, 3, 4 * c:4 * c + 4, :], 9), ALU.mult))
                    tt(re, re, catmp[0], ALU.subtract).then_inc(ca_re_ready, up(ca_re_ready, f"car{c}"))
                    dve.wait_ge(ca_re_ready, now(ca_re_ready))
                if c_ < KD:
                    c = c_
                    dve.wait_ge(acc_full, filled(f"K{c}"))
                    if c >= 2:
                        dve.wait_ge(acc_full, filled(f"ys{c - 2}"))
                    quad = bc(bc(cst[:, MISC, 0:4], 1, 8), 3, 32)
                    tt(KB[c % 2].rearrange("p m (j c) -> p m j c", j=4), bc(flatbuf(f"K{c}", 8, 32), 2, 4), quad,
                       ALU.mult).then_inc(dve_drained, up(dve_drained, f"read:K{c}", f"kb{c}"))
                    dve.wait_ge(dve_drained, now(dve_drained))
                if c_:
                    c = c_ - 1
                    dve.wait_ge(acc_full, filled(f"ys{c}"))
                    for b in range(2):
                        tc = lambda ap: ap.rearrange("p (c t) -> p t c", t=8)[:, 4 * b:4 * b + 4]
                        ins = stt(tc(hT[:, c, :]), tc(zT[:, c, :]), s5d[:, c:c + 1],
                                  buf(f"ys{c}")[:, b, 0:4 * NCK].rearrange("p (t c) -> p t c", t=4), ALU.mult, ALU.add)
                        if b:
                            ins.then_inc(dve_drained, up(dve_drained, f"read:ys{c}", "ysum" if c == KD - 1 else None))
                            dve.wait_ge(dve_drained, now(dve_drained))
                        else:
                            start(ins)
            for m in range(KD):
                dve.wait_ge(acc_full, filled(f"ga{m}"))
                dve.wait_ge(act_drained, at(f"read:gg{m}"))
                t_ = yflat[:, T * (m % 2):T * (m % 2) + T]
                tt(halves(t_), tok(f"ga{m}"), halves(extra[:, m % 2, 0:T]), ALU.mult).then_inc(
                    dve_drained, up(dve_drained, f"read:ga{m}", f"glu{m}"))
                dve.wait_ge(dve_drained, now(dve_drained))
                residual(m, 2, [(t_[:, 0:SEQ], 0, SEQ)], t_[:, SEQ:T], rb[:, 0:TS], f"x3_{m}")
            norm(3, 3)
            moe(1, 3, 3)
            norm(4, None)

        @block.gpsimd
        def _(pool):
            def step(ins):
                ins.then_inc(pool_order, up(pool_order))
                pool.wait_ge(pool_order, now(pool_order))

            tt = pool.tensor_tensor
            step(pool.memset(small[:, 0:1], EPS))
            step(pool.memset(small[:, 1:2], P * EPS))
            step(pool.memset(small[:, 2:3], float(np.pi / 2)))
            step(pool.memset(c32, 0.0))
            pool.memset(ones[:, :], 1.0).then_inc(ones_ready, up(ones_ready, "ones"))
            pool.wait_ge(ones_ready, now(ones_ready))
            pool.wait_ge(conv_in, 32)
            for m in range(QKV):
                pool.wait_ge(act_drained, at(f"read:p{m}"))
                if m >= 2:
                    pool.wait_ge(conv_done, at(f"conv{m - 2}"))
                r = raw[m % 2][:, 3:3 + T]
                rs = r[:, SEQ:T].rearrange("p (b s) -> p b s", s=LS)
                step(pool.tensor_copy(sraw[m % 2][:, :, 0:3], cs_in[:, m]))
                step(pool.tensor_copy(cs_out[:, m], rs[:, :, LS - 3:LS]))
                step(pool.tensor_copy(cp_out[:, m, :], r[:, SEQ - 3:SEQ]))
                pool.tensor_copy(sraw[m % 2][:, :, 3:11], rs).then_inc(history_ready, up(history_ready, f"cs{m}"))
                pool.wait_ge(history_ready, now(history_ready))
            for t, c0, n in tiles:
                for l in range(levels(t)):
                    if l == 0:
                        pool.wait_ge(dve_drained, at(f"AT{t}"))
                        if t:
                            pool.wait_ge(acc_full, filled(f"X{t - 1}_{levels(t - 1) - 1}"))
                    elif l == 1:
                        pool.wait_ge(first_inverse_ready, at(f"MT{t}_0"))
                    else:
                        pool.wait_ge(acc_full, filled(f"X{t}_{l - 1}"))
                    tt(um(AB, t, n), um(AT, t, n), bc(cst[0:n, LEV + l, 0:n], 1, H), ALU.mult).then_inc(
                        a_block_ready, up(a_block_ready, f"ab{t}_{l}"))
                    pool.wait_ge(a_block_ready, now(a_block_ready))
            pool.wait_ge(act_drained, at("read:vtr"))
            for h in range(H):
                if h >= 2:
                    pool.wait_ge(acc_full, filled(f"suS{h - 2}"))
                tt(vmask[h % 2], bc(ur(VN, t, TS)[:, h, :], 1, NSEQ), bc(cst[0:TS, ONES8, 0:TS:LS], 2, P),
                          ALU.mult).then_inc(v_masked, up(v_masked, f"vm{h}"))
                pool.wait_ge(v_masked, now(v_masked))
            pool.wait_ge(acc_full, filled("suS7"))
            pool.tensor_copy(head_rows, bc(cst[0:H, IDENT, 0:H], 2, P)).then_inc(head_rows_ready, 1)
            pool.wait_ge(head_rows_ready, 1)

            def scatter(layer):
                pool.wait_ge(routed, layer + 1)
                if layer == 0:
                    pool.wait_ge(zeros_stored, 80)
                for t, c0, n in tiles:
                    pool.wait_ge(act_drained, at(f"read:tm{layer}_{t}"))
                    for k in range(TOP):
                        pool.indirect_dma_start(
                            xs[:, :], bass.IndirectOffsetOnAxis(ap=row_of[0:n, k, t:t + 1], axis=0),
                            htok[t][0:n, :], None).then_inc(scattered, 16)

            def gather(layer):
                n_over = pool.value_load(over[0:1, 8:9], min_val=0, max_val=NOVER)
                for s in ys_stored:
                    pool.wait_ge(s, 16 * (E // 2) * (layer + 1))
                with pool.If(n_over > 0):
                    with pool.Fori(0, NOVER // 2) as i:
                        for p in range(2):
                            with pool.If(n_over > i * 2 + p):
                                pool.wait_ge(over_yc_ready[layer], i * 2 + (p + 1))
                                pool.dma_start(ys_chunks[i * 2 + (E + p)], yc[p]).then_inc(over_stored[layer], 16)
                                pool.wait_ge(over_stored[layer], i * 32 + (16 * p + 16))
                for t, c0, n in tiles:
                    for k in range(TOP):
                        pool.indirect_dma_start(
                            got[t][k][0:n, :], None, ys[:, :],
                            bass.IndirectOffsetOnAxis(ap=row_of[0:n, k, t:t + 1], axis=0)).then_inc(
                            gathered[t], up(gathered[t], f"g{layer}_{t}", by=16))

            scatter(0)
            gather(0)
            pool.wait_ge(s5_b_ready, at("bb"))
            for c in range(KD):
                if c:
                    pool.wait_ge(acc_full, filled(f"zi{c - 1}"))
                zv, ev = zview(Z[1]), zview(extra[:, 1, :])
                step(tt(zv, powers(0, 0, 8, c), over_m(BC[:, 1, 4 * c:4 * c + 4, :], 8), ALU.mult))
                step(tt(ev, powers(1, 0, 8, c), over_m(BC[:, 0, 4 * c:4 * c + 4, :], 8), ALU.mult))
                tt(zv, zv, ev, ALU.add).then_inc(zi_ready, up(zi_ready, f"zi{c}"))
                pool.wait_ge(zi_ready, now(zi_ready))
            pool.wait_ge(acc_full, filled("inc7"))
            for r in range(2):
                step(tt(CA[0][r], powers(0, 0, 9, 0), over_m(BC[:, 2 + r, 0:4, :], 9), ALU.mult))
                step(tt(catmp[2], powers(1, 0, 9, 0), over_m(BC[:, 3 - r, 0:4, :], 9), ALU.mult))
                tt(CA[0][r], CA[0][r], catmp[2], ALU.add if r else ALU.subtract).then_inc(
                    first_ca_ready, up(first_ca_ready))
                pool.wait_ge(first_ca_ready, now(first_ca_ready))
            pool.wait_ge(blocks_ready, 1)
            sinb = SIN[:, :, :, 0:NCP].rearrange("p r q (b j) -> p r q b j", j=8)
            for r, i_, j_, op in ((0, 0, 0, ALU.add), (1, 0, 1, ALU.add), (0, 1, 1, ALU.subtract), (1, 1, 0, ALU.add)):
                step(tt(sc5, bc(POW8[:, i_, Q_DVE:NPAIR], 2, 8),
                        bc(BLK[:, 0:8, j_, Q_DVE:NPAIR].rearrange("p b q -> p q b"), 3, 8), ALU.mult))
                own = sinb[:, r, Q_DVE:NPAIR]
                ins = tt(own, own, sc5, op)
                if (r, i_) != (1, 1):
                    step(ins)
            ins.then_inc(chunks_completed, 1)
            pool.wait_ge(chunks_completed, 1)
            pool.wait_ge(entry_states_ready, at("sin"))
            for c in range(1, KD):
                if c >= 2:
                    pool.wait_ge(acc_full, filled(f"yc{c - 2}"))
                im = CA[c % 2][1]
                step(tt(im, powers(0, 0, 9, c), over_m(BC[:, 3, 4 * c:4 * c + 4, :], 9), ALU.mult))
                step(tt(catmp[1], powers(1, 0, 9, c), over_m(BC[:, 2, 4 * c:4 * c + 4, :], 9), ALU.mult))
                tt(im, im, catmp[1], ALU.add).then_inc(ca_im_ready, up(ca_im_ready, f"cai{c}"))
                pool.wait_ge(ca_im_ready, now(ca_im_ready))
            scatter(1)
            gather(1)


def _layouts(x):
    f = lambda n: np.asarray(x[n])
    a = {}
    tokens = np.concatenate([f("x_prompt").reshape(SEQ, D), f("x_sample").reshape(TS, D)], 0)
    a["xT"] = tokens.T.reshape(KD, P, T).transpose(1, 0, 2)
    cc = np.concatenate([f("c_prompt"), f("c_sample")], 0)
    a["cT"] = cc.T.reshape(KD, P, 9).transpose(1, 0, 2)
    a["masks"] = constant_masks()
    col = lambda v: v.reshape(-1, P).T
    a["bmod"] = np.stack([col(f("b_mod_mix")[0]), col(f("b_mod_ffn")[0]), col(f("b_mod_mix")[1]),
                          col(f("b_mod_ffn")[1])], 1)
    a["nrm"] = np.stack([col(f("norm_mix")[0]), col(f("norm_ffn")[0]), col(f("norm_mix")[1]),
                         col(f("norm_ffn")[1]), col(f("norm_final"))], 1)
    for n in ("w_mod_mix", "w_mod_ffn"):
        a[n] = f(n).reshape(2, 2, 4, P, 6, 512).transpose(0, 4, 1, 3, 2, 5).reshape(2, 12, P, UNIT)

    def pairs(w):
        k, m = w.shape
        return w.reshape(k // P, P, m // 256, 2, P).transpose(2, 1, 3, 0, 4).reshape(m // 256, P, UNIT)

    w_in = f("gdn_w_in")[0]
    a["w_in"] = pairs(w_in[:, 0:4 * D])
    a["w_ba"] = w_in[:, 4 * D:].reshape(KD, P, 16).transpose(1, 0, 2)
    a["w_out"] = pairs(f("gdn_w_out")[0])
    a["s5in"] = pairs(f("s5_w_in")[0])
    a["glu"] = f("s5_w_glu")[0].reshape(KD, P, 2, KD, P).transpose(3, 1, 2, 0, 4).reshape(KD, P, UNIT)
    for n, s in (("w1", "moe_w1"), ("w3", "moe_w3")):
        a[n] = f(s).reshape(2, E, KD, P, 2, P).transpose(0, 1, 3, 4, 2, 5).reshape(2, E, P, UNIT)
    a["w2"] = f("moe_w2").reshape(2, E, 2, P, D).transpose(0, 1, 3, 2, 4).reshape(2, E, P, UNIT)
    a["wr"] = np.concatenate([f("moe_w_rg"), f("moe_w_re")], 2).reshape(2, KD, P, 20).transpose(2, 0, 1, 3)
    a["br"] = np.concatenate([f("moe_b_rg"), f("moe_b_re")], 1)
    a["conv"] = f("state_conv")[0].reshape(NSEQ, 3, QKV, P).transpose(3, 2, 0, 1)
    a["cw"] = f("gdn_conv_w")[0].reshape(CW, QKV, P).transpose(2, 1, 0)
    a["a_log"], a["dt_bias"] = f("gdn_a_log")[0], f("gdn_dt_bias")[0]
    a["onrm"] = f("gdn_o_norm")[0].reshape(P, 1)
    a["s0"] = f("state_delta")[0].transpose(1, 2, 0, 3)
    states = lambda v: v.reshape(NPAIR, 2, 64).transpose(1, 2, 0).reshape(P, NPAIR)
    a["lam"] = np.stack([states(f("s5_lam_re")[0]), states(f("s5_lam_im")[0])], 1)
    a["log_dt"] = f("s5_log_dt")[0].reshape(NPAIR, 2).T
    a["s5d"] = f("s5_d")[0].reshape(KD, P).T
    bcs = np.zeros((2, 64, 4, NPAIR, 2, 16), np.float32)
    for k, n in enumerate(("s5_b_re", "s5_b_im", "s5_c_re", "s5_c_im")):
        v = f(n)[0].reshape(NPAIR, 2, *f(n).shape[2:])
        v = v.transpose(1, 2, 0, 3) if k < 2 else v.transpose(1, 3, 0, 2)
        for g in range(2):
            bcs[g, :, k, :, g, :] = v[g]
    a["bc"] = bcs.reshape(P, 4, NPAIR, 32)
    s0 = np.stack([f("state_ssm_re")[0], f("state_ssm_im")[0]], 0).reshape(2, NSEQ, NPAIR, 2, 64)
    a["s0ri"] = s0.transpose(3, 4, 0, 2, 1).reshape(P, 2, NPAIR, NSEQ)
    return {n: np.ascontiguousarray(v) for n, v in a.items()}


_OUTS = {"y": (P, KD, T), "p_delta": (P, H, P), "p_conv": (P, QKV, 3), "s_conv": (P, QKV, NSEQ, 3),
         "s_delta": (H, P, NSEQ, P), "p_ssm": (P, 2, NPAIR), "s_ssm": (P, 2, NPAIR, NSEQ)}


def _build(arrays, bacc, book):
    nc = bacc.Bacc("TRN2", target_bir_lowering=False, num_devices=1)
    d = {n: nc.dram_tensor(f"in_{n}", v.shape, F32, kind="ExternalInput").ap() for n, v in arrays.items()}
    o = {n: nc.dram_tensor(f"out_{n}", s, F32, kind="ExternalOutput").ap() for n, s in _OUTS.items()}
    for n in ("xs", "ys"):
        d[n] = nc.dram_tensor(n, (CHUNKS * P, D), F32).ap()
    trunk(nc, d, o, book)
    return nc


def kernel(**inputs):
    import concourse.bacc as bacc
    from concourse.bass_utils import run_bass_kernel_spmd as run

    arrays = _layouts(inputs)
    book = {}
    _build(arrays, bacc, book)
    nc = _build(arrays, bacc, book)
    r = run(nc, [{f"in_{n}": v for n, v in arrays.items()}], core_ids=[0]).results[0]
    g = {n: r[f"out_{n}"] for n in _OUTS}
    y = g["y"].transpose(2, 1, 0).reshape(T, D)
    states = lambda v: v.reshape(2, 64, NPAIR).transpose(2, 0, 1).reshape(1, 1, 64, 64)
    sstates = lambda v: v.reshape(2, 64, NPAIR, NSEQ).transpose(3, 2, 0, 1).reshape(1, NSEQ, 64, 64)
    c = np.ascontiguousarray
    return (c(y[0:SEQ].reshape(1, SEQ, D)), c(y[SEQ:].reshape(NSEQ, LS, D)),
            c(g["p_delta"].transpose(1, 0, 2).reshape(1, 1, H, P, P)),
            c(g["p_conv"].transpose(2, 1, 0).reshape(1, 1, 3, QKV * P)),
            c(states(g["p_ssm"][:, 0])), c(states(g["p_ssm"][:, 1])),
            c(g["s_delta"].transpose(2, 0, 1, 3).reshape(1, NSEQ, H, P, P)),
            c(g["s_conv"].transpose(2, 3, 1, 0).reshape(1, NSEQ, 3, QKV * P)),
            c(sstates(g["s_ssm"][:, 0])), c(sstates(g["s_ssm"][:, 1])))
```
